# Optimizing a Trainium2 kernel written in Bass

```python
import jax, jax.numpy as jnp
from jax import lax
import numpy as np

D_MODEL = 1024
BATCH = 1
SEQ = 256
DEPTH = 2

HEAD_DIM = 64
ROPE_THETA = 10000.0
NORM_EPS = 1e-6

NSA_HEADS = 6
NSA_KV_HEADS = 2
NSA_GROUP = NSA_HEADS // NSA_KV_HEADS
NSA_WIDTH = NSA_HEADS * HEAD_DIM
NSA_KV_WIDTH = NSA_KV_HEADS * HEAD_DIM
CMP_BLOCK = 32
CMP_STRIDE = 16
SLC_BLOCK = 64
SLC_TOPN = 16
WINDOW = 512
NSA_Q_BLOCK = 128
FORCE_SCORE = 1e6

MOBA_HEADS = 4
MOBA_WIDTH = MOBA_HEADS * HEAD_DIM
MOBA_BLOCK = 256
MOBA_TOPK = 3
MOBA_Q_BLOCK = 64

RWKV_WIDTH = D_MODEL - NSA_WIDTH - MOBA_WIDTH
RWKV_HEADS = RWKV_WIDTH // HEAD_DIM
DECAY_LORA = 64
AAA_LORA = 64
GATE_LORA = 128
RWKV_SHIFT_COLS = 3 * RWKV_WIDTH + DECAY_LORA + AAA_LORA + GATE_LORA
DECAY_SCALE = 0.606531
GN_EPS = 64e-5

MIX_WIDTH = NSA_WIDTH + MOBA_WIDTH + RWKV_WIDTH
IN_SPLITS = (NSA_WIDTH,) + (NSA_KV_WIDTH,) * 6 + (NSA_HEADS * 3,) + (MOBA_WIDTH,) * 3 + (RWKV_SHIFT_COLS,)
IN_COLS = sum(IN_SPLITS)

N_EXPERTS = 16
N_EXPERT_GROUPS = 4
EXPERTS_PER_GROUP = N_EXPERTS // N_EXPERT_GROUPS
TOP_K = 2
EXPERT_FF = 256

kernel_name = 'hybrid_nsa_moba_rwkv7_groupmoe'

def split_cols(t, sizes):
    offs, acc = [], 0
    for s in sizes[:-1]:
        acc += s
        offs.append(acc)
    return jnp.split(t, offs, axis=-1)

def rms_norm(x, gain):
    xf = x.astype(jnp.float32)
    y = xf * lax.rsqrt(jnp.mean(xf * xf, axis=-1, keepdims=True) + NORM_EPS)
    return (y * gain.astype(jnp.float32)).astype(x.dtype)

def rope_tables(positions):
    inv = ROPE_THETA ** (-jnp.arange(0, HEAD_DIM, 2, dtype=jnp.float32) / HEAD_DIM)
    ang = positions.astype(jnp.float32)[..., None] * inv
    return jnp.cos(ang), jnp.sin(ang)

def apply_rope(x, cos, sin):
    x1, x2 = jnp.split(x, 2, axis=-1)
    c = cos[:, :, None, :].astype(x.dtype)
    s = sin[:, :, None, :].astype(x.dtype)
    return jnp.concatenate([x1 * c - x2 * s, x2 * c + x1 * s], axis=-1)

def masked_softmax(s, mask):
    s = jnp.where(mask, s.astype(jnp.float32), -jnp.inf)
    m = jnp.max(s, axis=-1, keepdims=True)
    e = jnp.where(mask, jnp.exp(s - jnp.where(jnp.isfinite(m), m, 0.0)), 0.0)
    return e / jnp.maximum(jnp.sum(e, axis=-1, keepdims=True), 1e-30)

def gather_blocks(blocks, idx):
    return jax.vmap(jax.vmap(lambda bl, ix: bl[ix]))(blocks, idx)

def nsa_compress(t, w1, w2, pos):
    S = t.shape[1]
    n_cmp = (S - CMP_BLOCK) // CMP_STRIDE + 1
    idx = jnp.arange(n_cmp)[:, None] * CMP_STRIDE + jnp.arange(CMP_BLOCK)[None, :]
    blk = t[:, idx] + pos[None, None, :, None, :]
    h = jax.nn.gelu(jnp.einsum('bnlhd,lde->bnhe', blk, w1))
    return jnp.einsum('bnhe,ef->bnhf', h, w2)

def nsa_mixer(q, kc, vc, ks, vs, kw, vw, gates, cos, sin, phi_w1, phi_w2, phi_pos):
    B, S = q.shape[:2]
    KV, G, QB = NSA_KV_HEADS, NSA_GROUP, NSA_Q_BLOCK
    scale = HEAD_DIM ** -0.5
    n_cmp = (S - CMP_BLOCK) // CMP_STRIDE + 1
    n_slc = S // SLC_BLOCK
    n_top = min(SLC_TOPN, n_slc)
    cmp_end = jnp.arange(n_cmp) * CMP_STRIDE + CMP_BLOCK - 1
    k_cmp = apply_rope(nsa_compress(kc, phi_w1[0], phi_w2[0], phi_pos[0]), cos[:, cmp_end], sin[:, cmp_end])
    v_cmp = nsa_compress(vc, phi_w1[1], phi_w2[1], phi_pos[1])
    c_start = jnp.arange(n_cmp) * CMP_STRIDE
    s_start = jnp.arange(n_slc) * SLC_BLOCK
    overlap = (jnp.minimum(c_start[:, None] + CMP_BLOCK, s_start[None, :] + SLC_BLOCK)
               - jnp.maximum(c_start[:, None], s_start[None, :]))
    cmp_to_slc = jnp.clip(overlap, 0, None).astype(jnp.float32) / CMP_BLOCK
    ks_blk = ks.reshape(B, n_slc, SLC_BLOCK, KV, HEAD_DIM).transpose(0, 3, 1, 2, 4)
    vs_blk = vs.reshape(B, n_slc, SLC_BLOCK, KV, HEAD_DIM).transpose(0, 3, 1, 2, 4)
    kw_pad = jnp.pad(kw, ((0, 0), (WINDOW, 0), (0, 0), (0, 0)))
    vw_pad = jnp.pad(vw, ((0, 0), (WINDOW, 0), (0, 0), (0, 0)))
    blk_id = jnp.arange(n_slc)

    def chunk(ci):
        s0 = ci * QB
        t = s0 + jnp.arange(QB)
        qb = lax.dynamic_slice_in_dim(q, s0, QB, axis=1).reshape(B, QB, KV, G, HEAD_DIM)
        gb = jax.nn.sigmoid(lax.dynamic_slice_in_dim(gates, s0, QB, axis=1)).reshape(B, QB, KV, G, 3)
        s_c = jnp.einsum('bqhgd,bnhd->bhgqn', qb, k_cmp) * scale
        p_c = masked_softmax(s_c, cmp_end[None, :] <= t[:, None])
        o_c = jnp.einsum('bhgqn,bnhd->bqhgd', p_c.astype(v_cmp.dtype), v_cmp)
        imp = jnp.einsum('bhgqn,ns->bhqs', p_c, cmp_to_slc)
        cur = t // SLC_BLOCK
        cand = blk_id[None, :] <= cur[:, None]
        forced = (blk_id[None, :] == 0) | (blk_id[None, :] == cur[:, None]) | (blk_id[None, :] == cur[:, None] - 1)
        score = jnp.where(cand, jnp.where(forced, FORCE_SCORE, imp), -1.0)
        _, idx = lax.top_k(score, n_top)
        k_sel = gather_blocks(ks_blk, idx)
        v_sel = gather_blocks(vs_blk, idx)
        kpos = idx[..., None] * SLC_BLOCK + jnp.arange(SLC_BLOCK)
        m_s = (idx <= cur[:, None])[..., None] & (kpos <= t[:, None, None])
        n_keys = n_top * SLC_BLOCK
        s_s = jnp.einsum('bqhgd,bhqnkd->bhgqnk', qb, k_sel) * scale
        p_s = masked_softmax(s_s.reshape(B, KV, G, QB, n_keys), m_s.reshape(B, KV, 1, QB, n_keys))
        o_s = jnp.einsum('bhgqm,bhqmd->bqhgd', p_s.astype(vs.dtype), v_sel.reshape(B, KV, QB, n_keys, HEAD_DIM))
        kwb = lax.dynamic_slice_in_dim(kw_pad, s0, QB + WINDOW, axis=1)
        vwb = lax.dynamic_slice_in_dim(vw_pad, s0, QB + WINDOW, axis=1)
        kpos_w = s0 - WINDOW + jnp.arange(QB + WINDOW)
        dist = t[:, None] - kpos_w[None, :]
        m_w = (kpos_w[None, :] >= 0) & (dist >= 0) & (dist < WINDOW)
        s_w = jnp.einsum('bqhgd,bkhd->bhgqk', qb, kwb) * scale
        p_w = masked_softmax(s_w, m_w)
        o_w = jnp.einsum('bhgqk,bkhd->bqhgd', p_w.astype(vw.dtype), vwb)
        o = gb[..., 0:1] * o_c + gb[..., 1:2] * o_s + gb[..., 2:3] * o_w
        return o.reshape(B, QB, NSA_WIDTH)

    out = lax.map(chunk, jnp.arange(S // QB))
    return jnp.moveaxis(out, 0, 1).reshape(B, S, NSA_WIDTH)

def moba_mixer(q, k, v):
    B, S = q.shape[:2]
    H, QB = MOBA_HEADS, MOBA_Q_BLOCK
    scale = HEAD_DIM ** -0.5
    nb = -(-S // MOBA_BLOCK)
    pad = nb * MOBA_BLOCK - S
    kp = jnp.pad(k, ((0, 0), (0, pad), (0, 0), (0, 0)))
    vp = jnp.pad(v, ((0, 0), (0, pad), (0, 0), (0, 0)))
    k_blk = kp.reshape(B, nb, MOBA_BLOCK, H, HEAD_DIM).transpose(0, 3, 1, 2, 4)
    v_blk = vp.reshape(B, nb, MOBA_BLOCK, H, HEAD_DIM).transpose(0, 3, 1, 2, 4)
    k_mean = jnp.mean(k_blk.astype(jnp.float32), axis=3).astype(k.dtype)
    n_top = min(MOBA_TOPK, nb)
    n_sel = n_top * MOBA_BLOCK
    blk_id = jnp.arange(nb)

    def chunk(ci):
        s0 = ci * QB
        t = s0 + jnp.arange(QB)
        own = s0 // MOBA_BLOCK
        qb = lax.dynamic_slice_in_dim(q, s0, QB, axis=1)
        gate = jnp.einsum('bqhd,bhnd->bhqn', qb, k_mean).astype(jnp.float32)
        gate = jnp.where(blk_id < own, gate, -jnp.inf)
        _, idx = lax.top_k(gate, n_top)
        valid = idx < own
        k_sel = gather_blocks(k_blk, idx)
        v_sel = gather_blocks(v_blk, idx)
        s_sel = jnp.einsum('bqhd,bhqnkd->bhqnk', qb, k_sel).reshape(B, H, QB, n_sel)
        m_sel = jnp.broadcast_to(valid[..., None], (B, H, QB, n_top, MOBA_BLOCK)).reshape(B, H, QB, n_sel)
        k_own = lax.dynamic_slice_in_dim(kp, own * MOBA_BLOCK, MOBA_BLOCK, axis=1)
        v_own = lax.dynamic_slice_in_dim(vp, own * MOBA_BLOCK, MOBA_BLOCK, axis=1)
        s_own = jnp.einsum('bqhd,bkhd->bhqk', qb, k_own)
        m_own = jnp.broadcast_to((own * MOBA_BLOCK + jnp.arange(MOBA_BLOCK))[None, :] <= t[:, None], (B, H, QB, MOBA_BLOCK))
        p = masked_softmax(jnp.concatenate([s_sel, s_own], axis=-1) * scale,
                           jnp.concatenate([m_sel, m_own], axis=-1)).astype(v.dtype)
        o = (jnp.einsum('bhqm,bhqmd->bqhd', p[..., :n_sel], v_sel.reshape(B, H, QB, n_sel, HEAD_DIM))
             + jnp.einsum('bhqk,bkhd->bqhd', p[..., n_sel:], v_own))
        return o.reshape(B, QB, MOBA_WIDTH)

    out = lax.map(chunk, jnp.arange(S // QB))
    return jnp.moveaxis(out, 0, 1).reshape(B, S, MOBA_WIDTH)

def _rwkv7_step(state, inp):
    r_t, w_t, k_t, v_t, kk_t, a_t = inp
    sa = jnp.einsum('bhvk,bhk->bhv', state, -kk_t)
    state = (state * w_t[:, :, None, :] + sa[..., None] * (kk_t * a_t)[:, :, None, :]
             + v_t[..., None] * k_t[:, :, None, :])
    return state, jnp.einsum('bhvk,bhk->bhv', state, r_t)

def rwkv7_mixer(feat, mu, w_up, w0, a_up, a0, g_up, k_k, k_a, r_k, ln_w, ln_b):
    B, S, _ = feat.shape
    H, N = RWKV_HEADS, HEAD_DIM
    prev = jnp.pad(feat, ((0, 0), (1, 0), (0, 0)))[:, :-1]
    feat = feat + (prev - feat) * mu
    r, k, v, wd, ad, gd = split_cols(feat, (RWKV_WIDTH,) * 3 + (DECAY_LORA, AAA_LORA, GATE_LORA))
    decay = jnp.exp(-DECAY_SCALE * jax.nn.sigmoid((w0 + jnp.tanh(wd) @ w_up).astype(jnp.float32)))
    a = jax.nn.sigmoid(a0 + ad @ a_up)
    g = jax.nn.sigmoid(gd) @ g_up
    heads = lambda t: t.reshape(B, S, H, N).astype(jnp.float32)
    kk = heads(k * k_k)
    kk = kk / jnp.maximum(jnp.sqrt(jnp.sum(kk * kk, axis=-1, keepdims=True)), 1e-12)
    k = k * (1 + (a - 1) * k_a)
    rh, kh, vh = heads(r), heads(k), heads(v)
    xs = tuple(jnp.moveaxis(t, 1, 0) for t in (rh, heads(decay), kh, vh, kk, heads(a)))
    _, ys = lax.scan(_rwkv7_step, jnp.zeros((B, H, N, N), jnp.float32), xs)
    y = jnp.moveaxis(ys, 0, 1)
    mean = jnp.mean(y, axis=-1, keepdims=True)
    var = jnp.mean(jnp.square(y - mean), axis=-1, keepdims=True)
    y = ((y - mean) * lax.rsqrt(var + GN_EPS)).reshape(B, S, RWKV_WIDTH) * ln_w + ln_b
    bonus = (jnp.sum(rh * kh * r_k, axis=-1, keepdims=True) * vh).reshape(B, S, RWKV_WIDTH)
    return ((y + bonus) * g).astype(feat.dtype)

def moe_ffn(h, w_router, router_bias, w_gate, w_up, w_down):
    B, S, D = h.shape
    ht = h.reshape(B * S, D)
    T = ht.shape[0]
    aff = jax.nn.sigmoid((ht @ w_router).astype(jnp.float32))
    biased = (aff + router_bias.astype(jnp.float32)).reshape(T, N_EXPERT_GROUPS, EXPERTS_PER_GROUP)
    grp_score = jnp.sum(lax.top_k(biased, TOP_K)[0], axis=-1)
    best = jnp.argmax(grp_score, axis=-1)
    in_grp = jnp.take_along_axis(biased, best[:, None, None], axis=1)[:, 0]
    _, loc = lax.top_k(in_grp, TOP_K)
    eidx = best[:, None] * EXPERTS_PER_GROUP + loc
    wsel = jnp.take_along_axis(aff, eidx, axis=-1)
    wsel = wsel / jnp.sum(wsel, axis=-1, keepdims=True)
    combine = jnp.sum(jax.nn.one_hot(eidx, N_EXPERTS, dtype=jnp.float32) * wsel[..., None], axis=1).astype(ht.dtype)
    y = jnp.zeros_like(ht)
    for e in range(N_EXPERTS):
        he = jax.nn.silu(ht @ w_gate[e]) * (ht @ w_up[e])
        y = y + combine[:, e:e + 1] * (he @ w_down[e])
    return y.reshape(B, S, D)

def setup_inputs(seed: int = 0) -> dict:
    key = jax.random.key(seed)
    ks = jax.random.split(key, 40)
    f32 = jnp.float32
    nrm = lambda k, shape, s: jax.random.normal(k, shape, f32) * s
    D, L = D_MODEL, DEPTH
    offset = jax.random.randint(ks[2], (BATCH, 1), 0, 4096, dtype=jnp.int32)
    return {
        'x': nrm(ks[0], (BATCH, SEQ, D), 1.0),
        'c': nrm(ks[1], (BATCH, D), 1.0),
        'positions': offset + jnp.arange(SEQ, dtype=jnp.int32)[None, :],
        'w_mod': nrm(ks[3], (L, D, 6 * D), 0.5 * D ** -0.5),
        'b_mod': nrm(ks[4], (L, 6 * D), 0.02),
        'norm_mix': 1.0 + nrm(ks[5], (L, D), 0.05),
        'norm_ffn': 1.0 + nrm(ks[6], (L, D), 0.05),
        'w_in': nrm(ks[7], (L, D, IN_COLS), D ** -0.5),
        'nsa_phi_w1': nrm(ks[8], (L, 2, CMP_BLOCK, HEAD_DIM, HEAD_DIM), (CMP_BLOCK * HEAD_DIM) ** -0.5),
        'nsa_phi_w2': nrm(ks[9], (L, 2, HEAD_DIM, HEAD_DIM), HEAD_DIM ** -0.5),
        'nsa_phi_pos': nrm(ks[10], (L, 2, CMP_BLOCK, HEAD_DIM), 0.1),
        'rwkv_mu': jax.random.uniform(ks[11], (L, RWKV_SHIFT_COLS), f32),
        'rwkv_w_up': nrm(ks[12], (L, DECAY_LORA, RWKV_WIDTH), DECAY_LORA ** -0.5),
        'rwkv_w0': nrm(ks[13], (L, RWKV_WIDTH), 0.5),
        'rwkv_a_up': nrm(ks[14], (L, AAA_LORA, RWKV_WIDTH), 0.5 * AAA_LORA ** -0.5),
        'rwkv_a0': nrm(ks[15], (L, RWKV_WIDTH), 0.5),
        'rwkv_g_up': nrm(ks[16], (L, GATE_LORA, RWKV_WIDTH), GATE_LORA ** -0.5),
        'rwkv_k_k': 0.85 + nrm(ks[17], (L, RWKV_WIDTH), 0.05),
        'rwkv_k_a': 1.0 + nrm(ks[18], (L, RWKV_WIDTH), 0.05),
        'rwkv_r_k': nrm(ks[19], (L, RWKV_HEADS, HEAD_DIM), 0.1),
        'rwkv_ln_w': 1.0 + nrm(ks[20], (L, RWKV_WIDTH), 0.05),
        'rwkv_ln_b': nrm(ks[21], (L, RWKV_WIDTH), 0.02),
        'norm_nsa_out': 1.0 + nrm(ks[22], (L, NSA_WIDTH), 0.05),
        'norm_moba_out': 1.0 + nrm(ks[23], (L, MOBA_WIDTH), 0.05),
        'w_out': nrm(ks[24], (L, MIX_WIDTH, D), MIX_WIDTH ** -0.5),
        'w_router': nrm(ks[25], (D, N_EXPERTS), D ** -0.5),
        'router_bias': nrm(ks[26], (N_EXPERTS,), 0.01),
        'moe_w_gate': nrm(ks[27], (L, N_EXPERTS, D, EXPERT_FF), D ** -0.5),
        'moe_w_up': nrm(ks[28], (L, N_EXPERTS, D, EXPERT_FF), D ** -0.5),
        'moe_w_down': nrm(ks[29], (L, N_EXPERTS, EXPERT_FF, D), EXPERT_FF ** -0.5),
        'norm_final': 1.0 + nrm(ks[30], (D,), 0.05),
    }

def reference(x, c, positions, w_mod, b_mod, norm_mix, norm_ffn, w_in, nsa_phi_w1, nsa_phi_w2,
              nsa_phi_pos, rwkv_mu, rwkv_w_up, rwkv_w0, rwkv_a_up, rwkv_a0, rwkv_g_up, rwkv_k_k,
              rwkv_k_a, rwkv_r_k, rwkv_ln_w, rwkv_ln_b, norm_nsa_out, norm_moba_out, w_out,
              w_router, router_bias, moe_w_gate, moe_w_up, moe_w_down, norm_final):
    B, S, D = x.shape
    cos, sin = rope_tables(positions)
    c_act = jax.nn.silu(c)
    for l in range(DEPTH):
        mod = (c_act @ w_mod[l] + b_mod[l])[:, None, :]
        sh1, sc1, g1, sh2, sc2, g2 = jnp.split(mod, 6, axis=-1)
        h = rms_norm(x, norm_mix[l]) * (1 + sc1) + sh1
        proj = h @ w_in[l]
        (nq, nkc, nvc, nks, nvs, nkw, nvw, ngate, mq, mk, mv, rfeat) = split_cols(proj, IN_SPLITS)
        kvh = lambda t: t.reshape(B, S, NSA_KV_HEADS, HEAD_DIM)
        mh = lambda t: t.reshape(B, S, MOBA_HEADS, HEAD_DIM)
        o_nsa = nsa_mixer(apply_rope(nq.reshape(B, S, NSA_HEADS, HEAD_DIM), cos, sin),
                          kvh(nkc), kvh(nvc), apply_rope(kvh(nks), cos, sin), kvh(nvs),
                          apply_rope(kvh(nkw), cos, sin), kvh(nvw),
                          ngate.reshape(B, S, NSA_HEADS, 3), cos, sin,
                          nsa_phi_w1[l], nsa_phi_w2[l], nsa_phi_pos[l])
        o_moba = moba_mixer(apply_rope(mh(mq), cos, sin), apply_rope(mh(mk), cos, sin), mh(mv))
        o_rwkv = rwkv7_mixer(rfeat, rwkv_mu[l], rwkv_w_up[l], rwkv_w0[l], rwkv_a_up[l], rwkv_a0[l],
                             rwkv_g_up[l], rwkv_k_k[l], rwkv_k_a[l], rwkv_r_k[l], rwkv_ln_w[l], rwkv_ln_b[l])
        mix = jnp.concatenate([rms_norm(o_nsa, norm_nsa_out[l]), rms_norm(o_moba, norm_moba_out[l]), o_rwkv], axis=-1)
        x = x + g1 * (mix @ w_out[l])
        h2 = rms_norm(x, norm_ffn[l]) * (1 + sc2) + sh2
        x = x + g2 * moe_ffn(h2, w_router, router_bias, moe_w_gate[l], moe_w_up[l], moe_w_down[l])
    return rms_norm(x, norm_final)


_drawn_inputs = setup_inputs


def setup_inputs(seed=0):
    import zlib

    import numpy as np

    out = dict(_drawn_inputs(seed))
    spreads = {}
    factors = {'rwkv_k_k': 16.36, 'rwkv_ln_b': 8.0, 'rwkv_ln_w': 2.928}
    for name, (base, spread) in spreads.items():
        noise = np.random.default_rng([zlib.crc32(name.encode()), seed]).standard_normal(out[name].shape)
        drawn = base * np.exp(spread * noise) if base else spread * noise
        out[name] = __import__('jax').numpy.asarray(drawn.astype(out[name].dtype))
    for name, factor in factors.items():
        out[name] = (out[name] * factor).astype(out[name].dtype)
    return out
```

```python
import math
from contextlib import ExitStack

import concourse.bass as bass
from concourse import mybir

F32 = mybir.dt.float32
BF16 = mybir.dt.bfloat16
I32 = mybir.dt.int32
ALU = mybir.AluOpType
ACT = mybir.ActivationFunctionType
AX = mybir.AxisListType.X

P = 128
SEQ, D, DEPTH = 256, 1024, 2
TB = SEQ // P
KD = D // P
HD = 64
NH, NKV = 6, 2
NSA_W, MOBA_W, RW = 384, 256, 384
CMP_BLOCK, CMP_STRIDE = 32, 16
NC = (SEQ - CMP_BLOCK) // CMP_STRIDE + 1
EPS, GN_EPS = 1e-6, 64e-5
DECAY = 0.606531
SCALE = HD ** -0.5
CH = 64
NCH = SEQ // CH
LEVELS = [1, 2, 4, 8, 16, 32]
E, FF = 16, 256
NEG = -1e30
NF = 11

IN_SLOTS = [(1938, 512), (2450, 512), (2962, 384), (0, 512), (512, 512), (1024, 402), (1426, 512)]
RING = 3
MIX_SLOTS = len(IN_SLOTS) + 2
LAYER_SLOTS = MIX_SLOTS + 3 * E // 2
MODJ = 12

C_IDENT, C_CAUSAL, C_BLK, C_ONES = 0, 128, 512, 640
C_STRICT, C_INCL, C_LEVEL, C_ID64 = 768, 832, 896, 1280
C_RESET, C_CBIAS, C_C01, C_LT, C_GT, C_INV, C_END = 1344, 1600, 1630, 1660, 1676, 1692, 1724

V_MOD, V_NMIX, V_NFFN, V_MU, V_W0, V_A0, V_KK, V_KA, V_RK = 0, 32, 40, 48, 59, 62, 65, 68, 71
V_LNW, V_LNB, V_NSA, V_MOBA, V_POS, V_END = 74, 77, 80, 83, 85, 117


def bank_plan():
    p = [("vec", "v")] + [(f"mod{j}", "v") for j in range(4)]
    p += [(f"hT{j}", "av"[j % 2]) for j in range(4)]
    p += [("rf0", "a"), ("rf1", "a"), ("mod4", "v"), ("rf2", "a"), ("rf3", "a"), ("mod5", "v"),
          ("rf4", "a"), ("mod6", "v"), ("rf5", "a"), ("mod7", "v"), ("q0", "v"), ("q1", "v"),
          ("mod8", "v"), ("cT", "a"), ("k0", "v"), ("mod9", "v"), ("k1", "v"), ("g0", "v"),
          ("mod10", "v"), ("g1", "v"), ("m0", "v"), ("mod11", "v"), ("m1", "v")]
    p += [("lw0", "a"), ("lw1", "a"), ("la0", "a"), ("la1", "a"), ("lg0", "a"), ("lg1", "a")]
    p += [("kn0", "v"), ("kn1", "v"), ("rv0", "a"), ("rv1", "a"), ("bo0", "v"), ("bo1", "v")]
    p += [(f"qk{i}", "a") for i in range(5)]
    p += [("ch", "v"), ("ckv", "v"), ("ckT", "v"), ("cs0", "v"), ("cs1", "v"), ("cpT", "v"),
          ("co0", "v"), ("co1", "v")]
    p += [(f"row{w}{t}", "a") for w in "abk" for t in range(2)]
    p += [(f"mb{b}{t}", "v") for b in range(2) for t in range(2)]
    p += [(f"mk{b}{t}", "v") for b in range(2) for t in range(2)]
    for s in mixed_steps():
        p += step_banks(s)
    p += [("ys0", "a"), ("ys1", "a"), ("yu0", "v"), ("yu1", "v")]
    p += [("gm0", "v"), ("gm1", "v"), ("gv0", "v"), ("gv1", "v")]
    p += [("mT0", "a"), ("mT1", "a"), ("mT2", "a")]
    p += [(f"out{i}", "v") for i in range(4)]
    p += [(f"h2T{j}", "av"[j % 2]) for j in range(4)] + [("route", "v"), ("rank", "v")]
    p += [(f"hs{j}", "av"[j % 2]) for j in range(4)] + [("combs", "v"), ("pT", "a")]
    return p


def mixed_steps():
    serial = [("x", n) for n in range(len(LEVELS))]
    order, t = [], 0
    for n in range(len(LEVELS)):
        order.append(("x", n))
        order.append(("head", t))
        t += 1
        if n:
            order.append(("t", n))
            order.append(("head", t))
            t += 1
    order += [("w1", 0), ("head", t), ("tw", 0), ("head", t + 1)]
    t += 2
    for c in range(NCH):
        order += [("u", c)]
        if t < 18:
            order += [("head", t)]
            t += 1
        if c < NCH - 1:
            order += [("g", c)]
    while t < 18:
        order += [("head", t)]
        t += 1
    return order


def step_banks(step):
    kind, n = step
    if kind == "x":
        return [(f"x{n}{b}", "a") for b in range(2)]
    if kind == "t":
        last = n == len(LEVELS) - 1
        return ([] if last else [(f"t{n}{b}", "v") for b in range(2)]) + [(f"tt{n}{b}", "v") for b in range(2)]
    if kind == "w1":
        return [("w10", "a"), ("w11", "a")]
    if kind == "tw":
        return [("ub0", "a"), ("ub1", "a"), ("ta0", "a"), ("ta1", "a")]
    if kind == "u":
        return [(f"u{n}{b}", "v") for b in range(2)]
    if kind == "g":
        return [(f"g{n}s", "v")]
    return ([(f"S{n}", "v")] if n < 16 else []) + ([(f"T{n - 1}", "a")] if 1 <= n <= 16 else []) \
        + ([(f"O{n - 2}", "v")] if n >= 2 else [])


class Chain:

    def __init__(self, eng, sem, base=0):
        self.eng, self.sem, self.base, self.n = eng, sem, base, 0

    def __call__(self, ins):
        self.n += 1
        return ins.then_inc(self.sem, 1)

    def sync(self):
        self.eng.wait_ge(self.sem, self.base + self.n)

    def fill_up(self, total):
        assert self.n < total, self.n
        self.sync()
        self.eng.sem_inc(self.sem, total - self.n)


def trunk(nc, x, c, positions, w_mod, b_mod, norm_mix, norm_ffn, w_in, phi_w1, phi_w2, phi_pos,
          mu, w_up, w0, a_up, a0, g_up, k_k, k_a, r_k, ln_w, ln_b, nsa_out, moba_out, w_out,
          w_router, router_bias, moe_g, moe_u, moe_d, norm_final, table, out):
    with ExitStack() as ctx:
        def sb(name, shape, dt=F32):
            return ctx.enter_context(nc.sbuf_tensor(name, shape, dt))

        def sem(name):
            return ctx.enter_context(nc.semaphore(name))

        ring = sb("weight_ring", [P, RING, 8, 512])
        modw = sb("modulation_ring", [P, 2, 4, 512])
        cst = sb("shape_constants", [P, C_END])
        xs = sb("residual", [P, TB, D])
        actT = sb("activations_T", [P, KD, SEQ])
        gate_rows = sb("gate_rows", [P, 2, D])
        vec_rows = sb("vector_rows", [V_END, P])
        vec = sb("vectors_T", [P, V_END])
        vx = sb("derived_vectors", [P, 9])
        modc = sb("modulation_T", [P, 32])
        amod = sb("norm_scale_T", [P, 16])
        acc = sb("modulation_acc", [P, 2, 512])
        cact = sb("silu_c", [P, 24])
        crow = sb("c_rows", [8, P])
        cosn = sb("cos_sin", [P, 2, 3, HD])
        posi = sb("positions_i", [P, 3], I32)
        w1s = sb("phi_w1", [P, 2, 16, HD])
        w2s = sb("phi_w2", [HD, 2, HD])
        lora = sb("lora_up", [P, 2, RW])
        wrt = sb("router_w", [P, KD, E])
        rbias = sb("router_bias", [P, E])
        comb = sb("combine", [P, TB, E])
        stat = sb("norm_stats", [P, 16])
        mhalf = sb("minus_half", [P, 1])
        zero16 = sb("zeros_bf16", [P, 512], BF16)
        feat = sb("rwkv_features_T", [P, NF, SEQ + 1])
        big = sb("rwkv_T", [P, 7, 3, SEQ])
        rows = sb("rwkv_rows", [P, 4, TB, RW])
        aak = sb("rwkv_Aak", [P, 2, TB, 3, CH])
        mo1b = sb("rwkv_spare", [P, 2, TB, 3, CH])
        st = sb("rwkv_state", [P, NCH, 3, HD])
        dtmp = sb("shift_difference", [P, 2, SEQ])
        pl = sb("chunk_decay", [P, 3, NCH])
        gtmp = sb("state_sum", [P, 3, HD])
        room = sb("attention_room", [P, 8960])

        def sub(t, at, shape):
            n = 1
            for s in shape:
                n *= s
            flat = t[:, at:at + n]
            if len(shape) == 1:
                return flat
            names = "abcd"[:len(shape)]
            return flat.rearrange(f"p ({' '.join(names)}) -> p {' '.join(names)}", **dict(zip(names, shape)))

        qrot = sub(room, 0, [TB, 9, P])
        xn = sub(room, 0, [TB, D])
        cPb = sub(room, 0, [TB, 2, 96])
        cVb = sub(room, 384, [2, 192])
        cSb = sub(room, 768, [2, TB, 3, NC])
        cpT = sub(room, 960, [TB, 2, P])
        ropeA = sub(room, 2304, [2, 512])
        ropeB = sub(room, 3328, [2, 512])
        Ssb = sub(room, 2304, [2, 384])
        PTs = sub(room, 3328, [2, 384])
        vsel = sub(room, 4352, [TB, P])
        vwin = sub(room, 4608, [TB, P])
        vmob = sub(room, 4864, [TB, 256])
        qkT = sub(room, 5376, [9, SEQ])
        onsa = sub(room, 7680, [TB, NSA_W])
        omob = sub(room, 8448, [TB, MOBA_W])
        kcT = sub(room, 7680, [2, SEQ])
        junk = sub(room, 2304, [D])
        junkv = sub(room, 3328, [2, 512])
        rflat = rows[:].rearrange("p a t c -> p (a t c)")
        before = sub(rflat, 0, [P])
        iota = sub(rflat, P, [SEQ])
        perm = sub(rflat, 384, [TB, SEQ])
        permT = sub(rflat, 896, [TB, SEQ])
        th_s = sub(rflat, 1408, [2, FF])
        t1_s = sub(rflat, 1920, [2, FF])
        he_s = sub(rflat, 2432, [2, FF])
        heT_s = sub(room, 3840, [2, 2, P])
        ysort = sub(room, 0, [TB, D])
        cS = sub(rflat, 768, [2, 2, SEQ])
        blk = sub(rflat, 1792, [2, 16, 2 * NC])
        cg = sub(rflat, 2752, [4, 4 * NC])[0:HD]
        ckr = sub(room, 1472, [4, P])[0:NC]
        ckT = sb("compress_kT", [P, NC])
        gsig = sb("branch_gates", [P, TB, 18])
        cst2 = sb("compress_stats", [P, 48])
        amx = sb("softmax_max", [P, 16, 2])
        asm = sb("softmax_sum", [P, 16, 2])
        awt = sb("softmax_weight", [P, 16, 2])
        rt = room[:, 4352:4992]
        combs = sub(rt, 0, [TB, E])
        counts = sb("block_counts", [P, 2 * (E // 2 + 1)], I32)

        final_row = sub(room, 5376, [D])
        Tm, TTm, Xm, mo0 = (big[:, i].rearrange("p i t -> p (i t)").rearrange(
            "p (b t i s) -> p b t i s", b=2, t=TB, i=3) for i in (0, 1, 4, 5))
        mo1 = mo1b[:]
        W1, Ub, Um = Xm, mo0, mo1
        TA = big[:, 0].rearrange("p i (n s) -> p i n s", n=NCH)
        ysq = big[:, 4]
        fflat = feat[:].rearrange("p a b -> p (a b)")
        Mst, Arb, Ark = (sub(fflat, 768 * i, [2, TB, 3, CH]) for i in range(3))
        yT = sub(fflat, 0, [3, SEQ])

        def group_of(t):
            return rt[:, 152 + 4 * t:156 + 4 * t]

        def below_of(t):
            return rt[:, 576 + 4 * t:580 + 4 * t]

        def head_of(t):
            if t < 12:
                i, hb, branch = t % 6 // 2, t % 2, t // 6
                v = (vsel, vwin)[branch]
                h = 3 * hb + i
                return i, hb, 3 + branch, (lambda k: v[:, k, hb * HD:(hb + 1) * HD]), (branch + 1, h)
            i, hb = (t - 12) // 2, t % 2
            h = 2 * i + hb
            return 5 + i, hb, 7 + i, (lambda k: vmob[:, k, h * HD:(h + 1) * HD]), (0, h)

        banks = [ctx.enter_context(nc.psum_tensor(f"bank{i}", [P, 512], F32)) for i in range(8)]

        s_const = sem("constants_loaded")
        s_setup = {e: sem(f"{e}_setup_steps") for e in ("vector", "scalar", "tensor", "gpsimd")}
        s_vs, s_as, s_ps = sem("vector_steps"), sem("scalar_steps"), sem("gpsimd_steps")
        s_vm, s_am = sem("vector_moe_steps"), sem("scalar_moe_steps")
        s_gate = sem("tensor_gate")
        s_fill = {"a": sem("banks_filled_for_scalar"), "v": sem("banks_filled_for_vector")}
        s_drain = {"a": sem("banks_drained_by_scalar"), "v": sem("banks_drained_by_vector")}
        s_slot = [sem(f"ring_slot{i}_loaded") for i in range(RING)]
        s_modl = [sem(f"modulation_half{i}_loaded") for i in range(2)]
        s_modu = sem("modulation_half_used")
        s_acc = sem("modulation_chunk_summed")
        s_small = sem("layer_vectors_loaded")
        s_smallw = sem("layer_small_weights_loaded")
        s_grow = sem("gate_bias_loaded")
        s_gused = sem("gate_rows_used")
        s_ss = sem("square_sums_ready")
        s_ms = sem("mean_squares_ready")
        s_rstd = sem("rstd_ready")
        s_xn = sem("normalised_rows_ready")
        s_x = sem("residual_updated")
        s_mix = sem("features_shifted")
        s_lin = sem("lora_tanh_ready")
        s_lsg = sem("lora_sigmoid_ready")
        s_sq = sem("key_squares_ready")
        s_kn = sem("key_norms_inverted")
        s_kni = sem("key_norm_roots_ready")
        s_cum = sem("decay_sums_ready")
        s_exp = sem("decay_exponentials_ready")
        s_rk = sem("bonus_products_ready")
        s_til = sem("scaled_operands_ready")
        s_ra = sem("rope_products_ready")
        s_rot = sem("rope_rows_ready")
        s_cw = sem("compress_windows_ready")
        s_cb = sem("compress_blocks_ready")
        s_ct = sem("compress_tanh_in")
        s_ct2 = sem("compress_tanh_out")
        s_cgr = sem("compress_gelu_ready")
        s_ckr = sem("compress_key_rows_ready")
        s_cs = sem("compress_scores_ready")
        s_ce = sem("compress_exp_ready")
        s_cp = sem("compress_probs_ready")
        s_gs = sem("branch_gates_ready")
        s_mask = sem("level_masks_ready")
        s_mm = sem("inverse_matrix_ready")
        s_sc = sem("scores_masked")
        s_ex = sem("scores_exponentiated")
        s_yv = sem("centred_squares_and_variance_ready")
        s_yr = sem("variance_inverse_roots_ready")
        s_mixT = sem("rwkv_mix_ready")
        s_o = sem("attention_rows_ready")
        s_comb = sem("combine_ready")
        s_gu, s_th, s_t1, s_he, s_hT, s_hTs, s_dn = (
            [sem(f"{n}_block{t}") for t in range(TB)]
            for n in ("gate_up_filled", "gate_tanh_ready", "gate_product_ready", "hidden_ready", "hiddenT_filled",
                      "hiddenT_ready", "expert_down_done"))
        s_down = [sem(f"down_weights_half{j}_loaded") for j in range(2)]
        s_grp = sem("token_groups_ready")
        s_perm = sem("permutation_ready")
        s_count = sem("block_counts_ready")
        s_y = sem("expert_sum_filled")
        s_ys = {e: sem(f"expert_sum_copied_by_{e}") for e in ("scalar", "vector")}
        s_unsort = sem("expert_sum_unsorted")
        s_out = sem("output_stored")

        plan = bank_plan()
        index = {n: i for i, (n, _) in enumerate(plan)}
        assert len(index) == len(plan)
        order_of, total = {}, {"a": 0, "v": 0}
        for n, e in plan:
            total[e] += 1
            order_of[n] = total[e]
        drainer = dict(plan)

        def filled(eng, l, name):
            e = drainer[name]
            eng.wait_ge(s_fill[e], l * total[e] + order_of[name])
            return banks[index[name] % 8]

        def drained(eng, l, name):
            e = drainer[name]
            eng.wait_ge(s_drain[e], l * total[e] + order_of[name])

        def con(at, n, p0=0, p1=P):
            return cst[p0:p1, at:at + n]

        def bc(ap, axis, n):
            v = ap.unsqueeze(axis)
            shape = list(v.shape)
            shape[axis] = n
            return v.to_broadcast(shape)

        V_STEPS, A_STEPS, G_STEPS = 1024, 512, 256
        SET_C, SET_ANG = 1, 13
        SMALL, SMALLW = 15, 6

        SLOT_LOADS = [16 * (3 + E)] * 2 + [16 * 3]
        PAIRS = E // 2

        def skip(eng, sem_, n):
            eng.wait_ge(sem_, n)
            eng.sem_inc(sem_, 1)

        def loads_counts(eng, q, at):
            return [eng.value_load(counts[0:1, bass.ds(2 * q + 2 * at + t, 1)], min_val=0, max_val=P) for t in range(TB)]
        s_on = sem("attention_values_ready")
        s_nf = sem("final_gain_loaded")
        s_fin = sem("output_ready")
        s_rt = sem("router_tanh_ready")
        s_gt = sem("branch_gates_in")
        s_gth = sem("branch_gates_tanh")
        s_st = sem("chunk_state_ready")
        s_vgate = sem("vector_gate")
        s_yd = sem("expert_sum_steps")

        block = ctx.enter_context(nc.Block())

        @block.sync
        def _(sp):
            def load_vectors(l):
                def put(r, n, src):
                    sp.dma_start(vec_rows[r:r + n, :], src).then_inc(s_small, 16)
                put(0, 16, b_mod[l, 0:2048].rearrange("(r c) -> r c", c=P))
                put(16, 16, b_mod[l, 3072:5120].rearrange("(r c) -> r c", c=P))
                for r, n, src in ((V_NMIX, 8, norm_mix), (V_NFFN, 8, norm_ffn), (V_MU, NF, mu), (V_W0, 3, w0),
                                  (V_A0, 3, a0), (V_KK, 3, k_k), (V_KA, 3, k_a), (V_LNW, 3, ln_w),
                                  (V_LNB, 3, ln_b), (V_NSA, 3, nsa_out), (V_MOBA, 2, moba_out)):
                    put(r, n, src[l].rearrange("(r c) -> r c", c=P))
                put(V_RK, 3, r_k[l].rearrange("(r h) c -> r (h c)", h=2))
                put(V_POS, 32, phi_pos[l].rearrange("k (j h) d -> (k j) (h d)", h=2))

            def load_small_weights(l):
                for kv in range(2):
                    sp.dma_start(w1s[:, kv], phi_w1[l, kv].rearrange("(j h) d e -> (h d) j e", h=2)).then_inc(s_smallw, 16)
                sp.dma_start(w2s[:], phi_w2[l].rearrange("k d e -> d k e")).then_inc(s_smallw, 16)
                sp.dma_start(lora[0:64, 0, :], w_up[l]).then_inc(s_smallw, 16)
                sp.dma_start(lora[64:128, 0, :], a_up[l]).then_inc(s_smallw, 16)
                sp.dma_start(lora[:, 1, :], g_up[l]).then_inc(s_smallw, 16)

            def load_gate_bias(l):
                for g, at in ((0, 2048), (1, 5120)):
                    sp.dma_start(gate_rows[:, g, :], b_mod[l, at:at + D].partition_broadcast(P)).then_inc(s_grow, 16)

            def load_mod(l, j):
                for h in range(2):
                    n = 2 * j + h
                    if n >= 2:
                        sp.wait_ge(s_modu, l * 2 * MODJ + n - 1)
                    sp.dma_start(modw[:, h], w_mod[l, 512 * h:512 * h + 512, 512 * j:512 * j + 512]
                                 .rearrange("(k p) n -> p k n", p=P)).then_inc(s_modl[h], 16)

            def load_in(l, i):
                at, n = IN_SLOTS[i]
                sp.dma_start(ring[:, i % RING, :, 0:n], w_in[l, :, at:at + n].rearrange("(k p) n -> p k n", p=P)
                             ).then_inc(s_slot[i % RING], 16)

            def load_out(l, i):
                r = (len(IN_SLOTS) + i) % RING
                sp.dma_start(ring[:, r], w_out[l, :, 512 * i:512 * i + 512].rearrange("(k p) n -> p k n", p=P)
                             ).then_inc(s_slot[r], 16)

            sp.dma_start(crow[:], c[0].rearrange("(r c) -> r c", c=P)).then_inc(s_const, 16)
            sp.dma_start(cst[:], table[:, :]).then_inc(s_const, 16)
            sp.dma_start(xs[:], x[0].rearrange("(t p) d -> p t d", p=P)).then_inc(s_const, 16)
            sp.wait_ge(s_setup["gpsimd"], 1)
            sp.dma_start(posi[:, 0:2], positions[0].rearrange("(t p) -> p t", p=P), allow_slow_non_contiguous=True).then_inc(s_const, 16)
            sp.dma_start(posi[0:NC, 2:3], positions[0:1, CMP_BLOCK - 1:SEQ:CMP_STRIDE].rearrange("a n -> n a"), allow_slow_non_contiguous=True).then_inc(s_const, 16)
            sp.dma_start(wrt[:], w_router.rearrange("(k p) e -> p k e", p=P)).then_inc(s_const, 16)
            sp.dma_start(rbias[:], router_bias.partition_broadcast(P)).then_inc(s_const, 16)

            def load_gate_up(l, q, j):
                for w, at in ((moe_g, 0), (moe_u, FF)):
                    sp.dma_start(ring[:, j, :, at:at + FF], w[l, 2 * q + j].rearrange("(k p) n -> p k n", p=P)
                                 ).then_inc(s_slot[j], 16)

            def load_down(l, q, j):
                sp.dma_start(ring[:, 2, 4 * j:4 * j + 4, :].rearrange("p (k h) n -> p k (h n)", h=2),
                             moe_d[l, 2 * q + j].rearrange("(k p) n -> p k n", p=P)).then_inc(s_down[j], 16)

            def used(sems, n):
                for s_ in sems:
                    sp.wait_ge(s_, 1 + n)

            def rest_of(l):
                for j, slot, user in ((4, None, None), (5, 3, "rf1"), (6, None, None), (7, 4, "rf3"), (8, None, None),
                                      (9, 5, "rf5"), (10, None, None), (11, 6, "cT")):
                    load_mod(l, j)
                    if slot:
                        filled(sp, l, user)
                        load_in(l, slot)
                for i, user in ((0, "k1"), (1, "g1")):
                    filled(sp, l, user)
                    load_out(l, i)
                filled(sp, l, "m1")
                load_gate_up(l, 0, 0)
                filled(sp, l, "out1")
                load_gate_up(l, 0, 1)
                filled(sp, l, "out3")
                load_down(l, 0, 0)
                with sp.Fori(1, PAIRS) as q:
                    used(s_gu, l * E + 2 * q - 1)
                    load_gate_up(l, q, 0)
                    used(s_dn, l * (E + 1) + 2 * q - 1)
                    load_down(l, q - 1, 1)
                    used(s_gu, l * E + 2 * q)
                    load_gate_up(l, q, 1)
                    used(s_dn, l * (E + 1) + 2 * q)
                    load_down(l, q, 0)
                used(s_dn, l * (E + 1) + E - 1)
                load_down(l, PAIRS - 1, 1)

            sp.sem_inc(s_down[1], 16)
            load_vectors(0)
            for j in range(4):
                load_mod(0, j)
                if j < 3:
                    load_in(0, j)
            load_small_weights(0)
            load_gate_bias(0)
            if DEPTH > 1:
                with sp.Fori(0, DEPTH - 1) as l:
                    rest_of(l)
                    filled(sp, l, "route")
                    load_vectors(l + 1)
                    load_small_weights(l + 1)
                    load_mod(l + 1, 0)
                    used(s_gu, (l + 1) * E)
                    load_in(l + 1, 0)
                    load_in(l + 1, 1)
                    used(s_dn, (l + 1) * (E + 1))
                    load_in(l + 1, 2)
                    sp.wait_ge(s_x, (l + 1) * 2 + 1)
                    load_gate_bias(l + 1)
                    for j in range(1, 4):
                        load_mod(l + 1, j)
            rest_of(DEPTH - 1)
            filled(sp, DEPTH - 1, "route")
            sp.dma_start(final_row, norm_final.partition_broadcast(P)).then_inc(s_nf, 16)
            for t in range(TB):
                sp.wait_ge(s_fin, t + 1)
                sp.dma_start(out[0, t * P:(t + 1) * P, :], actT[:].rearrange("p (t k) c -> p t (k c)", t=TB)[:, t]).then_inc(s_out, 16)
            sp.wait_ge(s_out, 32)

        @block.tensor
        def _(pe):
            expected = []

            def hold():
                pe.sem_inc(s_gate, 1)

            def fill(l, name, small=False):
                i = index[name]
                assert plan[i][0] == expected.pop(0), name
                if i >= 8:
                    drained(pe, l, plan[i - 8][0])
                if small:
                    hold()
                return banks[i % 8]

            def done(name, ins):
                ins.then_inc(s_fill[drainer[name]], 1)

            mm = nc.tensor.matmul

            def transposes(l, name, blocks, small=False):
                b = fill(l, name, small)
                for at, src in blocks:
                    n, w = src.shape[0], src.shape[1]
                    last = nc.tensor.transpose(b[0:w, at:at + n], src, con(C_IDENT, n, 0, n))
                done(name, last)

            pe.wait_ge(s_const, 16 * 7)
            nc.tensor.transpose(banks[0][:, 0:8], crow[:], con(C_IDENT, 8, 0, 8)).then_inc(s_setup["tensor"], 1)
            pe.wait_ge(s_x, 1)
            for t in range(TB):
                for s_ in (s_gu, s_hT, s_dn):
                    pe.sem_inc(s_[t], 1)
            with pe.Fori(0, DEPTH) as l:
                expected[:] = [n for n, _ in plan]

                def slot(i, loads):
                    pe.wait_ge(s_slot[i], l * SLOT_LOADS[i] + 16 * loads)

                pe.wait_ge(s_x, l * 2 + 1)
                pe.wait_ge(s_small, (l + 1) * 16 * SMALL)
                transposes(l, "vec", [(0, vec_rows[:])])

                def mod(j):
                    b = fill(l, f"mod{j}")
                    pe.wait_ge(s_acc, l * MODJ + j + 1)
                    if j in (4, 5, 10, 11):
                        last = mm(b[:], con(C_ONES, P), acc[:, j % 2], start=True, stop=True)
                    else:
                        for i in range(4):
                            last = mm(b[:, i:i + 1], acc[:, j % 2, i * P:(i + 1) * P], con(C_ONES, 1), start=True, stop=True)
                    done(f"mod{j}", last)

                def to_T(prefix, n):
                    pe.wait_ge(s_xn, l * 2 + n)
                    for j in range(4):
                        transposes(l, f"{prefix}{j}", [(kk * SEQ + t * P, xn[:, t, (2 * j + kk) * P:(2 * j + kk + 1) * P])
                                                       for kk in range(2) for t in range(TB)])

                for j in range(4):
                    mod(j)
                to_T("hT", 1)
                drained(pe, l, "hT2")
                drained(pe, l, "hT3")

                def cols(b, at, r, c0, k0=0):
                    for k in range(KD):
                        last = mm(b[:, at:at + SEQ], ring[:, r, k, c0:c0 + P], actT[:, k, :], start=k == 0, stop=k == KD - 1)
                    return last

                def rf(j):
                    b = fill(l, f"rf{j}")
                    if j % 2 == 0:
                        slot(j // 2, 1)
                    for i in range(2):
                        n = 2 * j + i
                        if n < NF:
                            last = cols(b, i * SEQ, n // 4, (n % 4) * P)
                    done(f"rf{j}", last)

                def tok(name, r, c0, n, t):
                    b = fill(l, name)
                    for k in range(KD):
                        last = mm(b[:, 0:n], actT[:, k, t * P:(t + 1) * P], ring[:, r, k, c0:c0 + n], start=k == 0, stop=k == KD - 1)
                    done(name, last)

                rf(0), rf(1), mod(4), rf(2), rf(3), mod(5), rf(4), mod(6), rf(5), mod(7)
                slot(0, 2)
                tok("q0", 0, 0, 384, 0), tok("q1", 0, 0, 384, 1)
                mod(8)
                b = fill(l, "cT")
                cols(b, 0, 0, 384)
                slot(1, 2)
                done("cT", cols(b, SEQ, 1, 0))
                tok("k0", 1, 128, 384, 0)
                mod(9)
                tok("k1", 1, 128, 384, 1)
                slot(2, 2)
                tok("g0", 2, 0, 402, 0)
                mod(10)
                tok("g1", 2, 0, 402, 1)
                slot(0, 3)
                tok("m0", 0, 0, 512, 0)
                mod(11)
                tok("m1", 0, 0, 512, 1)

                pe.wait_ge(s_smallw, (l + 1) * 16 * SMALLW)
                pe.wait_ge(s_lin, l * 2 + 1)
                pe.wait_ge(s_lsg, l + 1)
                for name, h, p0, p1, ft in (("lw", 0, 0, 64, 9), ("la", 0, 64, 128, 9), ("lg", 1, 0, 128, 10)):
                    for part, tiles in ((0, (0, 1)), (1, (2,))):
                        b = fill(l, f"{name}{part}")
                        for n, i in enumerate(tiles):
                            last = mm(b[:, n * SEQ:(n + 1) * SEQ], lora[p0:p1, h, i * P:(i + 1) * P],
                                      feat[p0:p1, ft, 1:SEQ + 1], start=True, stop=True)
                        done(f"{name}{part}", last)

                def headsums(prefix, src):
                    for part, (t0, t1) in ((0, (0, 2)), (1, (2, 3))):
                        b = fill(l, f"{prefix}{part}")
                        done(f"{prefix}{part}", mm(b[:, 0:(t1 - t0) * SEQ], con(C_BLK, P), src[:, t0:t1].rearrange("p i t -> p (i t)"),
                                                   start=True, stop=True))

                pe.wait_ge(s_sq, l + 1)
                headsums("kn", big[:, 5])
                pe.wait_ge(s_mix, l * 6 + 6)
                for t in range(TB):
                    transposes(l, f"rv{t}", [(i * P, feat[:, 6 + i, 1 + t * P:1 + (t + 1) * P]) for i in range(3)])
                pe.wait_ge(s_rk, l + 1)
                headsums("bo", big[:, 5])

                pe.wait_ge(s_rot, (l + 1) * 8)
                for i in range(5):
                    transposes(l, f"qk{i}", [(kk * SEQ + t * P, qrot[:, t, 2 * i + kk, :])
                                             for kk in range(2) if 2 * i + kk < 9 for t in range(TB)])

                b = fill(l, "ch")
                pe.wait_ge(s_cb, l + 1)
                hold()
                for kv in range(2):
                    for j in range(16):
                        last = mm(b[0:HD, kv * 2 * NC:(kv + 1) * 2 * NC], w1s[:, kv, j, :], blk[:, kv, j, :],
                                  start=j == 0, stop=j == 15)
                done("ch", last)
                b = fill(l, "ckv")
                pe.wait_ge(s_cgr, l + 1)
                hold()
                for h in range(NKV):
                    mm(b[0:NC, h * HD:(h + 1) * HD], cg[:, 3, h * NC:(h + 1) * NC], w2s[:, 0, :], start=True, stop=True)
                for h in range(NKV):
                    for i in range(3):
                        last = mm(b[32 * i:32 * i + NC, P + h * HD:P + (h + 1) * HD],
                                  cg[:, 3, (NKV + h) * NC:(NKV + h + 1) * NC], w2s[:, 1, :], start=True, stop=True)
                done("ckv", last)
                pe.wait_ge(s_ckr, l + 1)
                transposes(l, "ckT", [(0, ckr[:, 3, :])], small=True)
                drained(pe, l, "ckT")
                for h in range(NKV):
                    b = fill(l, f"cs{h}", small=True)
                    for t in range(TB):
                        for i in range(3):
                            at = (t * 3 + i) * NC
                            last = mm(b[:, at:at + NC], qkT[64 * h:64 * h + 64, i, t * P:(t + 1) * P],
                                      ckT[64 * h:64 * h + 64, :], start=True, stop=True)
                    done(f"cs{h}", last)
                pe.wait_ge(s_cp, l + 1)
                transposes(l, "cpT", [((t * 2 + h) * P, cPb[:, t, h, :]) for t in range(TB) for h in range(2)])
                drained(pe, l, "cpT")
                for t in range(TB):
                    b = fill(l, f"co{t}")
                    for h in range(2):
                        last = mm(b[:, h * 192:(h + 1) * 192], cpT[0:96, t, h, :], cVb[0:96, h, :], start=True, stop=True)
                    done(f"co{t}", last)

                pe.wait_ge(s_til, l * 4 + 4)
                for w, bi in (("a", 0), ("b", 4), ("k", 1)):
                    for t in range(TB):
                        transposes(l, f"row{w}{t}", [(i * P, big[:, bi, i, t * P:(t + 1) * P]) for i in range(3)])
                for kind, lhs in (("mb", 4), ("mk", 1)):
                    for hb in range(2):
                        for t in range(TB):
                            b = fill(l, f"{kind}{hb}{t}", small=True)
                            for i in range(3):
                                for c2 in range(2):
                                    s0 = t * P + c2 * CH
                                    for w, rhs in ((0, 0), (1, 2)):
                                        last = mm(b[64 * c2:64 * c2 + 64, (i * 2 + w) * CH:(i * 2 + w + 1) * CH],
                                                  big[64 * hb:64 * hb + 64, lhs, i, s0:s0 + CH],
                                                  big[64 * hb:64 * hb + 64, rhs, i, s0:s0 + CH], start=True, stop=True)
                            done(f"{kind}{hb}{t}", last)

                def diag(name, lhs, rhs, hb):
                    b = fill(l, name, small=True)
                    for t in range(TB):
                        for i in range(3):
                            at = (t * 3 + i) * CH
                            for c2 in range(2):
                                q = slice(64 * c2, 64 * c2 + 64)
                                last = mm(b[q, at:at + CH], lhs(q, t, i), rhs(q, t, i), start=True, stop=True)
                    done(name, last)

                def head(t):
                    if t < 16:
                        i, hb, kt, _, _ = head_of(t)
                        b = fill(l, f"S{t}", small=True)
                        q = slice(64 * hb, 64 * hb + 64)
                        mm(b[:, 0:P], qkT[q, i, 0:P], qkT[q, kt, 0:P], start=True, stop=True)
                        done(f"S{t}", mm(b[:, P:P + SEQ], qkT[q, i, P:SEQ], qkT[q, kt, :], start=True, stop=True))
                    if 1 <= t <= 16:
                        pe.wait_ge(s_ex, l * 16 + t)
                        transposes(l, f"T{t - 1}", [(n * P, Ssb[:, (t - 1) % 2, n * P:(n + 1) * P]) for n in range(3)])
                    if t >= 2:
                        u = t - 2
                        _, _, _, v, _ = head_of(u)
                        b = fill(l, f"O{u}")
                        drained(pe, l, f"T{u}")
                        hold()
                        mm(b[:, 0:HD], PTs[:, u % 2, 0:P], v(0), start=True, stop=True)
                        mm(b[:, HD:2 * HD], PTs[:, u % 2, P:2 * P], v(0), start=True, stop=False)
                        done(f"O{u}", mm(b[:, HD:2 * HD], PTs[:, u % 2, 2 * P:3 * P], v(1), start=False, stop=True))

                drained(pe, l, "rowk1")
                for kind, n in mixed_steps():
                    if kind == "head":
                        head(n)
                    elif kind == "x":
                        pe.wait_ge(s_mask, l * len(LEVELS) + n + 1)
                        if n:
                            drained(pe, l, f"tt{n - 1}1") if n > 1 else pe.wait_ge(s_mm, l * 2 + 2)
                        for b2 in range(2):
                            off = (mo0, mo1)[n % 2]
                            diag(f"x{n}{b2}", lambda q, t, i: off[q, b2, t, i, :],
                                 (lambda q, t, i: con(C_ID64, CH)[q, :]) if n == 0 else (lambda q, t, i: Tm[q, b2, t, i, :]), b2)
                    elif kind == "t":
                        drained(pe, l, f"x{n}1")
                        if n < len(LEVELS) - 1:
                            for b2 in range(2):
                                diag(f"t{n}{b2}", lambda q, t, i: TTm[q, b2, t, i, :], lambda q, t, i: Xm[q, b2, t, i, :], b2)
                        for b2 in range(2):
                            diag(f"tt{n}{b2}", lambda q, t, i: Xm[q, b2, t, i, :], lambda q, t, i: TTm[q, b2, t, i, :], b2)
                    elif kind == "w1":
                        for b2 in range(2):
                            diag(f"w1{b2}", lambda q, t, i: aak[q, b2, t, i, :],
                                 lambda q, t, i: rows[q, 0, t, (2 * i + b2) * HD:(2 * i + b2 + 1) * HD], b2)
                    elif kind == "tw":
                        drained(pe, l, "w11")
                        drained(pe, l, f"tt{len(LEVELS) - 1}1")
                        for b2 in range(2):
                            diag(f"ub{b2}", lambda q, t, i: TTm[q, b2, t, i, :], lambda q, t, i: W1[q, b2, t, i, :], b2)
                        for c2 in range(2):
                            b = fill(l, f"ta{c2}", small=True)
                            q = slice(64 * c2, 64 * c2 + 64)
                            for t in range(TB):
                                for i in range(3):
                                    for b2 in range(2):
                                        at = (t * 3 + i) * CH
                                        last = mm(b[64 * b2:64 * b2 + 64, at:at + CH],
                                                  rows[q, 1, t, (2 * i + b2) * HD:(2 * i + b2 + 1) * HD],
                                                  TTm[q, b2, t, i, :], start=True, stop=True)
                            done(f"ta{c2}", last)
                    elif kind == "u":
                        t, c2 = n // 2, n % 2
                        if n == 0:
                            drained(pe, l, "ta1")
                        else:
                            pe.wait_ge(s_st, l * (NCH - 1) + n)
                        for b2 in range(2):
                            b = fill(l, f"u{n}{b2}", small=True)
                            q = slice(64 * b2, 64 * b2 + 64)
                            for i in range(3):
                                last = mm(b[64 * c2:64 * c2 + 64, i * HD:(i + 1) * HD], TA[q, i, n, :], st[q, n, i, :],
                                          start=True, stop=True)
                            done(f"u{n}{b2}", last)
                    elif kind == "g":
                        t, c2 = n // 2, n % 2
                        b = fill(l, f"g{n}s")
                        drained(pe, l, f"u{n}1")
                        hold()
                        q = slice(64 * c2, 64 * c2 + 64)
                        for b2 in range(2):
                            for i in range(3):
                                hc = slice((2 * i + b2) * HD, (2 * i + b2 + 1) * HD)
                                o = b[64 * b2:64 * b2 + 64, i * HD:(i + 1) * HD]
                                mm(o, rows[q, 3, t, hc], rows[q, 0, t, hc], start=True, stop=False)
                                last = mm(o, rows[q, 2, t, hc], Um[q, b2, t, i, :], start=False, stop=True)
                        done(f"g{n}s", last)

                drained(pe, l, f"u{NCH - 1}1")
                for part, tiles in ((0, (0, 1)), (1, (2,))):
                    b = fill(l, f"ys{part}", small=True)
                    for n, i in enumerate(tiles):
                        for ch in range(NCH):
                            for b2 in range(2):
                                q = slice(64 * b2, 64 * b2 + 64)
                                last = mm(b[q, n * SEQ + ch * CH:n * SEQ + (ch + 1) * CH], st[q, ch, i, :],
                                          big[q, 2, i, ch * CH:(ch + 1) * CH], start=True, stop=True)
                    done(f"ys{part}", last)
                for c2 in range(2):
                    b = fill(l, f"yu{c2}", small=True)
                    q = slice(64 * c2, 64 * c2 + 64)
                    for t in range(TB):
                        for i in range(3):
                            for b2 in range(2):
                                o = b[64 * b2:64 * b2 + 64, (t * 3 + i) * CH:(t * 3 + i + 1) * CH]
                                mm(o, rows[q, 0, t, (2 * i + b2) * HD:(2 * i + b2 + 1) * HD], Ark[q, b2, t, i, :],
                                   start=True, stop=False)
                                last = mm(o, Um[q, b2, t, i, :], Arb[q, b2, t, i, :], start=False, stop=True)
                    done(f"yu{c2}", last)
                drained(pe, l, "yu1")
                headsums("gm", yT)
                pe.wait_ge(s_yv, l * 2 + 1)
                headsums("gv", ysq)

                pe.wait_ge(s_o, l + 1)
                srcs = [lambda t, i=i: onsa[:, t, i * P:(i + 1) * P] for i in range(3)]                     + [lambda t, i=i: omob[:, t, i * P:(i + 1) * P] for i in range(2)]
                for j, tiles in ((0, (0, 1)), (1, (2, 3)), (2, (4,))):
                    transposes(l, f"mT{j}", [(n * SEQ + t * P, srcs[i](t)) for n, i in enumerate(tiles) for t in range(TB)])
                drained(pe, l, "mT2")
                pe.wait_ge(s_mixT, l + 1)
                for half in range(2):
                    slot(1 + half, 3)
                    for t in range(TB):
                        b = fill(l, f"out{2 * half + t}")
                        for k in range(KD):
                            last = mm(b[:], actT[:, k, t * P:(t + 1) * P], ring[:, 1 + half, k, :], start=k == 0, stop=k == KD - 1)
                        done(f"out{2 * half + t}", last)
                to_T("h2T", 2)
                drained(pe, l, "h2T2")
                drained(pe, l, "h2T3")
                b = fill(l, "route")
                for t in range(TB):
                    for k in range(KD):
                        last = mm(b[:, t * E:(t + 1) * E], actT[:, k, t * P:(t + 1) * P], wrt[:, k, :], start=k == 0, stop=k == KD - 1)
                done("route", last)

                b = fill(l, "rank")
                pe.wait_ge(s_grp, l + 1)
                for t in range(TB):
                    o = b[:, 4 * t:4 * t + 4]
                    mm(o, before, group_of(t), start=True, stop=False)
                    if t:
                        mm(o, con(C_ONES, P), group_of(0), start=False, stop=False)
                    for t2 in range(TB):
                        mm(o, con(C_ONES, P), below_of(t2), start=False, stop=t2 == TB - 1)
                for t2 in range(TB):
                    last = mm(b[:, 8:12], con(C_ONES, P), below_of(t2), start=t2 == 0, stop=t2 == TB - 1)
                done("rank", last)
                pe.wait_ge(s_perm, l + 1)
                for j in range(4):
                    b = fill(l, f"hs{j}")
                    for kk in range(2):
                        k = 2 * j + kk
                        for t in range(TB):
                            last = mm(b[:, kk * SEQ:(kk + 1) * SEQ], xn[:, t, k * P:(k + 1) * P], perm[:, t], start=t == 0, stop=t == TB - 1)
                    done(f"hs{j}", last)
                b = fill(l, "combs")
                pe.wait_ge(s_comb, l + 1)
                for s_ in range(TB):
                    for t in range(TB):
                        last = mm(b[:, s_ * E:(s_ + 1) * E], perm[:, t, s_ * P:(s_ + 1) * P], comb[:, t], start=t == 0, stop=t == TB - 1)
                done("combs", last)
                transposes(l, "pT", [((s_ * TB + t) * P, perm[:, t, s_ * P:(s_ + 1) * P]) for s_ in range(TB) for t in range(TB)])
                assert not expected
                drained(pe, l, "combs")
                drained(pe, l, "pT")

                for n in range(4):
                    last = mm(banks[n][:], zero16[:, 0:P], zero16[:], start=True, stop=False)

                def down(t, j):
                    for half in range(2):
                        for kk in range(2):
                            last = mm(banks[2 * t + half][:], heT_s[:, t, kk, :],
                                      ring[:, 2, 4 * j + 2 * kk + half, :], start=False, stop=False)
                    last.then_inc(s_dn[t], 1)

                pe.wait_ge(s_count, l + 1)
                hold()
                with pe.Fori(0, PAIRS) as q:
                    before_, now = loads_counts(pe, q, 0), loads_counts(pe, q, 1)
                    for j in range(2):
                        n = l * E + 2 * q + j
                        nd = l * (E + 1) + 2 * q + j
                        pe.wait_ge(s_slot[j], l * SLOT_LOADS[j] + 48 + 32 * q + 32)
                        hold()
                        for t in range(TB):
                            with pe.If(now[t] > 0):
                                for k in range(KD):
                                    last = mm(banks[4 + t][:], actT[:, k, t * P:(t + 1) * P], ring[:, j, k, :], start=k == 0, stop=k == KD - 1)
                                last.then_inc(s_gu[t], 1)
                            with pe.Else():
                                skip(pe, s_gu[t], n + 1)
                        pe.wait_ge(s_down[1 - j], (l * PAIRS + q + 1) * 16)
                        hold()
                        for t in range(TB):
                            with pe.If((before_, now)[j][t] > 0):
                                pe.wait_ge(s_hTs[t], n + 1)
                                down(t, 1 - j)
                            with pe.Else():
                                skip(pe, s_dn[t], nd + 1)
                        for t in range(TB):
                            with pe.If(now[t] > 0):
                                pe.wait_ge(s_he[t], n + 2)
                                for kk in range(2):
                                    last = nc.tensor.transpose(banks[6 + t][:, kk * P:(kk + 1) * P], he_s[:, t, kk * P:(kk + 1) * P], con(C_IDENT, P))
                                last.then_inc(s_hT[t], 1)
                            with pe.Else():
                                skip(pe, s_hT[t], n + 1)
                now = loads_counts(pe, PAIRS, 0)
                pe.wait_ge(s_down[1], ((l + 1) * PAIRS + 1) * 16)
                hold()
                for t in range(TB):
                    with pe.If(now[t] > 0):
                        pe.wait_ge(s_hTs[t], (l + 1) * E + 1)
                        down(t, 1)
                    with pe.Else():
                        skip(pe, s_dn[t], l * (E + 1) + E + 1)
                for n in (0, 2, 1, 3):
                    mm(banks[n][:], zero16[:, 0:P], zero16[:], start=False, stop=True).then_inc(s_y, 1)
                for half in range(2):
                    pe.wait_ge(s_ys["scalar"], l * 2 + half + 1)
                    pe.wait_ge(s_ys["vector"], l * 2 + half + 1)
                    for t in range(TB):
                        for s_ in range(TB):
                            last = mm(banks[4 + 2 * half + t][:], permT[:, s_, t * P:(t + 1) * P], ysort[:, s_, 512 * half:512 * half + 512],
                                      start=s_ == 0, stop=s_ == TB - 1)
                        last.then_inc(s_unsort, 1)

        @block.scalar
        def _(act):
            A = nc.scalar.activation
            su = Chain(act, s_setup["scalar"])
            act.wait_ge(s_setup["vector"], SET_C)
            su(A(cact[:, 8:16], cact[:, 0:8], ACT.Tanh, scale=0.5))
            act.wait_ge(s_setup["vector"], SET_ANG)
            for w in range(2):
                for half in range(2):
                    su(A(cosn[:, w, :, 32 * half:32 * half + 32], sub(rt, 96 * (3 + w), [3, 32]), ACT.Sin))

            def square_sum(a, srcs, at):
                for n, (src, w) in enumerate(srcs):
                    a.sync()
                    a(A(junk[:, 0:w], src, ACT.Square, accum_out=stat[:, at + n:at + n + 1]))
                a.sync()

            for t in range(TB):
                for s_ in (s_th, s_hTs):
                    act.sem_inc(s_[t], 1)
            with act.Fori(0, DEPTH) as l:
                a = Chain(act, s_as, l * A_STEPS)
                expected = [n for n, e in plan if e == "a"]

                def take(name):
                    assert expected.pop(0) == name, name
                    return filled(act, l, name)

                def free(ins):
                    ins.then_inc(s_drain["a"], 1)

                act.wait_ge(s_x, l * 2 + 1)
                square_sum(a, [(xs[:, t, :], D) for t in range(TB)], 0)
                act.sem_inc(s_ss, 1)

                def to_T(prefix, at):
                    for j in (0, 2):
                        b = take(f"{prefix}{j}")
                        for kk in range(2):
                            k = 2 * j + kk
                            ins = A(actT[:, k, :], b[:, kk * SEQ:(kk + 1) * SEQ], ACT.Identity,
                                    scale=amod[:, at // 2 + k:at // 2 + k + 1], bias=modc[:, at + k:at + k + 1])
                            if kk:
                                free(ins)

                to_T("hT", 0)
                for j in range(6):
                    b = take(f"rf{j}")
                    n = min(2, NF - 2 * j)
                    free(A(feat[:, 2 * j:2 * j + n, 1:SEQ + 1], b[:, 0:n * SEQ].rearrange("p (a t) -> p a t", a=n), ACT.Copy))
                b = take("cT")
                free(A(kcT, b[:].rearrange("p (a t) -> p a t", a=2), ACT.Copy))
                drained(act, l, "cT")
                for half in range(2):
                    for h in range(NKV):
                        act.dma_start(cS[64 * half:64 * half + 64, :, h, 0:SEQ - half], kcT[64 * h:64 * h + 64, :, half:SEQ]
                                      ).then_inc(s_cw, 16)
                act.wait_ge(s_mix, l * 6 + 6)
                A(feat[0:64, 9, 1:SEQ + 1], feat[0:64, 9, 1:SEQ + 1], ACT.Tanh).then_inc(s_lin, 1)
                A(feat[:, 10, 1:SEQ + 1], feat[:, 10, 1:SEQ + 1], ACT.Tanh, scale=0.5).then_inc(s_lin, 1)
                for name, dst, bias in (("lw", 0, 0), ("la", 3, 3), ("lg", 6, None)):
                    for part, tiles in ((0, (0, 1)), (1, (2,))):
                        b = take(f"{name}{part}")
                        for n, i in enumerate(tiles):
                            src = b[:, n * SEQ:(n + 1) * SEQ]
                            if bias is None:
                                ins = A(big[:, dst, i, :], src, ACT.Copy)
                            else:
                                ins = A(big[:, dst, i, :], src, ACT.Tanh, scale=0.5, bias=vx[:, bias + i:bias + i + 1])
                        free(ins)
                act.wait_ge(s_gt, l + 1)
                A(gsig[:], gsig[:], ACT.Tanh, scale=0.5).then_inc(s_gth, 1)
                act.wait_ge(s_cum, l + 1)
                a(A(big[:, 2], big[:, 1], ACT.Exp))
                a.sync()
                A(big[:, 0], big[:, 0], ACT.Exp)
                A(big[:, 1], big[:, 1], ACT.Exp, scale=-1.0).then_inc(s_exp, 1)
                act.wait_ge(s_kn, l + 1)
                A(big[:, 5], big[:, 5], ACT.Sqrt).then_inc(s_kni, 1)
                for t in range(TB):
                    free(A(rows[:, 0, t, :], take(f"rv{t}")[:, 0:RW], ACT.Copy))
                for i in range(5):
                    b = take(f"qk{i}")
                    n = min(2, 9 - 2 * i)
                    free(A(qkT[:, 2 * i:2 * i + n, :], b[:, 0:n * SEQ].rearrange("p (a t) -> p a t", a=n), ACT.Copy))
                act.wait_ge(s_ct, l + 1)
                A(cg[:, 2], cg[:, 1], ACT.Tanh, scale=math.sqrt(2 / math.pi)).then_inc(s_ct2, 1)
                act.wait_ge(s_cs, l + 1)
                A(cSb, cSb, ACT.Exp, scale=SCALE).then_inc(s_ce, 1)
                for n, w in enumerate("abk"):
                    for t in range(TB):
                        free(A(rows[:, 1 + n, t, :], take(f"row{w}{t}")[:, 0:RW], ACT.Copy))
                six = "p (t i s) -> p t i s"

                def six_of(b):
                    return b[:, 0:RW].rearrange(six, t=TB, i=3)

                for kind, n in mixed_steps():
                    if kind == "head":
                        if n < 16:
                            drained(act, l, f"S{n}")
                            for j, (c0, c1) in enumerate(((0, P), (P, 3 * P))):
                                ins = A(Ssb[:, n % 2, c0:c1], Ssb[:, n % 2, c0:c1], ACT.Exp, scale=-1.0,
                                        bias=amx[:, n, j:j + 1], accum_out=asm[:, n, j:j + 1])
                            ins.then_inc(s_ex, 1)
                        if 1 <= n <= 16:
                            free(A(PTs[:, (n - 1) % 2, :], take(f"T{n - 1}")[:, 0:3 * P], ACT.Copy))
                    elif kind == "x":
                        for b2 in range(2):
                            free(A(Xm[:, b2], six_of(take(f"x{n}{b2}")), ACT.Copy))
                    elif kind == "w1":
                        for b2 in range(2):
                            free(A(W1[:, b2], six_of(take(f"w1{b2}")), ACT.Copy))
                    elif kind == "tw":
                        for b2 in range(2):
                            free(A(Ub[:, b2], six_of(take(f"ub{b2}")), ACT.Copy))
                        for c2 in range(2):
                            free(A(TA.rearrange("p i (t c) s -> p c t i s", c=2)[:, c2], six_of(take(f"ta{c2}")), ACT.Copy))
                free(A(yT[:, 0:2, :], take("ys0")[:].rearrange("p (a t) -> p a t", a=2), ACT.Copy))
                free(A(yT[:, 2, :], take("ys1")[:, 0:SEQ], ACT.Copy))
                act.wait_ge(s_yv, l * 2 + 2)
                A(big[:, 5], big[:, 5], ACT.Sqrt).then_inc(s_yr, 1)
                act.wait_ge(s_on, l + 1)
                square_sum(a, [(onsa[:, t, :], NSA_W) for t in range(TB)] + [(omob[:, t, :], MOBA_W) for t in range(TB)], 2)
                act.sem_inc(s_ss, 1)
                for j, tiles in ((0, (0, 1)), (1, (2, 3)), (2, (4,))):
                    b = take(f"mT{j}")
                    for n, i in enumerate(tiles):
                        ins = A(actT[:, i, :], b[:, n * SEQ:(n + 1) * SEQ], ACT.Copy, scale=vec[:, V_NSA + i:V_NSA + i + 1])
                    free(ins)
                act.wait_ge(s_x, l * 2 + 2)
                square_sum(a, [(xs[:, t, :], D) for t in range(TB)], 6)
                act.sem_inc(s_ss, 1)
                to_T("h2T", 16)
                drained(act, l, "route")
                A(rt[:, 32:64], rt[:, 0:32], ACT.Tanh, scale=0.5).then_inc(s_rt, 1)
                to_T("hs", 16)
                free(A(permT, take("pT")[:].rearrange("p (s t) -> p s t", s=TB), ACT.Copy))
                assert not expected
                a.fill_up(A_STEPS)
                act.wait_ge(s_count, l + 1)
                with act.Fori(0, PAIRS) as q:
                    now = loads_counts(act, q, 1)
                    for j in range(2):
                        n = l * E + 2 * q + j
                        for t in range(TB):
                            with act.If(now[t] > 0):
                                act.wait_ge(s_gu[t], n + 2)
                                A(th_s[:, t, :], banks[4 + t][:, 0:FF], ACT.Tanh, scale=0.5).then_inc(s_th[t], 1)
                            with act.Else():
                                skip(act, s_th[t], n + 1)
                        for t in range(TB):
                            with act.If(now[t] > 0):
                                act.wait_ge(s_hT[t], n + 2)
                                A(heT_s[:, t], banks[6 + t][:, 0:FF].rearrange("p (k t) -> p k t", k=2), ACT.Copy).then_inc(s_hTs[t], 1)
                            with act.Else():
                                skip(act, s_hTs[t], n + 1)
                for half in range(2):
                    act.wait_ge(s_y, l * 4 + 2 * half + 1)
                    A(ysort[:, 0, 512 * half:512 * half + 512], banks[half][:], ACT.Copy).then_inc(s_ys["scalar"], 1)
            fa = Chain(act, s_am)
            act.wait_ge(s_x, 2 * DEPTH + 1)
            square_sum(fa, [(xs[:, t, :], D) for t in range(TB)], 8)
            act.sem_inc(s_ss, 1)

        @block.gpsimd
        def _(pool):
            g = nc.gpsimd
            su = Chain(pool, s_setup["gpsimd"])
            su(g.memset(posi[:], 0))
            su(g.memset(mhalf[:], -0.5))

            def inverse_root(src, w):
                return g.tensor_tensor(src, src, mhalf[:].to_broadcast([P, w]), ALU.pow)

            def rstd(base, n, at, w):
                pool.wait_ge(s_ms, base + n)
                inverse_root(stat[:, at:at + w], w).then_inc(s_rstd, 1)

            su.sync()
            with pool.Fori(0, DEPTH) as l:
                gc = Chain(pool, s_ps, l * G_STEPS)
                rstd(l * 3, 1, 0, 2)
                for n, (name, dsts) in enumerate((("q", None), ("k", (3, 4)), ("g", (5,)), ("m", (7,)))):
                    for t in range(TB):
                        pool.wait_ge(s_ra, l * 8 + 2 * n + t + 1)
                        pa, pb = ropeA[:, t], ropeB[:, t]
                        if name == "q":
                            v = [z[:, 0:384].rearrange("p (b i d) -> p i b d", b=2, i=3) for z in (pa, pb)]
                            o = qrot[:, t, 0:3, :].rearrange("p i (b d) -> p i b d", b=2)
                        else:
                            v = [z[:, 0:256].rearrange("p (i b d) -> p i b d", i=2, b=2) for z in (pa, pb)]
                            o = qrot[:, t, dsts[0]:dsts[0] + 2, :].rearrange("p i (b d) -> p i b d", b=2)
                        g.tensor_tensor(o[:, :, :, 0:32], v[0][:, :, :, 0:32], v[1][:, :, :, 32:64], ALU.subtract)
                        g.tensor_tensor(o[:, :, :, 32:64], v[0][:, :, :, 32:64], v[1][:, :, :, 0:32], ALU.add).then_inc(s_rot, 1)
                pool.wait_ge(s_cw, (l + 1) * 64)
                for kv in range(2):
                    w = cS[:, kv].rearrange("p h (m s) -> p s h m", s=CMP_STRIDE)
                    for hi in range(2):
                        pos = vec[:, V_POS + 16 * kv + 8 * hi:V_POS + 16 * kv + 8 * hi + 8]
                        ins = g.tensor_tensor(blk[:, kv, 8 * hi:8 * hi + 8, :].rearrange("p j (h n) -> p j h n", h=2),
                                              w[:, 0:16:2, :, hi:hi + NC], bc(bc(pos, 2, 2), 3, NC), ALU.add)
                ins.then_inc(s_cb, 1)
                drained(pool, l, "mb11")
                filled(pool, l, "bo1")
                for n in range(len(LEVELS)):
                    if n >= 2:
                        filled(pool, l, f"x{n - 2}1")
                    if n == 2:
                        pool.wait_ge(s_mm, l * 2 + 2)
                    off = (mo0, mo1)[n % 2].rearrange("p b t i s -> p (b t i) s")
                    g.tensor_tensor(off, Mst.rearrange("p b t i s -> p (b t i) s"), bc(con(C_LEVEL + n * CH, CH), 1, 12),
                                    ALU.mult).then_inc(s_mask, 1)
                rstd(l * 3, 2, 2, 4)
                rstd(l * 3, 3, 6, 2)
            rstd(DEPTH * 3, 1, 8, 2)

        @block.vector
        def _(dve):
            v = nc.vector
            su = Chain(dve, s_setup["vector"])
            ts, tt, stt = v.tensor_scalar, v.tensor_tensor, v.scalar_tensor_tensor
            dve.wait_ge(s_const, 16 * 7)
            dve.wait_ge(s_setup["tensor"], 1)
            su(v.tensor_copy(cact[:, 0:8], banks[0][:, 0:8]))
            assert su.n == SET_C
            ang, kk, r, sn, cs = (sub(rt, 96 * n, [3, 32]) for n in (0, 1, 2, 4, 3))
            C1 = round(2 * math.pi * 32) / 32
            C2 = round((2 * math.pi - C1) * 2 ** 18) / 2 ** 18
            C3 = 2 * math.pi - C1 - C2
            LIM = 3.1415925
            for ins in (lambda: v.tensor_copy(stat[:, 10:13], posi[:]),
                        lambda: tt(ang, bc(con(C_INV, 32), 1, 3), bc(stat[:, 10:13], 2, 32), ALU.mult),
                        lambda: ts(kk, ang, 1 / (2 * math.pi), 12582912.0, ALU.mult, ALU.add),
                        lambda: ts(kk, kk, 12582912.0, None, ALU.subtract),
                        lambda: stt(r, kk, -C1, ang, ALU.mult, ALU.add),
                        lambda: stt(r, kk, -C2, r, ALU.mult, ALU.add),
                        lambda: stt(r, kk, -C3, r, ALU.mult, ALU.add),
                        lambda: ts(sn, r, LIM, -LIM, ALU.min, ALU.max),
                        lambda: ts(cs, r, math.pi / 2, None, ALU.add),
                        lambda: ts(kk, cs, LIM, -2 * math.pi, ALU.is_gt, ALU.mult),
                        lambda: tt(cs, cs, kk, ALU.add),
                        lambda: ts(cs, cs, LIM, -LIM, ALU.min, ALU.max)):
                su(ins())
                su.sync()
            assert su.n == SET_ANG, su.n
            su(v.memset(zero16[:], 0.0))
            su(v.memset(st[:, 0], 0.0))
            dve.wait_ge(s_setup["scalar"], 5)
            su(stt(cact[:, 16:24], cact[:, 8:16], 1.0, cact[:, 0:8], ALU.add, ALU.mult))
            su.sync()
            su(ts(cact[:, 16:24], cact[:, 16:24], 0.5, None, ALU.mult))
            su.sync()
            for t in range(TB):
                for s_ in (s_t1, s_he):
                    dve.sem_inc(s_[t], 1)
            dve.sem_inc(s_x, 1)

            with dve.Fori(0, DEPTH) as l:
                d = Chain(dve, s_vs, l * V_STEPS)
                expected = [n for n, e in plan if e == "v"]

                def take(name):
                    assert expected.pop(0) == name, name
                    return filled(dve, l, name)

                def free(ins):
                    ins.then_inc(s_drain["v"], 1)

                def seq(*steps):
                    for s_ in steps:
                        d.sync()
                        d(s_())

                b = take("vec")
                free(v.tensor_copy(vec[:], b[:, 0:V_END]))
                drained(dve, l, "vec")
                d(ts(vx[:, 0:6], vec[:, V_W0:V_W0 + 6], 0.5, None, ALU.mult))
                d(ts(vx[:, 6:9], vec[:, V_KA:V_KA + 3], -1.0, 1.0, ALU.mult, ALU.add))
                d(v.memset(feat[:, :, 0:1], 0.0))

                def mod_sum(j):
                    o = acc[:, j % 2]
                    if j >= 2:
                        filled(dve, l, f"mod{j - 2}")
                    for h in range(2):
                        dve.wait_ge(s_modl[h], (l * MODJ + j + 1) * 16)
                        for k in range(4):
                            n = 4 * h + k
                            sc = cact[:, 16 + n:17 + n]
                            if n:
                                if k or n == 4:
                                    d.sync()
                                ins = stt(o, modw[:, h, k], sc, o, ALU.mult, ALU.add)
                            else:
                                ins = ts(o, modw[:, h, k], sc, None, ALU.mult)
                            if k < 3:
                                d(ins)
                        ins.then_inc(s_modu, 1)
                        dve.wait_ge(s_modu, l * 2 * MODJ + 2 * j + h + 1)
                    dve.sem_inc(s_acc, 1)

                def mod_out(j):
                    b = take(f"mod{j}")
                    if j in (4, 5, 10, 11):
                        if j == 4:
                            dve.wait_ge(s_grow, (l + 1) * 32)
                        o = gate_rows[:, j // 6, (j % 2) * 512:(j % 2) * 512 + 512]
                        free(tt(o, b[:], o, ALU.add))
                    else:
                        at = 4 * j if j < 4 else 4 * j - 8
                        free(tt(modc[:, at:at + 4], b[:, 0:4], vec[:, at:at + 4], ALU.add))

                for j in range(4):
                    mod_sum(j)
                    mod_out(j)
                drained(dve, l, "mod3")
                d(stt(amod[:, 0:8], modc[:, 8:16], 1.0, vec[:, V_NMIX:V_NMIX + 8], ALU.add, ALU.mult))

                def mean_square(n, at, cols):
                    dve.wait_ge(s_ss, l * 3 + n)
                    for c0, c1, w in cols:
                        ins = ts(stat[:, c0:c1], stat[:, c0:c1], 1.0 / w, EPS, ALU.mult, ALU.add)
                        if (c0, c1, w) != cols[-1]:
                            d(ins)
                    ins.then_inc(s_ms, 1)
                    dve.wait_ge(s_rstd, l * 3 + n)

                def normalised(n, at):
                    mean_square(n, at, [(at, at + 2, D)])
                    for t in range(TB):
                        ins = ts(xn[:, t], xs[:, t], stat[:, at + t:at + t + 1], None, ALU.mult)
                        if t == 0:
                            d(ins)
                    ins.then_inc(s_xn, 1)

                def to_T(prefix, at):
                    for j in (1, 3):
                        b = take(f"{prefix}{j}")
                        for k2 in range(2):
                            k = 2 * j + k2
                            ins = ts(actT[:, k, :], b[:, k2 * SEQ:(k2 + 1) * SEQ], amod[:, at // 2 + k:at // 2 + k + 1],
                                     modc[:, at + k:at + k + 1], ALU.mult, ALU.add)
                            if k2:
                                free(ins)

                d.sync()
                normalised(1, 0)
                to_T("hT", 0)

                def shift(j):
                    drained(dve, l, f"rf{j}")
                    n = min(2, NF - 2 * j)
                    if j:
                        dve.wait_ge(s_mix, l * 6 + j)
                    d(tt(dtmp[:, 0:n], feat[:, 2 * j:2 * j + n, 0:SEQ], feat[:, 2 * j:2 * j + n, 1:SEQ + 1], ALU.subtract))
                    d.sync()
                    for i in range(n):
                        f = feat[:, 2 * j + i, 1:SEQ + 1]
                        ins = stt(f, dtmp[:, i], vec[:, V_MU + 2 * j + i:V_MU + 2 * j + i + 1], f, ALU.mult, ALU.add)
                    ins.then_inc(s_mix, 1)

                mod_sum(4), shift(0), shift(1), mod_sum(5), mod_out(4), shift(2), shift(3)
                mod_sum(6), mod_out(5), shift(4), mod_sum(7), mod_out(6), shift(5)
                mod_sum(8), mod_out(7)

                def rope(name, t, n, parts, copies):
                    b = take(name)
                    if n >= 1:
                        dve.wait_ge(s_rot, l * 8 + 2 * n + t - 1)
                    for w, buf in ((0, ropeA), (1, ropeB)):
                        for o0, c0, heads in parts:
                            ins = tt(buf[:, t, o0:o0 + heads * HD].rearrange("p (h d) -> p h d", d=HD),
                                     b[:, c0:c0 + heads * HD].rearrange("p (h d) -> p h d", d=HD),
                                     bc(cosn[:, w, t, :], 1, heads), ALU.mult)
                            last = w == 1 and (o0, c0, heads) == parts[-1]
                            if last:
                                ins.then_inc(s_ra, 1)
                    for n_, (dst, c0, w) in enumerate(copies):
                        ins = v.tensor_copy(dst, b[:, c0:c0 + w])
                    return ins

                for t in range(TB):
                    rope(f"q{t}", t, 0, [(0, 0, 6)], [])
                    dve.wait_ge(s_ra, l * 8 + t + 1)
                    dve.sem_inc(s_drain["v"], 1)
                mod_sum(9), mod_out(8)
                free(rope("k0", 0, 1, [(0, 0, 2), (128, 256, 2)], [(vsel[:, 0, :], 128, 128)]))
                mod_sum(10), mod_out(9)
                free(rope("k1", 1, 1, [(0, 0, 2), (128, 256, 2)], [(vsel[:, 1, :], 128, 128)]))
                free(rope("g0", 0, 2, [(0, 146, 4)], [(vwin[:, 0, :], 0, 128), (gsig[:, 0, :], 128, 18)]))
                mod_sum(11), mod_out(10)
                free(rope("g1", 1, 2, [(0, 146, 4)], [(vwin[:, 1, :], 0, 128), (gsig[:, 1, :], 128, 18)]))
                drained(dve, l, "g1")
                dve.sem_inc(s_gt, 1)
                free(rope("m0", 0, 3, [(0, 0, 4)], [(vmob[:, 0, :], 256, 256)]))
                mod_out(11)
                free(rope("m1", 1, 3, [(0, 0, 4)], [(vmob[:, 1, :], 256, 256)]))
                drained(dve, l, "m1")
                d(stt(amod[:, 8:16], modc[:, 24:32], 1.0, vec[:, V_NFFN:V_NFFN + 8], ALU.add, ALU.mult))

                R, K, V = (feat[:, 3 * i:3 * i + 3, 1:SEQ + 1] for i in range(3))
                spare = mo1.rearrange("p b t i s -> p (b t i s)").rearrange("p (i t) -> p i t", i=3)
                for i in range(3):
                    d(ts(big[:, 4, i], K[:, i], vec[:, V_KK + i:V_KK + i + 1], None, ALU.mult))
                d.sync()
                tt(big[:, 5], big[:, 4], big[:, 4], ALU.mult).then_inc(s_sq, 1)
                dve.wait_ge(s_lin, l * 2 + 2)
                ts(feat[:, 10, 1:SEQ + 1], feat[:, 10, 1:SEQ + 1], 0.5, 0.5, ALU.mult, ALU.add).then_inc(s_lsg, 1)
                drained(dve, l, "lg1")
                d(ts(big[:, 0], big[:, 0], -DECAY / 2, -DECAY / 2, ALU.mult, ALU.add))
                d(ts(big[:, 3], big[:, 3], 0.5, 0.5, ALU.mult, ALU.add))
                d.sync()
                for i in range(3):
                    d(v.tensor_tensor_scan(big[:, 1, i], con(C_RESET, SEQ), big[:, 0, i], 0.0, ALU.mult, ALU.add))
                d.sync()
                tt(big[:, 0], big[:, 1], big[:, 0], ALU.subtract).then_inc(s_cum, 1)
                for i in range(3):
                    d(ts(spare[:, i], big[:, 3, i], vec[:, V_KA + i:V_KA + i + 1], vx[:, 6 + i:7 + i], ALU.mult, ALU.add))
                d.sync()
                d(tt(K, K, spare, ALU.mult))
                for part, (t0, t1) in ((0, (0, 2)), (1, (2, 3))):
                    b = take(f"kn{part}")
                    free(ts(big[:, 5, t0:t1].rearrange("p i t -> p (i t)"), b[:, 0:(t1 - t0) * SEQ], 1e-24, None, ALU.max))
                drained(dve, l, "kn1")
                v.reciprocal(big[:, 5], big[:, 5]).then_inc(s_kn, 1)
                dve.wait_ge(s_kni, l + 1)
                d(tt(big[:, 4], big[:, 4], big[:, 5], ALU.mult))
                d.sync()
                for i in range(3):
                    ins = stt(big[:, 5, i], R[:, i], vec[:, V_RK + i:V_RK + i + 1], K[:, i], ALU.mult, ALU.mult)
                ins.then_inc(s_rk, 1)
                dve.wait_ge(s_exp, l + 1)
                stt(big[:, 0].rearrange("p i t -> p (i t)"), big[:, 4].rearrange("p i t -> p (i t)"), -1.0,
                    big[:, 0].rearrange("p i t -> p (i t)"), ALU.mult, ALU.mult).then_inc(s_til, 1)
                dve.wait_ge(s_til, l * 4 + 1)
                d(tt(big[:, 4], big[:, 4], big[:, 3], ALU.mult))
                d.sync()
                tt(big[:, 4], big[:, 4], big[:, 1], ALU.mult).then_inc(s_til, 1)
                dve.wait_ge(s_til, l * 4 + 2)
                tt(big[:, 1], K, big[:, 1], ALU.mult).then_inc(s_til, 1)
                d(v.tensor_copy(pl[:], big[:, 2].rearrange("p i (n s) -> p i n s", n=NCH)[:, :, :, CH - 1]))
                d.sync()
                tt(big[:, 2], R, big[:, 2], ALU.mult).then_inc(s_til, 1)
                for part, (t0, t1) in ((0, (0, 2)), (1, (2, 3))):
                    b = take(f"bo{part}")
                    free(tt(big[:, 3, t0:t1], b[:, 0:(t1 - t0) * SEQ].rearrange("p (i t) -> p i t", t=SEQ), V[:, t0:t1], ALU.mult))
                dve.wait_ge(s_gth, l + 1)
                d(ts(gsig[:], gsig[:], 0.5, 0.5, ALU.mult, ALU.add))

                b = take("ch")
                free(v.tensor_copy(cg[:, 0], b[0:HD, 0:4 * NC]))
                drained(dve, l, "ch")
                seq(lambda: tt(cg[:, 1], cg[:, 0], cg[:, 0], ALU.mult),
                    lambda: ts(cg[:, 1], cg[:, 1], 0.044715, 1.0, ALU.mult, ALU.add))
                d.sync()
                tt(cg[:, 1], cg[:, 1], cg[:, 0], ALU.mult).then_inc(s_ct, 1)
                dve.wait_ge(s_ct2, l + 1)
                d(stt(cg[:, 3], cg[:, 2], 1.0, cg[:, 0], ALU.add, ALU.mult))
                d.sync()
                ts(cg[:, 3], cg[:, 3], 0.5, None, ALU.mult).then_inc(s_cgr, 1)
                filled(dve, l, "qk4")
                d(v.memset(cPb, 0.0))
                d(v.memset(cVb, 0.0))
                d.sync()
                b = take("ckv")
                for w in range(2):
                    d(tt(ckr[:, w, :].rearrange("p (h d) -> p h d", h=2), b[0:NC, 0:P].rearrange("p (h d) -> p h d", h=2),
                         bc(cosn[0:NC, w, 2, :], 1, 2), ALU.mult))
                for h in range(NKV):
                    for i in range(3):
                        ins = v.tensor_copy(cVb[32 * i:32 * i + NC, h, i * HD:(i + 1) * HD],
                                            b[32 * i:32 * i + NC, P + h * HD:P + (h + 1) * HD])
                free(ins)
                drained(dve, l, "ckv")
                kr = [ckr[:, w, :].rearrange("p (h d) -> p h d", h=2) for w in (0, 1, 3)]
                tt(kr[2][:, :, 0:32], kr[0][:, :, 0:32], kr[1][:, :, 32:64], ALU.subtract)
                tt(kr[2][:, :, 32:64], kr[0][:, :, 32:64], kr[1][:, :, 0:32], ALU.add).then_inc(s_ckr, 1)
                b = take("ckT")
                free(v.tensor_copy(ckT[:], b[:, 0:NC]))
                cbias = con(C_CBIAS, TB * NC).rearrange("p (t n) -> p t n", t=TB)
                for h in range(NKV):
                    b = take(f"cs{h}")
                    free(tt(cSb[:, h], b[:, 0:TB * 3 * NC].rearrange("p (t i n) -> p t i n", t=TB, i=3), bc(cbias, 2, 3), ALU.add))
                drained(dve, l, "cs1")
                c12 = cSb.rearrange("p h t i n -> p (h t i) n")
                d(v.tensor_reduce(cst2[:, 0:12], c12, AX, ALU.max))
                d.sync()
                tt(c12, c12, bc(cst2[:, 0:12], 2, NC), ALU.subtract).then_inc(s_cs, 1)
                dve.wait_ge(s_ce, l + 1)
                c01 = con(C_C01, TB * NC).rearrange("p (t n) -> p t n", t=TB)
                for h in range(NKV):
                    d(tt(cSb[:, h], cSb[:, h], bc(c01, 2, 3), ALU.mult))
                seq(lambda: v.tensor_reduce(cst2[:, 12:24], c12, AX, ALU.add),
                    lambda: ts(cst2[:, 12:24], cst2[:, 12:24], 1e-30, None, ALU.max),
                    lambda: v.reciprocal(cst2[:, 24:36], cst2[:, 12:24]))
                d.sync()
                w12 = cst2[:, 24:36].rearrange("p (h t i) -> p h t i", h=2, t=TB)
                d(tt(w12, w12, gsig[:].rearrange("p t (h i g) -> p h t i g", h=2, i=3)[:, :, :, :, 0], ALU.mult))
                d.sync()
                for h in range(NKV):
                    ins = tt(cPb[:, :, h, :].rearrange("p t (i n) -> p t i n", i=3)[:, :, :, 0:NC], cSb[:, h],
                             bc(w12[:, h], 3, NC), ALU.mult)
                    if h == 0:
                        d(ins)
                ins.then_inc(s_cp, 1)
                b = take("cpT")
                free(v.tensor_copy(cpT[0:96], b[0:96, :].rearrange("p (t h q) -> p t h q", t=TB, h=2)))
                for t in range(TB):
                    b = take(f"co{t}")
                    free(v.tensor_copy(onsa[:, t, :], b[:, 0:NSA_W]))

                def masked(dst, src, mask):
                    return tt(dst, src, bc(con(mask, CH), 1, 3), ALU.mult)

                for kind, first, second in (("mb", Mst, Arb), ("mk", aak, Ark)):
                    for hb in range(2):
                        for t in range(TB):
                            b = take(f"{kind}{hb}{t}")[:, 0:6 * CH].rearrange("p (i w s) -> p w i s", i=3, w=2)
                            d(masked(first[:, hb, t], b[:, 0], C_STRICT))
                            free(masked(second[:, hb, t], b[:, 1], C_INCL))

                def twelve(z):
                    return z.rearrange("p b t i s -> p (b t i) s")

                for kind, n in mixed_steps():
                    if kind == "head":
                        if n < 16:
                            b = take(f"S{n}")
                            if n >= 2:
                                filled(dve, l, f"T{n - 2}")
                            dve.sem_inc(s_vgate, 1)
                            for j, (c0, c1) in enumerate(((0, P), (P, 3 * P))):
                                ins = v.tensor_tensor_reduce(out=Ssb[:, n % 2, c0:c1], in0=b[:, c0:c1], in1=con(C_CAUSAL + c0, c1 - c0),
                                                             scale=-SCALE, scalar=3e38, op0=ALU.add, op1=ALU.min,
                                                             accum_out=amx[:, n, j:j + 1])
                            free(ins)
                        if n >= 2:
                            u = n - 2
                            branch, h = head_of(u)[4]
                            b = take(f"O{u}")
                            d(v.reciprocal(awt[:, u, :], asm[:, u, :]))
                            d.sync()
                            if branch:
                                d(tt(awt[:, u, :], awt[:, u, :], gsig[:, :, 3 * h + branch], ALU.mult))
                                d.sync()
                            o = (onsa if branch else omob)[:, :, h * HD:(h + 1) * HD]
                            for t in range(TB):
                                if branch:
                                    ins = stt(o[:, t], b[:, t * HD:(t + 1) * HD], awt[:, u, t:t + 1], o[:, t], ALU.mult, ALU.add)
                                else:
                                    ins = ts(o[:, t], b[:, t * HD:(t + 1) * HD], awt[:, u, t:t + 1], None, ALU.mult)
                                if t == 0:
                                    d(ins)
                            free(ins)
                    elif kind == "x" and n == 0:
                        drained(dve, l, "x01")
                        dve.wait_ge(s_mask, l * len(LEVELS) + 1)
                        i64 = bc(con(C_ID64, CH), 1, 12)
                        tt(twelve(Tm), twelve(Xm), i64, ALU.add).then_inc(s_mm, 1)
                        tt(twelve(TTm), twelve(mo0), i64, ALU.add).then_inc(s_mm, 1)
                    elif kind == "t":
                        for w, M_ in (("t", Tm), ("tt", TTm)):
                            if w == "t" and n == len(LEVELS) - 1:
                                continue
                            for b2 in range(2):
                                b = take(f"{w}{n}{b2}")
                                o = M_[:, b2].rearrange("p t i s -> p (t i s)")
                                free(tt(o, b[:, 0:RW], o, ALU.add))
                    elif kind == "u":
                        t, c2 = n // 2, n % 2
                        q = slice(64 * c2, 64 * c2 + 64)
                        for b2 in range(2):
                            b = take(f"u{n}{b2}")
                            free(tt(Um[q, b2, t], b[q, 0:3 * HD].rearrange("p (i s) -> p i s", i=3), Ub[q, b2, t], ALU.add))
                    elif kind == "g":
                        b = take(f"g{n}s")
                        free(tt(gtmp[:], b[:, 0:3 * HD].rearrange("p (i s) -> p i s", i=3), st[:, n], ALU.add))
                        drained(dve, l, f"g{n}s")
                        tt(st[:, n + 1], gtmp[:], bc(pl[:, :, n], 2, HD), ALU.mult).then_inc(s_st, 1)
                        dve.wait_ge(s_st, l * (NCH - 1) + n + 1)
                d.sync()
                drained(dve, l, "O15")
                dve.sem_inc(s_on, 1)
                drained(dve, l, "ys1")
                for c2 in range(2):
                    b = take(f"yu{c2}")
                    y4 = yT.rearrange("p i (t c s) -> p c t i s", t=TB, c=2)[:, c2]
                    free(tt(y4, b[:, 0:RW].rearrange("p (t i s) -> p t i s", t=TB, i=3), y4, ALU.add))
                drained(dve, l, "yu1")
                yf, sf, rf_ = (z.rearrange("p i t -> p (i t)") for z in (yT, ysq, big[:, 5]))
                for part, (c0, c1) in ((0, (0, 512)), (1, (512, 768))):
                    b = take(f"gm{part}")
                    free(stt(yf[:, c0:c1], b[:, 0:c1 - c0], -1.0 / HD, yf[:, c0:c1], ALU.mult, ALU.add))
                drained(dve, l, "gm1")
                tt(sf, yf, yf, ALU.mult).then_inc(s_yv, 1)
                for part, (c0, c1) in ((0, (0, 512)), (1, (512, 768))):
                    b = take(f"gv{part}")
                    free(ts(rf_[:, c0:c1], b[:, 0:c1 - c0], 1.0 / HD, GN_EPS, ALU.mult, ALU.add))
                drained(dve, l, "gv1")
                v.reciprocal(rf_, rf_).then_inc(s_yv, 1)
                dve.wait_ge(s_yr, l + 1)
                seq(lambda: tt(yf, yf, rf_, ALU.mult))
                d.sync()
                for i in range(3):
                    d(ts(yT[:, i], yT[:, i], vec[:, V_LNW + i:V_LNW + i + 1], vec[:, V_LNB + i:V_LNB + i + 1], ALU.mult, ALU.add))
                seq(lambda: tt(yf, yf, big[:, 3].rearrange("p i t -> p (i t)"), ALU.add))
                d.sync()
                tt(actT[:, 5:8, :], yT, big[:, 6], ALU.mult).then_inc(s_mixT, 1)
                mean_square(2, 2, [(2, 4, NSA_W), (4, 6, MOBA_W)])
                for t in range(TB):
                    d(ts(onsa[:, t], onsa[:, t], stat[:, 2 + t:3 + t], None, ALU.mult))
                for t in range(TB):
                    ins = ts(omob[:, t], omob[:, t], stat[:, 4 + t:5 + t], None, ALU.mult)
                    if t == 0:
                        d(ins)
                ins.then_inc(s_o, 1)

                def add_to_residual(b, g, t, half, signal):
                    h = slice(512 * half, 512 * half + 512)
                    tmp = junkv[:, (2 * half + t) % 2]
                    ins = tt(tmp, b[:], gate_rows[:, g, h], ALU.mult)
                    return ins, (lambda: tt(xs[:, t, h], xs[:, t, h], tmp, ALU.add))

                d(ts(before, con(C_CAUSAL, P), 0.0, None, ALU.is_lt))
                d(v.tensor_tensor_scan(iota[:, 0:P], con(C_ONES, P), con(C_ONES, P), -1.0, ALU.mult, ALU.add))
                d.sync()
                d(ts(iota[:, P:SEQ], iota[:, 0:P], float(P), None, ALU.add))
                for half in range(2):
                    for t in range(TB):
                        b = take(f"out{2 * half + t}")
                        d.sync()
                        ins, add = add_to_residual(b, 0, t, half, None)
                        free(ins)
                        drained(dve, l, f"out{2 * half + t}")
                        d(add())
                d.sync()
                dve.sem_inc(s_x, 1)
                normalised(3, 6)
                to_T("h2T", 16)

                b = take("route")
                free(v.tensor_copy(rt[:, 0:32], b[:, 0:32]))
                dve.wait_ge(s_rt, l + 1)
                aff, bia = rt[:, 32:64], rt[:, 64:96]
                d(ts(aff, aff, 0.5, 0.5, ALU.mult, ALU.add))
                d.sync()
                d(tt(bia.rearrange("p (t e) -> p t e", t=TB), aff.rearrange("p (t e) -> p t e", t=TB), bc(rbias[:], 1, TB), ALU.add))
                b8 = bia.rearrange("p (g e) -> p g e", e=4)
                d.sync()
                pair = rt[:, 96:144].rearrange("p (g n) -> p g n", n=6)
                for n, (e0, e1) in enumerate(((0, 1), (0, 2), (0, 3), (1, 2), (1, 3), (2, 3))):
                    d(tt(pair[:, :, n], b8[:, :, e0], b8[:, :, e1], ALU.add))
                d.sync()
                gs = rt[:, 144:152]
                d(v.tensor_reduce(gs, pair, AX, ALU.max))
                d.sync()

                def rank(dst, z, n, w):
                    gt, ge = (rt[:, o:o + 16 * n].rearrange("p (g a b) -> p g a b", a=4, b=4) for o in (w, w + 16 * n))
                    other, own = bc(z, 2, 4), bc(z, 3, 4)
                    d(tt(gt, other, own, ALU.is_gt))
                    d(tt(ge, other, own, ALU.is_ge))
                    d.sync()
                    m = con(C_LT, 16)
                    d(tt(rt[:, w + 16 * n:w + 32 * n].rearrange("p (g c) -> p g c", g=n),
                         rt[:, w + 16 * n:w + 32 * n].rearrange("p (g c) -> p g c", g=n), bc(m, 1, n), ALU.mult))
                    m2 = con(C_GT, 16)
                    d(tt(rt[:, w:w + 16 * n].rearrange("p (g c) -> p g c", g=n),
                         rt[:, w:w + 16 * n].rearrange("p (g c) -> p g c", g=n), bc(m2, 1, n), ALU.mult))
                    d.sync()
                    d(tt(gt, gt, ge, ALU.add))
                    d.sync()
                    d(v.tensor_reduce(dst, gt, AX, ALU.add))
                    d.sync()

                rank(rt[:, 152:160].rearrange("p (g a) -> p g a", g=TB), gs.rearrange("p (g a) -> p g a", g=TB), TB, 256)
                grp = rt[:, 152:160].rearrange("p (t g) -> p t g", t=TB)
                bel = rt[:, 576:584].rearrange("p (t g) -> p t g", t=TB)
                d(v.memset(bel[:, :, 0], 0.0))
                d(ts(grp, grp, 0.5, None, ALU.is_lt))
                d.sync()
                d(v.tensor_copy(bel[:, :, 1], grp[:, :, 0]))
                d(tt(bel[:, :, 2], grp[:, :, 0], grp[:, :, 1], ALU.add))
                d.sync()
                tt(bel[:, :, 3], bel[:, :, 2], grp[:, :, 2], ALU.add).then_inc(s_grp, 1)
                gt8 = rt[:, 160:192].rearrange("p (g a) -> p g a", g=8)
                rank(gt8, b8, 8, 320)
                b = take("rank")
                start = rt[:, 600:605]
                d(v.memset(start[:, 4:5], float(SEQ)))
                d(v.tensor_copy(start[:, 0:4], b[:, 8:12]))
                free(tt(rt[:, 592:600], b[:, 0:8], rt[:, 152:160], ALU.mult))
                drained(dve, l, "rank")
                seq(lambda: v.tensor_reduce(rt[:, 588:590], rt[:, 592:600].rearrange("p (t g) -> p t g", t=TB), AX, ALU.add))
                d.sync()
                for t in range(TB):
                    ins = ts(perm[:, t], iota, rt[:, 588 + t:589 + t], None, ALU.is_equal)
                    if t == 0:
                        d(ins)
                ins.then_inc(s_perm, 1)
                d(ts(rt[:, 160:192], rt[:, 160:192], 1.5, None, ALU.is_lt))
                sel = rt[:, 160:192]
                seq(lambda: tt(sel.rearrange("p (g e) -> p g e", e=4), sel.rearrange("p (g e) -> p g e", e=4), bc(rt[:, 152:160], 2, 4), ALU.mult),
                    lambda: tt(sel, sel, aff, ALU.mult),
                    lambda: v.tensor_reduce(rt[:, 192:194], sel.rearrange("p (t e) -> p t e", t=TB), AX, ALU.add),
                    lambda: v.reciprocal(rt[:, 194:196], rt[:, 192:194]),
                    lambda: ts(rt[:, 194:196], rt[:, 194:196], 0.5, None, ALU.mult))
                d.sync()
                tt(comb[:], sel.rearrange("p (t e) -> p t e", t=TB), bc(rt[:, 194:196], 2, E), ALU.mult).then_inc(s_comb, 1)
                cl, ov_ = rt[:, 608:613], rt[:, 640 - 6:639]
                cnt = rt[:, 614:632]
                d(v.memset(cnt[:, 0:2], 0.0))
                seq(lambda: ts(cl, start, float(P), None, ALU.min),
                    lambda: tt(ov_, start, cl, ALU.subtract))
                d.sync()
                for t, z in ((0, cl), (1, ov_)):
                    d(tt(cnt[:, 2:18].rearrange("p (g r t) -> p g r t", g=4, t=TB)[:, :, :, t], bc(z[:, 1:5], 2, 2), bc(z[:, 0:4], 2, 2), ALU.subtract))
                d.sync()
                v.tensor_copy(counts[:], cnt).then_inc(s_count, 1)
                to_T("hs", 16)
                b = take("combs")
                free(v.tensor_copy(combs, b[:, 0:2 * E].rearrange("p (t e) -> p t e", t=TB)))
                drained(dve, l, "combs")
                dve.wait_ge(s_count, l + 1)
                assert not expected, expected
                d.fill_up(V_STEPS)

                with dve.Fori(0, PAIRS) as q:
                    now = loads_counts(dve, q, 1)
                    for j in range(2):
                        for t in range(TB):
                            n = l * E + 2 * q + j
                            with dve.If(now[t] > 0):
                                dve.wait_ge(s_th[t], n + 2)
                                b = banks[4 + t]
                                stt(t1_s[:, t], th_s[:, t], 1.0, b[:, 0:FF], ALU.add, ALU.mult).then_inc(s_t1[t], 1)
                                dve.wait_ge(s_t1[t], n + 2)
                                stt(he_s[:, t], t1_s[:, t], combs[:, t, bass.ds(2 * q + j, 1)], b[:, FF:2 * FF],
                                    ALU.mult, ALU.mult).then_inc(s_he[t], 1)
                            with dve.Else():
                                skip(dve, s_t1[t], n + 1)
                                skip(dve, s_he[t], n + 1)
                for half in range(2):
                    dve.wait_ge(s_y, l * 4 + 2 * half + 2)
                    v.tensor_copy(ysort[:, 1, 512 * half:512 * half + 512], banks[2 + half][:]).then_inc(s_ys["vector"], 1)
                for half in range(2):
                    for t in range(TB):
                        n = 2 * half + t
                        dve.wait_ge(s_unsort, l * 4 + n + 1)
                        ins, add = add_to_residual(banks[4 + n], 1, t, half, None)
                        ins.then_inc(s_yd, 1)
                        dve.wait_ge(s_yd, l * 8 + 2 * n + 1)
                        add().then_inc(s_yd, 1)
                        dve.wait_ge(s_yd, l * 8 + 2 * n + 2)
                dve.sem_inc(s_x, 1)

            fv = Chain(dve, s_vm)
            dve.wait_ge(s_ss, DEPTH * 3 + 1)
            ts(stat[:, 8:10], stat[:, 8:10], 1.0 / D, EPS, ALU.mult, ALU.add).then_inc(s_ms, 1)
            dve.wait_ge(s_rstd, DEPTH * 3 + 1)
            dve.wait_ge(s_nf, 16)
            ov = actT[:].rearrange("p (t k) c -> p t (k c)", t=TB)
            for t in range(TB):
                stt(ov[:, t], xs[:, t], stat[:, 8 + t:9 + t], final_row, ALU.mult, ALU.mult).then_inc(s_fin, 1)


_INS = ["x", "c", "positions", "w_mod", "b_mod", "norm_mix", "norm_ffn", "w_in", "nsa_phi_w1", "nsa_phi_w2",
        "nsa_phi_pos", "rwkv_mu", "rwkv_w_up", "rwkv_w0", "rwkv_a_up", "rwkv_a0", "rwkv_g_up", "rwkv_k_k",
        "rwkv_k_a", "rwkv_r_k", "rwkv_ln_w", "rwkv_ln_b", "norm_nsa_out", "norm_moba_out", "w_out",
        "w_router", "router_bias", "moe_w_gate", "moe_w_up", "moe_w_down", "norm_final"]


def shape_table():
    import numpy as np
    z = np.zeros((P, C_END), np.float32)
    p = np.arange(P)[:, None]
    z[:, C_IDENT:C_IDENT + P] = p == np.arange(P)
    tri = np.where(np.arange(P)[None, :] > p, NEG, 0.0)
    z[:, C_CAUSAL:C_CAUSAL + P] = tri
    z[:, C_CAUSAL + 2 * P:C_CAUSAL + 3 * P] = tri
    z[:, C_BLK:C_BLK + P] = p // HD == np.arange(P) // HD
    z[:, C_ONES:C_ONES + P] = 1
    s, t = p % CH, np.arange(CH)[None, :]
    z[:, C_STRICT:C_STRICT + CH] = s < t
    z[:, C_INCL:C_INCL + CH] = s <= t
    for n, w in enumerate(LEVELS):
        z[:, C_LEVEL + n * CH:C_LEVEL + (n + 1) * CH] = (s // (2 * w) == t // (2 * w)) & (t % (2 * w) >= w) & (s % (2 * w) < w)
    z[:, C_ID64:C_ID64 + CH] = s == t
    z[:, C_RESET:C_RESET + SEQ] = np.arange(SEQ) % CH != 0
    for b in range(TB):
        seen = CMP_STRIDE * np.arange(NC) + CMP_BLOCK - 1 <= b * P + p
        z[:, C_CBIAS + b * NC:C_CBIAS + (b + 1) * NC] = np.where(seen, 0.0, NEG)
        z[:, C_C01 + b * NC:C_C01 + (b + 1) * NC] = seen
    a, o = np.divmod(np.arange(16), 4)
    z[:, C_LT:C_LT + 16] = o < a
    z[:, C_GT:C_GT + 16] = o > a
    z[:, C_INV:C_INV + 32] = (10000.0 ** (-np.arange(0, HD, 2) / HD)).astype(np.float32)
    return z


def kernel(**inputs):
    import numpy as _np
    import concourse.bacc as _bacc
    from concourse import mybir as _mybir
    from concourse.bass_utils import run_bass_kernel_spmd as _run

    nc = _bacc.Bacc("TRN2", target_bir_lowering=False, num_devices=1)
    arrays, args = {}, []
    for name, a in [(n, inputs[n]) for n in _INS] + [("shape_table", shape_table())]:
        a = _np.ascontiguousarray(a)
        arrays[f"in_{name}_dram"] = a
        args.append(nc.dram_tensor(f"in_{name}_dram", a.shape, _mybir.dt.from_np(a.dtype), kind="ExternalInput").ap())
    args.append(nc.dram_tensor("out_0_dram", (1, SEQ, D), F32, kind="ExternalOutput").ap())
    trunk(nc, *args)
    r = _run(nc, [arrays], core_ids=[0])
    return r.results[0]["out_0_dram"]
```

```python
import math
from contextlib import ExitStack

import concourse.bass as bass
from concourse import mybir

F32 = mybir.dt.float32
F32R = mybir.dt.float32r
BF16 = mybir.dt.bfloat16
I32 = mybir.dt.int32
ALU = mybir.AluOpType
ACT = mybir.ActivationFunctionType
AX = mybir.AxisListType.X

P = 128
SEQ, D, DEPTH = 256, 1024, 2
TB = SEQ // P
KD = D // P
HD = 64
NH, NKV = 6, 2
NSA_W, MOBA_W, RW = 384, 256, 384
CMP_BLOCK, CMP_STRIDE = 32, 16
NC = (SEQ - CMP_BLOCK) // CMP_STRIDE + 1
EPS, GN_EPS = 1e-6, 64e-5
DECAY = 0.606531
SCALE = HD ** -0.5
CH = 64
NCH = SEQ // CH
LEVELS = [1, 2, 4, 8, 16, 32]
E, FF = 16, 256
GROUPS = 4
PER_GROUP = E // GROUPS
NEG = -1e30
NF = 11

IN_SLOTS = [(1938, 512), (2450, 512), (2962, 384), (0, 512), (512, 512), (1024, 402), (1426, 512)]
RING = 3
MIX_SLOTS = len(IN_SLOTS) + 2
LAYER_SLOTS = MIX_SLOTS + 3 * E // 2
MODJ = 12

C_IDENT, C_CAUSAL, C_BLK, C_ONES = 0, 128, 512, 640
C_STRICT, C_INCL, C_LEVEL, C_ID64 = 768, 832, 896, 1280
C_RESET, C_CBIAS, C_C01, C_LT, C_GT, C_INV, C_END = 1344, 1600, 1630, 1660, 1676, 1692, 1724

V_MOD, V_NMIX, V_NFFN, V_MU, V_W0, V_A0, V_KK, V_KA, V_RK = 0, 32, 40, 48, 59, 62, 65, 68, 71
V_LNW, V_LNB, V_NSA, V_MOBA, V_POS, V_END = 74, 77, 80, 83, 85, 117


def bank_plan():
    p = [("vec", "v")] + [(f"mod{j}", "v") for j in range(4)]
    p += [(f"hT{j}", "av"[j % 2]) for j in range(4)]
    p += [("rf0", "a"), ("rf1", "a"), ("mod4", "v"), ("rf2", "a"), ("rf3", "a"), ("mod5", "v"),
          ("rf4", "a"), ("mod6", "v"), ("rf5", "a"), ("mod7", "v"), ("q0", "v"), ("q1", "v"),
          ("mod8", "v"), ("cT", "a"), ("k0", "v"), ("mod9", "v"), ("k1", "v"), ("g0", "v"),
          ("mod10", "v"), ("g1", "v"), ("m0", "v"), ("mod11", "v"), ("m1", "v")]
    p += [("lw0", "a"), ("lw1", "a"), ("la0", "a"), ("la1", "a"), ("lg0", "a"), ("lg1", "a")]
    p += [("kn0", "v"), ("kn1", "v"), ("rv0", "a"), ("rv1", "a")]
    p += [(f"qk{i}", "a") for i in range(5)]
    p += [("ch", "v"), ("bo0", "v"), ("bo1", "v"), ("rowa0", "a"), ("rowa1", "a"), ("ckv", "v"),
          ("rowb0", "a"), ("rowb1", "a"), ("ckT", "v"), ("rowk0", "a"), ("rowk1", "a"), ("cs0", "v"), ("cs1", "v")]
    p += [(f"mb{b}{t}", "v") for b in range(2) for t in range(2)] + [("cpT", "v")]
    p += [(f"mk{b}{t}", "v") for b in range(2) for t in range(2)] + [("co0", "v"), ("co1", "v")]
    for s in mixed_steps():
        p += step_banks(s)
    p += [("ys0", "a"), ("ys1", "a"), ("yu0", "v"), ("yu1", "v"), ("mT0", "a"), ("mT1", "a"), ("mT2", "a")]
    p += [("gm0", "v"), ("gm1", "v"), ("gv0", "v"), ("gv1", "v")]
    p += [(f"out{i}", "v") for i in range(4)]
    p += [(f"h2T{j}", "av"[j % 2]) for j in range(4)] + [("route", "v"), ("rank", "v")]
    p += [(f"hs{j}", "av"[j % 2]) for j in range(4)] + [("combs", "v"), ("pT", "a")]
    return p


def mixed_steps():
    serial = [("x", n) for n in range(len(LEVELS))]
    order, t = [], 0
    for n in range(len(LEVELS)):
        order.append(("x", n))
        order.append(("head", t))
        t += 1
        if n:
            order.append(("t", n))
            order.append(("head", t))
            t += 1
    order += [("w1", 0), ("head", t), ("tw", 0), ("head", t + 1)]
    t += 2
    for c in range(NCH):
        order += [("u", c)]
        if t < 18:
            order += [("head", t)]
            t += 1
        if c < NCH - 1:
            order += [("g", c)]
    while t < 18:
        order += [("head", t)]
        t += 1
    return order


def step_banks(step):
    kind, n = step
    if kind == "x":
        return [(f"x{n}{b}", "a") for b in range(2)]
    if kind == "t":
        last = n == len(LEVELS) - 1
        return ([] if last else [(f"t{n}{b}", "v") for b in range(2)]) + [(f"tt{n}{b}", "v") for b in range(2)]
    if kind == "w1":
        return [("w10", "a"), ("w11", "a")]
    if kind == "tw":
        return [("ub0", "a"), ("ub1", "a"), ("ta0", "a"), ("ta1", "a")]
    if kind == "u":
        return [(f"u{n}{b}", "v") for b in range(2)]
    if kind == "g":
        return [(f"g{n}s", "v")]
    return ([(f"S{n}", "v")] if n < 16 else []) + ([(f"T{n - 1}", "a")] if 1 <= n <= 16 else []) \
        + ([(f"O{n - 2}", "v")] if n >= 2 else [])


class Chain:

    def __init__(self, eng, sem, base=0):
        self.eng, self.sem, self.base, self.n = eng, sem, base, 0

    def __call__(self, ins):
        self.n += 1
        return ins.then_inc(self.sem, 1)

    def sync(self):
        self.eng.wait_ge(self.sem, self.base + self.n)

    def fill_up(self, total):
        assert self.n < total, self.n
        self.sync()
        self.eng.sem_inc(self.sem, total - self.n)


def trunk(nc, x, c, positions, w_mod, b_mod, norm_mix, norm_ffn, w_in, phi_w1, phi_w2, phi_pos,
          mu, w_up, w0, a_up, a0, g_up, k_k, k_a, r_k, ln_w, ln_b, nsa_out, moba_out, w_out,
          w_router, router_bias, moe_g, moe_u, moe_d, norm_final, table, out):
    with ExitStack() as ctx:
        at_byte = {}

        def sb(name, shape, dt=F32):
            at_byte[name] = -(-nc.sbuf_base // 32) * 32
            return ctx.enter_context(nc.sbuf_tensor(name, shape, dt))

        def split_part(name, shape, room_, column):
            return nc.alloc_sbuf_tensor_at(name, shape, F32R, offset=at_byte[room_] + 4 * column)

        def sem(name):
            return ctx.enter_context(nc.semaphore(name))

        ring = sb("weight_ring", [P, RING, 8, 512])
        modw = sb("modulation_ring", [P, 2, 4, 512])
        cst = sb("shape_constants", [P, C_END])
        xs = sb("residual", [P, TB, D])
        actT = sb("activations_T", [P, KD, SEQ])
        gate_rows = sb("gate_rows", [P, 2, D])
        vec_rows = sb("vector_rows", [V_END, P])
        vec = sb("vectors_T", [P, V_END])
        vx = sb("derived_vectors", [P, 9])
        modc = sb("modulation_T", [P, 32])
        amod = sb("norm_scale_T", [P, 16])
        acc = sb("modulation_acc", [P, 2, 512])
        FIRST = 4
        cact = sb("silu_c", [P, 24])
        crow = sb("c_rows", [8, P])
        cosn = sb("cos_sin", [P, 2, 3, HD])
        posi = sb("positions_i", [P, 3], I32)
        w1s = sb("phi_w1", [P, 2, 16, HD])
        w2s = sb("phi_w2", [HD, 2, HD])
        lora = sb("lora_up", [P, 2, RW])
        wrt = sb("router_w", [P, KD, E])
        rbias = sb("router_bias", [P, E])
        comb = sb("combine", [P, TB, E])
        stat = sb("norm_stats", [P, 16])
        mhalf = sb("minus_half", [P, 1])
        zero16 = sb("zeros_bf16", [P, 512], BF16)
        feat = sb("rwkv_features_T", [P, NF, SEQ + 1])
        big = sb("rwkv_T", [P, 7, 3, SEQ])
        rows = sb("rwkv_rows", [P, 4, TB, RW])
        aak = sb("rwkv_Aak", [P, 2, TB, 3, CH])
        mo1b = sb("rwkv_spare", [P, 2, TB, 3, CH])
        st = sb("rwkv_state", [P, NCH, 3, HD])
        dtmp = sb("shift_difference", [P, 2, SEQ])
        pl = sb("chunk_decay", [P, 3, NCH])
        gtmp = sb("state_sum", [P, 3, HD])
        room = sb("attention_room", [P, 8960])

        def sub(t, at, shape):
            n = 1
            for s in shape:
                n *= s
            flat = t[:, at:at + n]
            if len(shape) == 1:
                return flat
            names = "abcd"[:len(shape)]
            return flat.rearrange(f"p ({' '.join(names)}) -> p {' '.join(names)}", **dict(zip(names, shape)))

        qrot = sub(room, 0, [TB, 9, P])
        xn = sub(room, 0, [TB, D])
        cPb = sub(room, 0, [TB, 2, 96])
        cVb = sub(room, 384, [2, 192])
        cSb = sub(room, 768, [2, TB, 3, NC])
        cpT = sub(room, 960, [TB, 2, P])
        ropeA = sub(room, 2304, [2, 512])
        ropeB = sub(room, 3328, [2, 512])
        Ssb = sub(room, 2304, [2, 384])
        PTs = sub(room, 3328, [2, 384])
        vsel = sub(room, 4352, [TB, P])
        vwin = sub(room, 4608, [TB, P])
        vmob = sub(room, 4864, [TB, 256])
        qkT = sub(room, 5376, [9, SEQ])
        onsa = sub(room, 7680, [TB, NSA_W])
        omob = sub(room, 8448, [TB, MOBA_W])
        kcT = sub(room, 7680, [2, SEQ])
        junk = sub(room, 2304, [D])
        junkv = sub(room, 3328, [2, 512])
        rflat = rows[:].rearrange("p a t c -> p (a t c)")
        before = sub(rflat, 0, [P])
        iota = sub(rflat, P, [SEQ])
        perm = sub(rflat, 384, [TB, SEQ])
        permT = sub(rflat, 896, [TB, SEQ])
        th_s = sub(rflat, 1408, [2, FF])
        t1_s = sub(rflat, 1920, [2, FF])
        he_s = sub(rflat, 2432, [2, FF])
        gu_hi = [split_part("gate_up_high0", [P, KD, 512], "rwkv_T", 0),
                 split_part("gate_up_high1", [P, KD, 512], "attention_room", 0)]
        gu_lo = [split_part(f"gate_up_low{j}", [P, KD, 512], "weight_ring", 4096 * j) for j in range(2)]
        dn_hi = [split_part("down_high0", [P, 4, 512], "rwkv_features_T", 0),
                 split_part("down_high1", [P, 4, 512], "attention_room", 5376)]
        dn_lo = [split_part(f"down_low{j}", [P, 4, 512], "weight_ring", 8192 + 2048 * j) for j in range(2)]
        act_hi = split_part("h2_T_high", [P, KD, SEQ], "phi_w1", 0)
        act_lo = split_part("h2_T_low", [P, KD, SEQ], "activations_T", 0)
        heT_hi = split_part("hidden_T_high", [P, 2, 2, P], "rwkv_Aak", 0)
        heT_lo = split_part("hidden_T_low", [P, 2, 2, P], "rwkv_spare", 0)
        ysort = sub(room, 0, [TB, D])
        cS = sub(rflat, 768, [2, 2, SEQ])
        blk = sub(rflat, 1792, [2, 16, 2 * NC])
        cg = sub(rflat, 2752, [4, 4 * NC])[0:HD]
        ckr = sub(room, 1472, [4, P])[0:NC]
        ckT = sb("compress_kT", [P, NC])
        gsig = sb("branch_gates", [P, TB, 18])
        cst2 = sb("compress_stats", [P, 48])
        amx = sb("softmax_max", [P, 16, 2])
        asm = sb("softmax_sum", [P, 16, 2])
        awt = sb("softmax_weight", [P, 16, 2])
        rt = room[:, 4352:4992]
        combs = sub(rt, 0, [TB, E])
        counts = sb("block_counts", [P, 2 * (GROUPS + 1)], I32)

        final_row = sub(room, 7424, [D])
        Tm, TTm, Xm, mo0 = (big[:, i].rearrange("p i t -> p (i t)").rearrange(
            "p (b t i s) -> p b t i s", b=2, t=TB, i=3) for i in (0, 1, 4, 5))
        mo1 = mo1b[:]
        W1, Ub, Um = Xm, mo0, mo1
        TA = big[:, 0].rearrange("p i (n s) -> p i n s", n=NCH)
        ysq = big[:, 4]
        after_hi = big[:].rearrange("p a i t -> p (a i t)")[:, 4096:5120]
        acc_of = [acc[:, 0], acc[:, 1], after_hi[:, 0:512], after_hi[:, 512:1024]] + [acc[:, j % 2] for j in range(FIRST, MODJ)]
        fflat = feat[:].rearrange("p a b -> p (a b)")
        Mst, Arb, Ark = (sub(fflat, 768 * i, [2, TB, 3, CH]) for i in range(3))
        yT = sub(fflat, 0, [3, SEQ])

        def group_of(t):
            return rt[:, 152 + 4 * t:156 + 4 * t]

        def below_of(t):
            return rt[:, 576 + 4 * t:580 + 4 * t]

        def head_of(t):
            if t < 12:
                i, hb, branch = t % 6 // 2, t % 2, t // 6
                v = (vsel, vwin)[branch]
                h = 3 * hb + i
                return i, hb, 3 + branch, (lambda k: v[:, k, hb * HD:(hb + 1) * HD]), (branch + 1, h)
            i, hb = (t - 12) // 2, t % 2
            h = 2 * i + hb
            return 5 + i, hb, 7 + i, (lambda k: vmob[:, k, h * HD:(h + 1) * HD]), (0, h)

        banks = [ctx.enter_context(nc.psum_tensor(f"bank{i}", [P, 512], F32)) for i in range(8)]

        s_const = sem("constants_loaded")
        s_setup = {e: sem(f"{e}_setup_steps") for e in ("vector", "scalar", "tensor", "gpsimd")}
        s_vs, s_as, s_ps = sem("vector_steps"), sem("scalar_steps"), sem("gpsimd_steps")
        s_vm, s_am = sem("vector_moe_steps"), sem("scalar_moe_steps")
        s_gate = sem("tensor_gate")
        s_fill = {"a": sem("banks_filled_for_scalar"), "v": sem("banks_filled_for_vector")}
        s_drain = {"a": sem("banks_drained_by_scalar"), "v": sem("banks_drained_by_vector")}
        s_slot = [sem(f"ring_slot{i}_loaded") for i in range(RING)]
        s_modl = [sem(f"modulation_half{i}_loaded") for i in range(2)]
        s_modu = sem("modulation_half_used")
        s_acc = sem("modulation_chunk_summed")
        s_small = sem("layer_vectors_loaded")
        s_smallw = sem("layer_small_weights_loaded")
        s_grow = sem("gate_bias_loaded")
        s_gused = sem("gate_rows_used")
        s_ss = sem("square_sums_ready")
        s_ms = sem("mean_squares_ready")
        s_rstd = sem("rstd_ready")
        s_xn = sem("normalised_rows_ready")
        s_x = sem("residual_updated")
        s_mix = sem("features_shifted")
        s_lin = sem("lora_tanh_ready")
        s_lsg = sem("lora_sigmoid_ready")
        s_sq = sem("key_squares_ready")
        s_kn = sem("key_norms_inverted")
        s_kni = sem("key_norm_roots_ready")
        s_cum = sem("decay_sums_ready")
        s_exp = sem("decay_exponentials_ready")
        s_rk = sem("bonus_products_ready")
        s_til = sem("scaled_operands_ready")
        s_ra = sem("rope_products_ready")
        s_rot = sem("rope_rows_ready")
        s_cw = sem("compress_windows_ready")
        s_cb = sem("compress_blocks_ready")
        s_ct = sem("compress_tanh_in")
        s_ct2 = sem("compress_tanh_out")
        s_cgr = sem("compress_gelu_ready")
        s_ckr = sem("compress_key_rows_ready")
        s_cs = sem("compress_scores_ready")
        s_ce = sem("compress_exp_ready")
        s_cp = sem("compress_probs_ready")
        s_gs = sem("branch_gates_ready")
        s_mask = sem("level_masks_ready")
        s_mm = sem("inverse_matrix_ready")
        s_sc = sem("scores_masked")
        s_ex = sem("scores_exponentiated")
        s_yv = sem("centred_squares_and_variance_ready")
        s_yr = sem("variance_inverse_roots_ready")
        s_mixT = sem("rwkv_mix_ready")
        s_o = sem("attention_rows_ready")
        s_comb = sem("combine_ready")
        s_gu, s_th, s_t1, s_he, s_hT, s_hTs, s_dn = (
            [sem(f"{n}_block{t}") for t in range(TB)]
            for n in ("gate_up_filled", "gate_tanh_ready", "gate_product_ready", "hidden_ready", "hiddenT_filled",
                      "hiddenT_ready", "expert_down_done"))
        s_guw = [[sem(f"gate_up_half{c}_slot{j}_loaded") for j in range(2)] for c in range(2)]
        s_guread = [sem(f"gate_up_half0_read_block{t}") for t in range(TB)]
        s_hTl = [sem(f"hiddenT_low_block{t}") for t in range(TB)]
        s_guhi = [sem(f"gate_up_half{c}_high_ready") for c in range(2)]
        s_gulo = [sem(f"gate_up_half{c}_low_ready") for c in range(2)]
        s_dhi, s_dlo = sem("down_high_ready"), sem("down_low_ready")
        s_ahi, s_alo = sem("activations_high_ready"), sem("activations_low_ready")
        s_down = [sem(f"down_weights_half{j}_loaded") for j in range(2)]
        s_grp = sem("token_groups_ready")
        s_perm = sem("permutation_ready")
        s_count = sem("block_counts_ready")
        s_y = sem("expert_sum_filled")
        s_ys = {e: sem(f"expert_sum_copied_by_{e}") for e in ("scalar", "vector")}
        s_unsort = sem("expert_sum_unsorted")
        s_out = sem("output_stored")

        plan = bank_plan()
        index = {n: i for i, (n, _) in enumerate(plan)}
        assert len(index) == len(plan)
        order_of, total = {}, {"a": 0, "v": 0}
        for n, e in plan:
            total[e] += 1
            order_of[n] = total[e]
        drainer = dict(plan)

        def filled(eng, l, name):
            e = drainer[name]
            eng.wait_ge(s_fill[e], l * total[e] + order_of[name])
            return banks[index[name] % 8]

        def drained(eng, l, name):
            e = drainer[name]
            eng.wait_ge(s_drain[e], l * total[e] + order_of[name])

        def con(at, n, p0=0, p1=P):
            return cst[p0:p1, at:at + n]

        def bc(ap, axis, n):
            v = ap.unsqueeze(axis)
            shape = list(v.shape)
            shape[axis] = n
            return v.to_broadcast(shape)

        V_STEPS, A_STEPS, G_STEPS = 1024, 512, 256
        SET_C, SET_ANG = 1, 13
        SMALL, SMALLW = 15, 6

        SLOT_LOADS = 16 * MIX_SLOTS // RING
        PAIRS = E // 2

        def split_counts(l, q, j, c):
            return l * 2 * E + 4 * q + 2 * j + c + 1

        def parts(t_, k0=0):
            return [t_[:, k0 + 2 * c:k0 + 2 * c + 2] for c in range(2)]

        def skip(eng, sem_, n):
            eng.wait_ge(sem_, n)
            eng.sem_inc(sem_, 1)

        def load_counts(eng, g):
            return [eng.value_load(counts[0:1, bass.ds(2 * g + t, 1)], min_val=0, max_val=P) for t in range(TB)]
        s_on = sem("attention_values_ready")
        s_nf = sem("final_gain_loaded")
        s_fin = sem("output_ready")
        s_rt = sem("router_tanh_ready")
        s_gt = sem("branch_gates_in")
        s_gth = sem("branch_gates_tanh")
        s_st = sem("chunk_state_ready")
        s_vgate, s_pgate = sem("vector_gate"), sem("gpsimd_gate")
        s_pre = sem("next_modulation_steps")
        s_yd = sem("expert_sum_steps")

        block = ctx.enter_context(nc.Block())

        @block.sync
        def _(sp):
            def load_vectors(l):
                def put(r, n, src):
                    sp.dma_start(vec_rows[r:r + n, :], src).then_inc(s_small, 16)
                put(0, 16, b_mod[l, 0:2048].rearrange("(r c) -> r c", c=P))
                put(16, 16, b_mod[l, 3072:5120].rearrange("(r c) -> r c", c=P))
                for r, n, src in ((V_NMIX, 8, norm_mix), (V_NFFN, 8, norm_ffn), (V_MU, NF, mu), (V_W0, 3, w0),
                                  (V_A0, 3, a0), (V_KK, 3, k_k), (V_KA, 3, k_a), (V_LNW, 3, ln_w),
                                  (V_LNB, 3, ln_b), (V_NSA, 3, nsa_out), (V_MOBA, 2, moba_out)):
                    put(r, n, src[l].rearrange("(r c) -> r c", c=P))
                put(V_RK, 3, r_k[l].rearrange("(r h) c -> r (h c)", h=2))
                put(V_POS, 32, phi_pos[l].rearrange("k (j h) d -> (k j) (h d)", h=2))

            def load_small_weights(l):
                sp.dma_start(w2s[:], phi_w2[l].rearrange("k d e -> d k e")).then_inc(s_smallw, 16)
                sp.dma_start(lora[0:64, 0, :], w_up[l]).then_inc(s_smallw, 16)
                sp.dma_start(lora[64:128, 0, :], a_up[l]).then_inc(s_smallw, 16)
                sp.dma_start(lora[:, 1, :], g_up[l]).then_inc(s_smallw, 16)

            def load_phi(l):
                for kv in range(2):
                    sp.dma_start(w1s[:, kv], phi_w1[l, kv].rearrange("(j h) d e -> (h d) j e", h=2)).then_inc(s_smallw, 16)

            def load_gate_bias(l):
                for g, at in ((0, 2048), (1, 5120)):
                    sp.dma_start(gate_rows[:, g, :], b_mod[l, at:at + D].partition_broadcast(P)).then_inc(s_grow, 16)

            def load_mod_half(l, j, h, first=False):
                if not first:
                    sp.wait_ge(s_modu, l * 2 * MODJ + 2 * j + h - 1)
                sp.dma_start(modw[:, h], w_mod[l, 512 * h:512 * h + 512, bass.ds(512 * j, 512)]
                             .rearrange("(k p) n -> p k n", p=P)).then_inc(s_modl[h], 16)

            def load_mod(l, j, first=False):
                for h in range(2):
                    load_mod_half(l, j, h, first)

            def load_in(l, i):
                at, n = IN_SLOTS[i]
                sp.dma_start(ring[:, i % RING, :, 0:n], w_in[l, :, at:at + n].rearrange("(k p) n -> p k n", p=P)
                             ).then_inc(s_slot[i % RING], 16)

            def load_out(l, i):
                r = (len(IN_SLOTS) + i) % RING
                sp.dma_start(ring[:, r], w_out[l, :, 512 * i:512 * i + 512].rearrange("(k p) n -> p k n", p=P)
                             ).then_inc(s_slot[r], 16)

            sp.dma_start(crow[:], c[0].rearrange("(r c) -> r c", c=P)).then_inc(s_const, 16)
            sp.dma_start(cst[:], table[:, :]).then_inc(s_const, 16)
            sp.dma_start(xs[:], x[0].rearrange("(t p) d -> p t d", p=P)).then_inc(s_const, 16)
            sp.wait_ge(s_setup["gpsimd"], 1)
            sp.dma_start(posi[:, 0:2], positions[0].rearrange("(t p) -> p t", p=P), allow_slow_non_contiguous=True).then_inc(s_const, 16)
            sp.dma_start(posi[0:NC, 2:3], positions[0:1, CMP_BLOCK - 1:SEQ:CMP_STRIDE].rearrange("a n -> n a"), allow_slow_non_contiguous=True).then_inc(s_const, 16)
            sp.dma_start(wrt[:], w_router.rearrange("(k p) e -> p k e", p=P)).then_inc(s_const, 16)
            sp.dma_start(rbias[:], router_bias.partition_broadcast(P)).then_inc(s_const, 16)

            def load_gate_up(l, q, j, c):
                for w, at in ((moe_g, 0), (moe_u, FF)):
                    sp.dma_start(ring[:, j, 4 * c:4 * c + 4, at:at + FF],
                                 w[l, 2 * q + j, 512 * c:512 * c + 512].rearrange("(k p) n -> p k n", p=P)
                                 ).then_inc(s_guw[c][j], 16)

            def load_down(l, q, j):
                sp.dma_start(ring[:, 2, 4 * j:4 * j + 4, :].rearrange("p (k h) n -> p k (h n)", h=2),
                             moe_d[l, 2 * q + j].rearrange("(k p) n -> p k n", p=P)).then_inc(s_down[j], 16)

            def used(sems, n):
                for s_ in sems:
                    sp.wait_ge(s_, 1 + n)

            def rest_of(l, ahead):
                for j, slot, user in ((5, 3, "rf1"), (6, None, None), (7, 4, "rf3"), (8, None, None),
                                      (9, 5, "rf5"), (10, None, None), (11, 6, "cT")):
                    load_mod(l, j)
                    if slot:
                        filled(sp, l, user)
                        load_in(l, slot)
                for i, user in ((0, "k1"), (1, "g1")):
                    filled(sp, l, user)
                    load_out(l, i)
                filled(sp, l, "m1")
                for c in range(2):
                    load_gate_up(l, 0, 0, c)
                filled(sp, l, "out1")
                for c in range(2):
                    load_gate_up(l, 0, 1, c)
                filled(sp, l, "out3")
                load_down(l, 0, 0)
                if ahead:
                    load_mod(l + 1, 0)

                def pair(q):
                    for j in range(2):
                        used(s_guread, l * E + 2 * q + j - 1)
                        load_gate_up(l, q, j, 0)
                        used(s_gu, l * E + 2 * q + j - 1)
                        load_gate_up(l, q, j, 1)
                        used(s_dn, l * (E + 1) + 2 * q + j - 1)
                        load_down(l, q + j - 1, 1 - j)

                pair(1)
                with sp.Fori(1, GROUPS) as g:
                    for h in range(2):
                        pair(2 * g + h)
                        if ahead:
                            load_mod_half(l + 1, g, h)
                used(s_dn, l * (E + 1) + E - 1)
                load_down(l, PAIRS - 1, 1)

            load_vectors(0)
            for j in range(FIRST):
                load_mod(0, j, first=j == 0)
            load_in(0, 0)
            load_mod(0, FIRST)
            for i in range(1, 3):
                load_in(0, i)
            load_small_weights(0)
            load_phi(0)
            load_gate_bias(0)
            if DEPTH > 1:
                with sp.Fori(0, DEPTH - 1) as l:
                    rest_of(l, True)
                    filled(sp, l, "pT")
                    load_vectors(l + 1)
                    load_small_weights(l + 1)
                    load_mod(l + 1, FIRST)
                    used(s_gu, (l + 1) * E - 1)
                    load_in(l + 1, 0)
                    used(s_gu, (l + 1) * E)
                    load_in(l + 1, 1)
                    used(s_dn, (l + 1) * (E + 1))
                    load_in(l + 1, 2)
                    load_phi(l + 1)
                    sp.wait_ge(s_x, (l + 1) * 2 + 1)
                    load_gate_bias(l + 1)
            rest_of(DEPTH - 1, False)
            filled(sp, DEPTH - 1, "route")
            sp.dma_start(final_row, norm_final.partition_broadcast(P)).then_inc(s_nf, 16)
            for t in range(TB):
                sp.wait_ge(s_fin, t + 1)
                sp.dma_start(out[0, t * P:(t + 1) * P, :], actT[:].rearrange("p (t k) c -> p t (k c)", t=TB)[:, t]).then_inc(s_out, 16)
            sp.wait_ge(s_out, 32)

        @block.tensor
        def _(pe):
            expected = []

            def hold():
                pe.sem_inc(s_gate, 1)

            def fill(l, name, small=False):
                i = index[name]
                assert plan[i][0] == expected.pop(0), name
                if i >= 8:
                    drained(pe, l, plan[i - 8][0])
                if small:
                    hold()
                return banks[i % 8]

            def done(name, ins):
                ins.then_inc(s_fill[drainer[name]], 1)

            mm = nc.tensor.matmul

            def transposes(l, name, blocks, small=False):
                b = fill(l, name, small)
                for at, src in blocks:
                    n, w = src.shape[0], src.shape[1]
                    last = nc.tensor.transpose(b[0:w, at:at + n], src, con(C_IDENT, n, 0, n))
                done(name, last)

            pe.wait_ge(s_const, 16 * 7)
            nc.tensor.transpose(banks[0][:, 0:8], crow[:], con(C_IDENT, 8, 0, 8)).then_inc(s_setup["tensor"], 1)
            pe.wait_ge(s_x, 1)
            for t in range(TB):
                for s_ in (s_guread, s_gu, s_hT, s_dn):
                    pe.sem_inc(s_[t], 1)
            with pe.Fori(0, DEPTH) as l:
                expected[:] = [n for n, _ in plan]

                def slot(i, loads):
                    pe.wait_ge(s_slot[i], l * SLOT_LOADS + 16 * loads)

                pe.wait_ge(s_small, (l + 1) * 16 * SMALL)
                transposes(l, "vec", [(0, vec_rows[:])])

                def mod(j):
                    b = fill(l, f"mod{j}")
                    pe.wait_ge(s_acc, l * MODJ + j + 1)
                    if j in (4, 5, 10, 11):
                        last = mm(b[:], con(C_ONES, P), acc_of[j], start=True, stop=True)
                    else:
                        for i in range(4):
                            last = mm(b[:, i:i + 1], acc_of[j][:, i * P:(i + 1) * P], con(C_ONES, 1), start=True, stop=True)
                    done(f"mod{j}", last)

                def to_T(prefix, n):
                    pe.wait_ge(s_xn, l * 2 + n)
                    for j in range(4):
                        transposes(l, f"{prefix}{j}", [(kk * SEQ + t * P, xn[:, t, (2 * j + kk) * P:(2 * j + kk + 1) * P])
                                                       for kk in range(2) for t in range(TB)])

                for j in range(FIRST):
                    if j == FIRST - 1:
                        pe.wait_ge(s_x, l * 2 + 1)
                    mod(j)
                to_T("hT", 1)
                drained(pe, l, "hT2")
                drained(pe, l, "hT3")

                def cols(b, at, r, c0, k0=0):
                    for k in range(KD):
                        last = mm(b[:, at:at + SEQ], ring[:, r, k, c0:c0 + P], actT[:, k, :], start=k == 0, stop=k == KD - 1)
                    return last

                def rf(j):
                    b = fill(l, f"rf{j}")
                    if j % 2 == 0:
                        slot(j // 2, 1)
                    for i in range(2):
                        n = 2 * j + i
                        if n < NF:
                            last = cols(b, i * SEQ, n // 4, (n % 4) * P)
                    done(f"rf{j}", last)

                def tok(name, r, c0, n, t):
                    b = fill(l, name)
                    for k in range(KD):
                        last = mm(b[:, 0:n], actT[:, k, t * P:(t + 1) * P], ring[:, r, k, c0:c0 + n], start=k == 0, stop=k == KD - 1)
                    done(name, last)

                rf(0), rf(1), mod(4), rf(2), rf(3), mod(5), rf(4), mod(6), rf(5), mod(7)
                slot(0, 2)
                tok("q0", 0, 0, 384, 0), tok("q1", 0, 0, 384, 1)
                mod(8)
                b = fill(l, "cT")
                cols(b, 0, 0, 384)
                slot(1, 2)
                done("cT", cols(b, SEQ, 1, 0))
                tok("k0", 1, 128, 384, 0)
                mod(9)
                tok("k1", 1, 128, 384, 1)
                slot(2, 2)
                tok("g0", 2, 0, 402, 0)
                mod(10)
                tok("g1", 2, 0, 402, 1)
                slot(0, 3)
                tok("m0", 0, 0, 512, 0)
                mod(11)
                tok("m1", 0, 0, 512, 1)

                pe.wait_ge(s_smallw, (l + 1) * 16 * SMALLW)
                pe.wait_ge(s_lin, l * 2 + 1)
                for name, h, p0, p1, ft in (("lw", 0, 0, 64, 9), ("la", 0, 64, 128, 9), ("lg", 1, 0, 128, 10)):
                    if name == "lg":
                        pe.wait_ge(s_lsg, l + 1)
                    for part, tiles in ((0, (0, 1)), (1, (2,))):
                        b = fill(l, f"{name}{part}")
                        for n, i in enumerate(tiles):
                            last = mm(b[:, n * SEQ:(n + 1) * SEQ], lora[p0:p1, h, i * P:(i + 1) * P],
                                      feat[p0:p1, ft, 1:SEQ + 1], start=True, stop=True)
                        done(f"{name}{part}", last)

                def headsums(prefix, src):
                    for part, (t0, t1) in ((0, (0, 2)), (1, (2, 3))):
                        b = fill(l, f"{prefix}{part}")
                        done(f"{prefix}{part}", mm(b[:, 0:(t1 - t0) * SEQ], con(C_BLK, P), src[:, t0:t1].rearrange("p i t -> p (i t)"),
                                                   start=True, stop=True))

                pe.wait_ge(s_sq, l + 1)
                headsums("kn", big[:, 5])
                pe.wait_ge(s_mix, l * 6 + 6)
                for t in range(TB):
                    transposes(l, f"rv{t}", [(i * P, feat[:, 6 + i, 1 + t * P:1 + (t + 1) * P]) for i in range(3)])
                pe.wait_ge(s_rot, (l + 1) * 8)
                for i in range(5):
                    transposes(l, f"qk{i}", [(kk * SEQ + t * P, qrot[:, t, 2 * i + kk, :])
                                             for kk in range(2) if 2 * i + kk < 9 for t in range(TB)])

                def scaled_rows(w, bi):
                    for t in range(TB):
                        transposes(l, f"row{w}{t}", [(i * P, big[:, bi, i, t * P:(t + 1) * P]) for i in range(3)])

                def chunk_products(kind, lhs):
                    for hb in range(2):
                        for t in range(TB):
                            b = fill(l, f"{kind}{hb}{t}", small=True)
                            for i in range(3):
                                for c2 in range(2):
                                    s0 = t * P + c2 * CH
                                    last = mm(b[64 * c2:64 * c2 + 64, i * 2 * CH:(i + 1) * 2 * CH],
                                              big[64 * hb:64 * hb + 64, lhs, i, s0:s0 + CH],
                                              big[64 * hb:64 * hb + 64, 0:3:2, i, s0:s0 + CH], start=True, stop=True)
                            done(f"{kind}{hb}{t}", last)

                b = fill(l, "ch")
                pe.wait_ge(s_cb, l + 1)
                hold()
                for kv in range(2):
                    for j in range(16):
                        last = mm(b[0:HD, kv * 2 * NC:(kv + 1) * 2 * NC], w1s[:, kv, j, :], blk[:, kv, j, :],
                                  start=j == 0, stop=j == 15)
                done("ch", last)
                pe.wait_ge(s_rk, l + 1)
                headsums("bo", big[:, 5])

                pe.wait_ge(s_til, l * 4 + 4)
                scaled_rows("a", 0)
                b = fill(l, "ckv")
                pe.wait_ge(s_cgr, l + 1)
                hold()
                for h in range(NKV):
                    mm(b[0:NC, h * HD:(h + 1) * HD], cg[:, 3, h * NC:(h + 1) * NC], w2s[:, 0, :], start=True, stop=True)
                for h in range(NKV):
                    for i in range(3):
                        last = mm(b[32 * i:32 * i + NC, P + h * HD:P + (h + 1) * HD],
                                  cg[:, 3, (NKV + h) * NC:(NKV + h + 1) * NC], w2s[:, 1, :], start=True, stop=True)
                done("ckv", last)
                scaled_rows("b", 4)
                pe.wait_ge(s_ckr, l + 1)
                transposes(l, "ckT", [(0, ckr[:, 3, :])], small=True)
                scaled_rows("k", 1)
                drained(pe, l, "ckT")
                for h in range(NKV):
                    b = fill(l, f"cs{h}", small=True)
                    for t in range(TB):
                        for i in range(3):
                            at = (t * 3 + i) * NC
                            last = mm(b[:, at:at + NC], qkT[64 * h:64 * h + 64, i, t * P:(t + 1) * P],
                                      ckT[64 * h:64 * h + 64, :], start=True, stop=True)
                    done(f"cs{h}", last)
                chunk_products("mb", 4)
                pe.wait_ge(s_cp, l + 1)
                transposes(l, "cpT", [((t * 2 + h) * P, cPb[:, t, h, :]) for t in range(TB) for h in range(2)])
                chunk_products("mk", 1)
                drained(pe, l, "cpT")
                for t in range(TB):
                    b = fill(l, f"co{t}")
                    for h in range(2):
                        last = mm(b[:, h * 192:(h + 1) * 192], cpT[0:96, t, h, :], cVb[0:96, h, :], start=True, stop=True)
                    done(f"co{t}", last)

                def diag(name, lhs, rhs, hb):
                    b = fill(l, name, small=True)
                    for t in range(TB):
                        for i in range(3):
                            at = (t * 3 + i) * CH
                            for c2 in range(2):
                                q = slice(64 * c2, 64 * c2 + 64)
                                last = mm(b[q, at:at + CH], lhs(q, t, i), rhs(q, t, i), start=True, stop=True)
                    done(name, last)

                def head(t):
                    if t < 16:
                        i, hb, kt, _, _ = head_of(t)
                        b = fill(l, f"S{t}", small=True)
                        q = slice(64 * hb, 64 * hb + 64)
                        mm(b[:, 0:P], qkT[q, i, 0:P], qkT[q, kt, 0:P], start=True, stop=True)
                        done(f"S{t}", mm(b[:, P:P + SEQ], qkT[q, i, P:SEQ], qkT[q, kt, :], start=True, stop=True))
                    if 1 <= t <= 16:
                        pe.wait_ge(s_ex, l * 16 + t)
                        transposes(l, f"T{t - 1}", [(n * P, Ssb[:, (t - 1) % 2, n * P:(n + 1) * P]) for n in range(3)])
                    if t >= 2:
                        u = t - 2
                        _, _, _, v, _ = head_of(u)
                        b = fill(l, f"O{u}")
                        drained(pe, l, f"T{u}")
                        hold()
                        mm(b[:, 0:HD], PTs[:, u % 2, 0:P], v(0), start=True, stop=True)
                        mm(b[:, HD:2 * HD], PTs[:, u % 2, P:2 * P], v(0), start=True, stop=False)
                        done(f"O{u}", mm(b[:, HD:2 * HD], PTs[:, u % 2, 2 * P:3 * P], v(1), start=False, stop=True))

                drained(pe, l, "rowk1")
                for kind, n in mixed_steps():
                    if kind == "head":
                        head(n)
                    elif kind == "x":
                        pe.wait_ge(s_mask, l * len(LEVELS) + n + 1)
                        if n:
                            drained(pe, l, f"tt{n - 1}1") if n > 1 else pe.wait_ge(s_mm, l * 2 + 2)
                        for b2 in range(2):
                            off = (mo0, mo1)[n % 2]
                            diag(f"x{n}{b2}", lambda q, t, i: off[q, b2, t, i, :],
                                 (lambda q, t, i: con(C_ID64, CH)[q, :]) if n == 0 else (lambda q, t, i: Tm[q, b2, t, i, :]), b2)
                    elif kind == "t":
                        drained(pe, l, f"x{n}1")
                        if n < len(LEVELS) - 1:
                            for b2 in range(2):
                                diag(f"t{n}{b2}", lambda q, t, i: TTm[q, b2, t, i, :], lambda q, t, i: Xm[q, b2, t, i, :], b2)
                        for b2 in range(2):
                            diag(f"tt{n}{b2}", lambda q, t, i: Xm[q, b2, t, i, :], lambda q, t, i: TTm[q, b2, t, i, :], b2)
                    elif kind == "w1":
                        for b2 in range(2):
                            diag(f"w1{b2}", lambda q, t, i: aak[q, b2, t, i, :],
                                 lambda q, t, i: rows[q, 0, t, (2 * i + b2) * HD:(2 * i + b2 + 1) * HD], b2)
                    elif kind == "tw":
                        drained(pe, l, "w11")
                        drained(pe, l, f"tt{len(LEVELS) - 1}1")
                        for b2 in range(2):
                            diag(f"ub{b2}", lambda q, t, i: TTm[q, b2, t, i, :], lambda q, t, i: W1[q, b2, t, i, :], b2)
                        for c2 in range(2):
                            b = fill(l, f"ta{c2}", small=True)
                            q = slice(64 * c2, 64 * c2 + 64)
                            for t in range(TB):
                                for i in range(3):
                                    for b2 in range(2):
                                        at = (t * 3 + i) * CH
                                        last = mm(b[64 * b2:64 * b2 + 64, at:at + CH],
                                                  rows[q, 1, t, (2 * i + b2) * HD:(2 * i + b2 + 1) * HD],
                                                  TTm[q, b2, t, i, :], start=True, stop=True)
                            done(f"ta{c2}", last)
                    elif kind == "u":
                        t, c2 = n // 2, n % 2
                        if n == 0:
                            drained(pe, l, "ta1")
                        else:
                            pe.wait_ge(s_st, l * (NCH - 1) + n)
                        for b2 in range(2):
                            b = fill(l, f"u{n}{b2}", small=True)
                            q = slice(64 * b2, 64 * b2 + 64)
                            for i in range(3):
                                last = mm(b[64 * c2:64 * c2 + 64, i * HD:(i + 1) * HD], TA[q, i, n, :], st[q, n, i, :],
                                          start=True, stop=True)
                            done(f"u{n}{b2}", last)
                    elif kind == "g":
                        t, c2 = n // 2, n % 2
                        b = fill(l, f"g{n}s")
                        drained(pe, l, f"u{n}1")
                        hold()
                        q = slice(64 * c2, 64 * c2 + 64)
                        for b2 in range(2):
                            for i in range(3):
                                hc = slice((2 * i + b2) * HD, (2 * i + b2 + 1) * HD)
                                o = b[64 * b2:64 * b2 + 64, i * HD:(i + 1) * HD]
                                mm(o, rows[q, 3, t, hc], rows[q, 0, t, hc], start=True, stop=False)
                                last = mm(o, rows[q, 2, t, hc], Um[q, b2, t, i, :], start=False, stop=True)
                        done(f"g{n}s", last)

                drained(pe, l, f"u{NCH - 1}1")
                for part, tiles in ((0, (0, 1)), (1, (2,))):
                    b = fill(l, f"ys{part}", small=True)
                    for n, i in enumerate(tiles):
                        for ch in range(NCH):
                            for b2 in range(2):
                                q = slice(64 * b2, 64 * b2 + 64)
                                last = mm(b[q, n * SEQ + ch * CH:n * SEQ + (ch + 1) * CH], st[q, ch, i, :],
                                          big[q, 2, i, ch * CH:(ch + 1) * CH], start=True, stop=True)
                    done(f"ys{part}", last)
                for c2 in range(2):
                    b = fill(l, f"yu{c2}", small=True)
                    q = slice(64 * c2, 64 * c2 + 64)
                    for t in range(TB):
                        for i in range(3):
                            for b2 in range(2):
                                o = b[64 * b2:64 * b2 + 64, (t * 3 + i) * CH:(t * 3 + i + 1) * CH]
                                mm(o, rows[q, 0, t, (2 * i + b2) * HD:(2 * i + b2 + 1) * HD], Ark[q, b2, t, i, :],
                                   start=True, stop=False)
                                last = mm(o, Um[q, b2, t, i, :], Arb[q, b2, t, i, :], start=False, stop=True)
                    done(f"yu{c2}", last)
                pe.wait_ge(s_o, l + 1)
                srcs = [lambda t, i=i: onsa[:, t, i * P:(i + 1) * P] for i in range(3)]                     + [lambda t, i=i: omob[:, t, i * P:(i + 1) * P] for i in range(2)]
                for j, tiles in ((0, (0, 1)), (1, (2, 3)), (2, (4,))):
                    transposes(l, f"mT{j}", [(n * SEQ + t * P, srcs[i](t)) for n, i in enumerate(tiles) for t in range(TB)])
                drained(pe, l, "yu1")
                headsums("gm", yT)
                pe.wait_ge(s_yv, l * 2 + 1)
                headsums("gv", ysq)

                drained(pe, l, "mT2")
                for half in range(2):
                    slot(1 + half, 3)
                outs = {(half, t): fill(l, f"out{2 * half + t}") for half in range(2) for t in range(TB)}
                for ks in (range(0, 5), range(5, KD)):
                    if ks[0]:
                        pe.wait_ge(s_mixT, l + 1)
                    for (half, t), b in outs.items():
                        for k in ks:
                            last = mm(b[:], actT[:, k, t * P:(t + 1) * P], ring[:, 1 + half, k, :], start=k == 0, stop=k == KD - 1)
                        if ks[0]:
                            done(f"out{2 * half + t}", last)
                to_T("h2T", 2)
                drained(pe, l, "h2T2")
                drained(pe, l, "h2T3")
                b = fill(l, "route")
                for t in range(TB):
                    for k in range(KD):
                        last = mm(b[:, t * E:(t + 1) * E], actT[:, k, t * P:(t + 1) * P], wrt[:, k, :], start=k == 0, stop=k == KD - 1)
                done("route", last)

                b = fill(l, "rank")
                pe.wait_ge(s_grp, l + 1)
                for t in range(TB):
                    o = b[:, 4 * t:4 * t + 4]
                    mm(o, before, group_of(t), start=True, stop=False)
                    if t:
                        mm(o, con(C_ONES, P), group_of(0), start=False, stop=False)
                    for t2 in range(TB):
                        mm(o, con(C_ONES, P), below_of(t2), start=False, stop=t2 == TB - 1)
                for t2 in range(TB):
                    last = mm(b[:, 8:12], con(C_ONES, P), below_of(t2), start=t2 == 0, stop=t2 == TB - 1)
                done("rank", last)
                pe.wait_ge(s_perm, l + 1)
                for j in range(4):
                    b = fill(l, f"hs{j}")
                    for kk in range(2):
                        k = 2 * j + kk
                        for t in range(TB):
                            last = mm(b[:, kk * SEQ:(kk + 1) * SEQ], xn[:, t, k * P:(k + 1) * P], perm[:, t], start=t == 0, stop=t == TB - 1)
                    done(f"hs{j}", last)
                b = fill(l, "combs")
                pe.wait_ge(s_comb, l + 1)
                for s_ in range(TB):
                    for t in range(TB):
                        last = mm(b[:, s_ * E:(s_ + 1) * E], perm[:, t, s_ * P:(s_ + 1) * P], comb[:, t], start=t == 0, stop=t == TB - 1)
                done("combs", last)
                transposes(l, "pT", [((s_ * TB + t) * P, perm[:, t, s_ * P:(s_ + 1) * P]) for s_ in range(TB) for t in range(TB)])
                assert not expected
                drained(pe, l, "combs")
                drained(pe, l, "pT")

                for n in range(4):
                    last = mm(banks[n][:], zero16[:, 0:P], zero16[:], start=True, stop=False)

                def split_product(out_, a_hi, a_lo, b_hi, b_lo, start=False, stop=False):
                    mm(out_, a_hi, b_hi, start=start, stop=False)
                    mm(out_, a_hi, b_lo, start=False, stop=False)
                    return mm(out_, a_lo, b_hi, start=False, stop=stop)

                def down(t, j):
                    for half in range(2):
                        for kk in range(2):
                            last = split_product(banks[2 * t + half][:], heT_hi[:, t, kk, :], heT_lo[:, t, kk, :],
                                                 dn_hi[j][:, 2 * kk + half], dn_lo[j][:, 2 * kk + half])
                    last.then_inc(s_dn[t], 1)

                pe.wait_ge(s_alo, l * 4 + 4)
                pe.wait_ge(s_count, l + 1)
                hold()
                with pe.Fori(0, GROUPS) as g:
                    now = load_counts(pe, g + 1)
                    for r in range(PER_GROUP):
                        q, j = 2 * g + r // 2, r % 2
                        n = l * E + 4 * g + r
                        nd = l * (E + 1) + 4 * g + r
                        for c, read in ((0, s_guread), (1, s_gu)):
                            pe.wait_ge(s_gulo[c], split_counts(l, q, j, 1))
                            hold()
                            for t in range(TB):
                                with pe.If(now[t] > 0):
                                    for k in range(4 * c, 4 * c + 4):
                                        tok_ = slice(t * P, (t + 1) * P)
                                        last = split_product(banks[4 + t][:], act_hi[:, k, tok_], act_lo[:, k, tok_],
                                                             gu_hi[j][:, k], gu_lo[j][:, k], k == 0, k == KD - 1)
                                    last.then_inc(read[t], 1)
                                with pe.Else():
                                    skip(pe, read[t], n + 1)
                        pe.wait_ge(s_dlo, split_counts(l, q, j, 1))
                        hold()
                        counts_before = now if r else load_counts(pe, g)
                        for t in range(TB):
                            with pe.If(counts_before[t] > 0):
                                pe.wait_ge(s_hTl[t], n + 1)
                                down(t, 1 - j)
                            with pe.Else():
                                skip(pe, s_dn[t], nd + 1)
                        for t in range(TB):
                            with pe.If(now[t] > 0):
                                pe.wait_ge(s_he[t], n + 2)
                                for kk in range(2):
                                    last = nc.tensor.transpose(banks[6 + t][:, kk * P:(kk + 1) * P], he_s[:, t, kk * P:(kk + 1) * P], con(C_IDENT, P))
                                last.then_inc(s_hT[t], 1)
                            with pe.Else():
                                skip(pe, s_hT[t], n + 1)
                now = load_counts(pe, GROUPS)
                pe.wait_ge(s_dlo, (l + 1) * 2 * E + 2)
                hold()
                for t in range(TB):
                    with pe.If(now[t] > 0):
                        pe.wait_ge(s_hTl[t], (l + 1) * E + 1)
                        down(t, 1)
                    with pe.Else():
                        skip(pe, s_dn[t], l * (E + 1) + E + 1)
                for n in (0, 2, 1, 3):
                    mm(banks[n][:], zero16[:, 0:P], zero16[:], start=False, stop=True).then_inc(s_y, 1)
                for half in range(2):
                    pe.wait_ge(s_ys["scalar"], l * 2 + half + 1)
                    pe.wait_ge(s_ys["vector"], l * 2 + half + 1)
                    for t in range(TB):
                        for s_ in range(TB):
                            last = mm(banks[4 + 2 * half + t][:], permT[:, s_, t * P:(t + 1) * P], ysort[:, s_, 512 * half:512 * half + 512],
                                      start=s_ == 0, stop=s_ == TB - 1)
                        last.then_inc(s_unsort, 1)

        @block.scalar
        def _(act):
            A = nc.scalar.activation
            su = Chain(act, s_setup["scalar"])
            act.wait_ge(s_setup["vector"], SET_C)
            su(A(cact[:, 8:16], cact[:, 0:8], ACT.Tanh, scale=0.5))
            act.wait_ge(s_setup["vector"], SET_ANG)
            for w in range(2):
                for half in range(2):
                    su(A(cosn[:, w, :, 32 * half:32 * half + 32], sub(rt, 96 * (3 + w), [3, 32]), ACT.Sin))

            def square_sum(a, srcs, at):
                for n, (src, w) in enumerate(srcs):
                    a.sync()
                    a(A(junk[:, 0:w], src, ACT.Square, accum_out=stat[:, at + n:at + n + 1]))
                a.sync()

            for t in range(TB):
                for s_ in (s_th, s_hTs):
                    act.sem_inc(s_[t], 1)
            with act.Fori(0, DEPTH) as l:
                a = Chain(act, s_as, l * A_STEPS)
                expected = [n for n, e in plan if e == "a"]

                def take(name):
                    assert expected.pop(0) == name, name
                    return filled(act, l, name)

                def free(ins):
                    ins.then_inc(s_drain["a"], 1)

                act.wait_ge(s_x, l * 2 + 1)
                square_sum(a, [(xs[:, t, :], D) for t in range(TB)], 0)
                act.sem_inc(s_ss, 1)

                def to_T(prefix, at):
                    for j in (0, 2):
                        b = take(f"{prefix}{j}")
                        for kk in range(2):
                            k = 2 * j + kk
                            ins = A(actT[:, k, :], b[:, kk * SEQ:(kk + 1) * SEQ], ACT.Identity,
                                    scale=amod[:, at // 2 + k:at // 2 + k + 1], bias=modc[:, at + k:at + k + 1])
                            if kk:
                                free(ins)

                to_T("hT", 0)
                for j in range(6):
                    b = take(f"rf{j}")
                    n = min(2, NF - 2 * j)
                    free(A(feat[:, 2 * j:2 * j + n, 1:SEQ + 1], b[:, 0:n * SEQ].rearrange("p (a t) -> p a t", a=n), ACT.Copy))
                b = take("cT")
                free(A(kcT, b[:].rearrange("p (a t) -> p a t", a=2), ACT.Copy))
                drained(act, l, "cT")
                for half in range(2):
                    for h in range(NKV):
                        act.dma_start(cS[64 * half:64 * half + 64, :, h, 0:SEQ - half], kcT[64 * h:64 * h + 64, :, half:SEQ]
                                      ).then_inc(s_cw, 16)
                act.wait_ge(s_mix, l * 6 + 6)
                A(feat[0:64, 9, 1:SEQ + 1], feat[0:64, 9, 1:SEQ + 1], ACT.Tanh).then_inc(s_lin, 1)
                A(feat[:, 10, 1:SEQ + 1], feat[:, 10, 1:SEQ + 1], ACT.Tanh, scale=0.5).then_inc(s_lin, 1)
                for name, dst, bias in (("lw", 0, 0), ("la", 3, 3), ("lg", 6, None)):
                    for part, tiles in ((0, (0, 1)), (1, (2,))):
                        b = take(f"{name}{part}")
                        for n, i in enumerate(tiles):
                            src = b[:, n * SEQ:(n + 1) * SEQ]
                            if bias is None:
                                ins = A(big[:, dst, i, :], src, ACT.Copy)
                            else:
                                ins = A(big[:, dst, i, :], src, ACT.Tanh, scale=0.5, bias=vx[:, bias + i:bias + i + 1])
                        free(ins)
                act.wait_ge(s_gt, l + 1)
                A(gsig[:], gsig[:], ACT.Tanh, scale=0.5).then_inc(s_gth, 1)
                act.wait_ge(s_cum, l + 1)
                a(A(big[:, 2], big[:, 1], ACT.Exp))
                a.sync()
                A(big[:, 0], big[:, 0], ACT.Exp)
                A(big[:, 1], big[:, 1], ACT.Exp, scale=-1.0).then_inc(s_exp, 1)
                act.wait_ge(s_kn, l + 1)
                A(big[:, 5], big[:, 5], ACT.Sqrt).then_inc(s_kni, 1)
                for t in range(TB):
                    free(A(rows[:, 0, t, :], take(f"rv{t}")[:, 0:RW], ACT.Copy))
                for i in range(5):
                    b = take(f"qk{i}")
                    n = min(2, 9 - 2 * i)
                    free(A(qkT[:, 2 * i:2 * i + n, :], b[:, 0:n * SEQ].rearrange("p (a t) -> p a t", a=n), ACT.Copy))
                act.wait_ge(s_ct, l + 1)
                A(cg[:, 2], cg[:, 1], ACT.Tanh, scale=math.sqrt(2 / math.pi)).then_inc(s_ct2, 1)
                for n, w in enumerate("abk"):
                    for t in range(TB):
                        free(A(rows[:, 1 + n, t, :], take(f"row{w}{t}")[:, 0:RW], ACT.Copy))
                act.wait_ge(s_cs, l + 1)
                A(cSb, cSb, ACT.Exp, scale=SCALE).then_inc(s_ce, 1)
                six = "p (t i s) -> p t i s"

                def six_of(b):
                    return b[:, 0:RW].rearrange(six, t=TB, i=3)

                for kind, n in mixed_steps():
                    if kind == "head":
                        if n < 16:
                            drained(act, l, f"S{n}")
                            for j, (c0, c1) in enumerate(((0, P), (P, 3 * P))):
                                ins = A(Ssb[:, n % 2, c0:c1], Ssb[:, n % 2, c0:c1], ACT.Exp, scale=-1.0,
                                        bias=amx[:, n, j:j + 1], accum_out=asm[:, n, j:j + 1])
                            ins.then_inc(s_ex, 1)
                        if 1 <= n <= 16:
                            free(A(PTs[:, (n - 1) % 2, :], take(f"T{n - 1}")[:, 0:3 * P], ACT.Copy))
                    elif kind == "x":
                        for b2 in range(2):
                            free(A(Xm[:, b2], six_of(take(f"x{n}{b2}")), ACT.Copy))
                    elif kind == "w1":
                        for b2 in range(2):
                            free(A(W1[:, b2], six_of(take(f"w1{b2}")), ACT.Copy))
                    elif kind == "tw":
                        for b2 in range(2):
                            free(A(Ub[:, b2], six_of(take(f"ub{b2}")), ACT.Copy))
                        for c2 in range(2):
                            free(A(TA.rearrange("p i (t c) s -> p c t i s", c=2)[:, c2], six_of(take(f"ta{c2}")), ACT.Copy))
                free(A(yT[:, 0:2, :], take("ys0")[:].rearrange("p (a t) -> p a t", a=2), ACT.Copy))
                free(A(yT[:, 2, :], take("ys1")[:, 0:SEQ], ACT.Copy))
                act.wait_ge(s_on, l + 1)
                square_sum(a, [(onsa[:, t, :], NSA_W) for t in range(TB)] + [(omob[:, t, :], MOBA_W) for t in range(TB)], 2)
                act.sem_inc(s_ss, 1)
                for j, tiles in ((0, (0, 1)), (1, (2, 3)), (2, (4,))):
                    b = take(f"mT{j}")
                    for n, i in enumerate(tiles):
                        ins = A(actT[:, i, :], b[:, n * SEQ:(n + 1) * SEQ], ACT.Copy, scale=vec[:, V_NSA + i:V_NSA + i + 1])
                    free(ins)
                act.wait_ge(s_yv, l * 2 + 2)
                A(big[:, 5], big[:, 5], ACT.Sqrt).then_inc(s_yr, 1)

                def high(sem_, dsts, srcs):
                    for dst, src in zip(dsts, srcs):
                        A(dst, src, ACT.Copy).then_inc(sem_, 1)

                def gate_up_high(q, j, c):
                    act.wait_ge(s_guw[c][j], (l * PAIRS + q + 1) * 32)
                    high(s_guhi[c], parts(gu_hi[j], 4 * c), parts(ring[:, j], 4 * c))

                def down_high(q, j):
                    act.wait_ge(s_down[j], (l * PAIRS + q + 1) * 16)
                    high(s_dhi, parts(dn_hi[j]), parts(ring[:, 2], 4 * j))

                act.wait_ge(s_mixT, l + 1)
                for c in range(2):
                    gate_up_high(0, 0, c)
                act.wait_ge(s_x, l * 2 + 2)
                square_sum(a, [(xs[:, t, :], D) for t in range(TB)], 6)
                act.sem_inc(s_ss, 1)
                to_T("h2T", 16)
                drained(act, l, "route")
                A(rt[:, 32:64], rt[:, 0:32], ACT.Tanh, scale=0.5).then_inc(s_rt, 1)
                for j in range(4):
                    if j % 2 == 0:
                        b = take(f"hs{j}")
                        for k in (2 * j, 2 * j + 1):
                            ins = A(actT[:, k, :], b[:, (k % 2) * SEQ:(k % 2 + 1) * SEQ], ACT.Identity,
                                    scale=amod[:, 8 + k:9 + k], bias=modc[:, 16 + k:17 + k])
                        free(ins)
                    drained(act, l, f"hs{j}")
                    A(act_hi[:, 2 * j:2 * j + 2], actT[:, 2 * j:2 * j + 2, :], ACT.Copy).then_inc(s_ahi, 1)
                free(A(permT, take("pT")[:].rearrange("p (s t) -> p s t", s=TB), ACT.Copy))
                assert not expected
                a.fill_up(A_STEPS)
                act.wait_ge(s_count, l + 1)

                with act.Fori(0, GROUPS) as g:
                    now = load_counts(act, g + 1)
                    for r in range(PER_GROUP):
                        q, j = 2 * g + r // 2, r % 2
                        n = l * E + 4 * g + r
                        ahead = (q + j, 1 - j)
                        if r < PER_GROUP - 1:
                            gate_up_high(*ahead, 0)
                        else:
                            with act.If(g < GROUPS - 1):
                                gate_up_high(*ahead, 0)
                        for t in range(TB):
                            with act.If(now[t] > 0):
                                act.wait_ge(s_gu[t], n + 2)
                                A(th_s[:, t, :], banks[4 + t][:, 0:FF], ACT.Tanh, scale=0.5).then_inc(s_th[t], 1)
                            with act.Else():
                                skip(act, s_th[t], n + 1)
                        if r < PER_GROUP - 1:
                            gate_up_high(*ahead, 1)
                        else:
                            with act.If(g < GROUPS - 1):
                                gate_up_high(*ahead, 1)
                        for t in range(TB):
                            with act.If(now[t] > 0):
                                act.wait_ge(s_hT[t], n + 2)
                                A(heT_hi[:, t], banks[6 + t][:, 0:FF].rearrange("p (k t) -> p k t", k=2), ACT.Copy).then_inc(s_hTs[t], 1)
                            with act.Else():
                                skip(act, s_hTs[t], n + 1)
                        down_high(q, j)

                for half in range(2):
                    act.wait_ge(s_y, l * 4 + 2 * half + 1)
                    A(ysort[:, 0, 512 * half:512 * half + 512], banks[half][:], ACT.Copy).then_inc(s_ys["scalar"], 1)
            fa = Chain(act, s_am)
            act.wait_ge(s_x, 2 * DEPTH + 1)
            square_sum(fa, [(xs[:, t, :], D) for t in range(TB)], 8)
            act.sem_inc(s_ss, 1)

        @block.gpsimd
        def _(pool):
            g = nc.gpsimd
            su = Chain(pool, s_setup["gpsimd"])
            su(g.memset(posi[:], 0))
            su(g.memset(mhalf[:], -0.5))

            def inverse_root(src, w):
                return g.tensor_tensor(src, src, mhalf[:].to_broadcast([P, w]), ALU.pow)

            def rstd(base, n, at, w):
                pool.wait_ge(s_ms, base + n)
                inverse_root(stat[:, at:at + w], w).then_inc(s_rstd, 1)

            su.sync()
            with pool.Fori(0, DEPTH) as l:
                gc = Chain(pool, s_ps, l * G_STEPS)
                rstd(l * 3, 1, 0, 2)
                for n, (name, dsts) in enumerate((("q", None), ("k", (3, 4)), ("g", (5,)), ("m", (7,)))):
                    for t in range(TB):
                        pool.wait_ge(s_ra, l * 8 + 2 * n + t + 1)
                        pa, pb = ropeA[:, t], ropeB[:, t]
                        if name == "q":
                            v = [z[:, 0:384].rearrange("p (b i d) -> p i b d", b=2, i=3) for z in (pa, pb)]
                            o = qrot[:, t, 0:3, :].rearrange("p i (b d) -> p i b d", b=2)
                        else:
                            v = [z[:, 0:256].rearrange("p (i b d) -> p i b d", i=2, b=2) for z in (pa, pb)]
                            o = qrot[:, t, dsts[0]:dsts[0] + 2, :].rearrange("p i (b d) -> p i b d", b=2)
                        g.tensor_tensor(o[:, :, :, 0:32], v[0][:, :, :, 0:32], v[1][:, :, :, 32:64], ALU.subtract)
                        g.tensor_tensor(o[:, :, :, 32:64], v[0][:, :, :, 32:64], v[1][:, :, :, 0:32], ALU.add).then_inc(s_rot, 1)
                pool.wait_ge(s_cw, (l + 1) * 64)
                for kv in range(2):
                    w = cS[:, kv].rearrange("p h (m s) -> p s h m", s=CMP_STRIDE)
                    for hi in range(2):
                        pos = vec[:, V_POS + 16 * kv + 8 * hi:V_POS + 16 * kv + 8 * hi + 8]
                        ins = g.tensor_tensor(blk[:, kv, 8 * hi:8 * hi + 8, :].rearrange("p j (h n) -> p j h n", h=2),
                                              w[:, 0:16:2, :, hi:hi + NC], bc(bc(pos, 2, 2), 3, NC), ALU.add)
                ins.then_inc(s_cb, 1)
                drained(pool, l, "mb11")
                filled(pool, l, "bo1")
                for n in range(len(LEVELS)):
                    if n >= 2:
                        filled(pool, l, f"x{n - 2}1")
                    if n == 2:
                        pool.wait_ge(s_mm, l * 2 + 2)
                    off = (mo0, mo1)[n % 2].rearrange("p b t i s -> p (b t i) s")
                    g.tensor_tensor(off, Mst.rearrange("p b t i s -> p (b t i) s"), bc(con(C_LEVEL + n * CH, CH), 1, 12),
                                    ALU.mult).then_inc(s_mask, 1)
                rstd(l * 3, 2, 2, 4)
                rstd(l * 3, 3, 6, 2)
                pool.wait_ge(s_count, l + 1)
                pool.sem_inc(s_pgate, 1)
                with pool.If(l < DEPTH - 1):
                    pre = Chain(pool, s_pre, l * FIRST * 5)
                    for j in range(FIRST):
                        o = acc_of[j]
                        for h in range(2):
                            w = modw[:, h]
                            pool.wait_ge(s_modl[h], ((l + 1) * MODJ + j + 1) * 16)
                            pre(g.tensor_tensor(w, w, bc(cact[:, 16 + 4 * h:20 + 4 * h], 2, 512), ALU.mult))
                            pre.sync()
                            pre(g.tensor_tensor(w[:, 0:2], w[:, 0:2], w[:, 2:4], ALU.add))
                            pre.sync()
                            if h:
                                pre(g.tensor_tensor(w[:, 0], w[:, 0], w[:, 1], ALU.add))
                                pre.sync()
                                ins = g.tensor_tensor(o, o, w[:, 0], ALU.add)
                            else:
                                ins = g.tensor_tensor(o, w[:, 0], w[:, 1], ALU.add)
                            ins.then_inc(s_modu, 1)
                            pool.wait_ge(s_modu, (l + 1) * 2 * MODJ + 2 * j + h + 1)
                        pool.sem_inc(s_acc, 1)
            rstd(DEPTH * 3, 1, 8, 2)

        @block.vector
        def _(dve):
            v = nc.vector
            su = Chain(dve, s_setup["vector"])
            ts, tt, stt = v.tensor_scalar, v.tensor_tensor, v.scalar_tensor_tensor
            dve.wait_ge(s_const, 16 * 7)
            dve.wait_ge(s_setup["tensor"], 1)
            su(v.tensor_copy(cact[:, 0:8], banks[0][:, 0:8]))
            assert su.n == SET_C
            ang, kk, r, sn, cs = (sub(rt, 96 * n, [3, 32]) for n in (0, 1, 2, 4, 3))
            C1 = round(2 * math.pi * 32) / 32
            C2 = round((2 * math.pi - C1) * 2 ** 18) / 2 ** 18
            C3 = 2 * math.pi - C1 - C2
            LIM = 3.1415925
            for ins in (lambda: v.tensor_copy(stat[:, 10:13], posi[:]),
                        lambda: tt(ang, bc(con(C_INV, 32), 1, 3), bc(stat[:, 10:13], 2, 32), ALU.mult),
                        lambda: ts(kk, ang, 1 / (2 * math.pi), 12582912.0, ALU.mult, ALU.add),
                        lambda: ts(kk, kk, 12582912.0, None, ALU.subtract),
                        lambda: stt(r, kk, -C1, ang, ALU.mult, ALU.add),
                        lambda: stt(r, kk, -C2, r, ALU.mult, ALU.add),
                        lambda: stt(r, kk, -C3, r, ALU.mult, ALU.add),
                        lambda: ts(sn, r, LIM, -LIM, ALU.min, ALU.max),
                        lambda: ts(cs, r, math.pi / 2, None, ALU.add),
                        lambda: ts(kk, cs, LIM, -2 * math.pi, ALU.is_gt, ALU.mult),
                        lambda: tt(cs, cs, kk, ALU.add),
                        lambda: ts(cs, cs, LIM, -LIM, ALU.min, ALU.max)):
                su(ins())
                su.sync()
            assert su.n == SET_ANG, su.n
            su(v.memset(zero16[:], 0.0))
            su(v.memset(st[:, 0], 0.0))
            dve.wait_ge(s_setup["scalar"], 5)
            su(stt(cact[:, 16:24], cact[:, 8:16], 1.0, cact[:, 0:8], ALU.add, ALU.mult))
            su.sync()
            su(ts(cact[:, 16:24], cact[:, 16:24], 0.5, None, ALU.mult))
            su.sync()
            for t in range(TB):
                for s_ in (s_t1, s_he, s_hTl):
                    dve.sem_inc(s_[t], 1)
            dve.sem_inc(s_dlo, 2)
            dve.sem_inc(s_x, 1)

            def mod_sum(chain, l, j):
                o = acc_of[j]
                if j >= FIRST:
                    filled(dve, l, f"mod{j - 2}")
                for h in range(2):
                    dve.wait_ge(s_modl[h], (l * MODJ + j + 1) * 16)
                    for k in range(4):
                        n = 4 * h + k
                        sc = cact[:, 16 + n:17 + n]
                        if n:
                            if k or n == 4:
                                chain.sync()
                            ins = stt(o, modw[:, h, k], sc, o, ALU.mult, ALU.add)
                        else:
                            ins = ts(o, modw[:, h, k], sc, None, ALU.mult)
                        if k < 3:
                            chain(ins)
                    ins.then_inc(s_modu, 1)
                    dve.wait_ge(s_modu, l * 2 * MODJ + 2 * j + h + 1)
                dve.sem_inc(s_acc, 1)

            for j in range(FIRST):
                mod_sum(su, 0, j)
            with dve.Fori(0, DEPTH) as l:
                d = Chain(dve, s_vs, l * V_STEPS)
                expected = [n for n, e in plan if e == "v"]

                def take(name):
                    assert expected.pop(0) == name, name
                    return filled(dve, l, name)

                def free(ins):
                    ins.then_inc(s_drain["v"], 1)

                def seq(*steps):
                    for s_ in steps:
                        d.sync()
                        d(s_())

                b = take("vec")
                free(v.tensor_copy(vec[:], b[:, 0:V_END]))
                drained(dve, l, "vec")
                d(ts(vx[:, 0:6], vec[:, V_W0:V_W0 + 6], 0.5, None, ALU.mult))
                d(ts(vx[:, 6:9], vec[:, V_KA:V_KA + 3], -1.0, 1.0, ALU.mult, ALU.add))
                d(v.memset(feat[:, :, 0:1], 0.0))

                def mod_out(j):
                    b = take(f"mod{j}")
                    if j in (4, 5, 10, 11):
                        if j == 4:
                            dve.wait_ge(s_grow, (l + 1) * 32)
                        o = gate_rows[:, j // 6, (j % 2) * 512:(j % 2) * 512 + 512]
                        free(tt(o, b[:], o, ALU.add))
                    else:
                        at = 4 * j if j < 4 else 4 * j - 8
                        free(tt(modc[:, at:at + 4], b[:, 0:4], vec[:, at:at + 4], ALU.add))

                for j in range(FIRST):
                    mod_out(j)
                drained(dve, l, "mod3")
                d(stt(amod[:, 0:8], modc[:, 8:16], 1.0, vec[:, V_NMIX:V_NMIX + 8], ALU.add, ALU.mult))

                def mean_square(n, at, cols):
                    dve.wait_ge(s_ss, l * 3 + n)
                    for c0, c1, w in cols:
                        ins = ts(stat[:, c0:c1], stat[:, c0:c1], 1.0 / w, EPS, ALU.mult, ALU.add)
                        if (c0, c1, w) != cols[-1]:
                            d(ins)
                    ins.then_inc(s_ms, 1)
                    dve.wait_ge(s_rstd, l * 3 + n)

                def normalised(n, at):
                    mean_square(n, at, [(at, at + 2, D)])
                    for t in range(TB):
                        ins = ts(xn[:, t], xs[:, t], stat[:, at + t:at + t + 1], None, ALU.mult)
                        if t == 0:
                            d(ins)
                    ins.then_inc(s_xn, 1)

                def to_T(prefix, at):
                    for j in (1, 3):
                        b = take(f"{prefix}{j}")
                        for k2 in range(2):
                            k = 2 * j + k2
                            ins = ts(actT[:, k, :], b[:, k2 * SEQ:(k2 + 1) * SEQ], amod[:, at // 2 + k:at // 2 + k + 1],
                                     modc[:, at + k:at + k + 1], ALU.mult, ALU.add)
                            if k2:
                                free(ins)

                d.sync()
                normalised(1, 0)
                to_T("hT", 0)

                def shift(j):
                    drained(dve, l, f"rf{j}")
                    n = min(2, NF - 2 * j)
                    if j:
                        dve.wait_ge(s_mix, l * 6 + j)
                    d(tt(dtmp[:, 0:n], feat[:, 2 * j:2 * j + n, 0:SEQ], feat[:, 2 * j:2 * j + n, 1:SEQ + 1], ALU.subtract))
                    d.sync()
                    for i in range(n):
                        f = feat[:, 2 * j + i, 1:SEQ + 1]
                        ins = stt(f, dtmp[:, i], vec[:, V_MU + 2 * j + i:V_MU + 2 * j + i + 1], f, ALU.mult, ALU.add)
                    ins.then_inc(s_mix, 1)

                mod_sum(d, l, 4), shift(0), shift(1), mod_sum(d, l, 5), mod_out(4), shift(2), shift(3)
                mod_sum(d, l, 6), mod_out(5), shift(4), mod_sum(d, l, 7), mod_out(6), shift(5)
                mod_sum(d, l, 8), mod_out(7)

                def rope(name, t, n, parts, copies):
                    b = take(name)
                    if n >= 1:
                        dve.wait_ge(s_rot, l * 8 + 2 * n + t - 1)
                    for w, buf in ((0, ropeA), (1, ropeB)):
                        for o0, c0, heads in parts:
                            ins = tt(buf[:, t, o0:o0 + heads * HD].rearrange("p (h d) -> p h d", d=HD),
                                     b[:, c0:c0 + heads * HD].rearrange("p (h d) -> p h d", d=HD),
                                     bc(cosn[:, w, t, :], 1, heads), ALU.mult)
                            last = w == 1 and (o0, c0, heads) == parts[-1]
                            if last:
                                ins.then_inc(s_ra, 1)
                    for n_, (dst, c0, w) in enumerate(copies):
                        ins = v.tensor_copy(dst, b[:, c0:c0 + w])
                    return ins

                for t in range(TB):
                    rope(f"q{t}", t, 0, [(0, 0, 6)], [])
                    dve.wait_ge(s_ra, l * 8 + t + 1)
                    dve.sem_inc(s_drain["v"], 1)
                mod_sum(d, l, 9), mod_out(8)
                free(rope("k0", 0, 1, [(0, 0, 2), (128, 256, 2)], [(vsel[:, 0, :], 128, 128)]))
                mod_sum(d, l, 10), mod_out(9)
                free(rope("k1", 1, 1, [(0, 0, 2), (128, 256, 2)], [(vsel[:, 1, :], 128, 128)]))
                free(rope("g0", 0, 2, [(0, 146, 4)], [(vwin[:, 0, :], 0, 128), (gsig[:, 0, :], 128, 18)]))
                mod_sum(d, l, 11), mod_out(10)
                free(rope("g1", 1, 2, [(0, 146, 4)], [(vwin[:, 1, :], 0, 128), (gsig[:, 1, :], 128, 18)]))
                drained(dve, l, "g1")
                dve.sem_inc(s_gt, 1)
                dve.wait_ge(s_lin, l * 2 + 2)
                ts(feat[:, 10, 1:SEQ + 1], feat[:, 10, 1:SEQ + 1], 0.5, 0.5, ALU.mult, ALU.add).then_inc(s_lsg, 1)
                free(rope("m0", 0, 3, [(0, 0, 4)], [(vmob[:, 0, :], 256, 256)]))
                mod_out(11)
                free(rope("m1", 1, 3, [(0, 0, 4)], [(vmob[:, 1, :], 256, 256)]))
                drained(dve, l, "m1")
                d(stt(amod[:, 8:16], modc[:, 24:32], 1.0, vec[:, V_NFFN:V_NFFN + 8], ALU.add, ALU.mult))

                R, K, V = (feat[:, 3 * i:3 * i + 3, 1:SEQ + 1] for i in range(3))
                spare = mo1.rearrange("p b t i s -> p (b t i s)").rearrange("p (i t) -> p i t", i=3)
                for i in range(3):
                    d(ts(big[:, 4, i], K[:, i], vec[:, V_KK + i:V_KK + i + 1], None, ALU.mult))
                d.sync()
                tt(big[:, 5], big[:, 4], big[:, 4], ALU.mult).then_inc(s_sq, 1)
                drained(dve, l, "lg1")
                d(ts(big[:, 0], big[:, 0], -DECAY / 2, -DECAY / 2, ALU.mult, ALU.add))
                d(ts(big[:, 3], big[:, 3], 0.5, 0.5, ALU.mult, ALU.add))
                d.sync()
                for i in range(3):
                    d(v.tensor_tensor_scan(big[:, 1, i], con(C_RESET, SEQ), big[:, 0, i], 0.0, ALU.mult, ALU.add))
                d.sync()
                tt(big[:, 0], big[:, 1], big[:, 0], ALU.subtract).then_inc(s_cum, 1)
                for i in range(3):
                    d(ts(spare[:, i], big[:, 3, i], vec[:, V_KA + i:V_KA + i + 1], vx[:, 6 + i:7 + i], ALU.mult, ALU.add))
                d.sync()
                d(tt(K, K, spare, ALU.mult))
                for part, (t0, t1) in ((0, (0, 2)), (1, (2, 3))):
                    b = take(f"kn{part}")
                    free(ts(big[:, 5, t0:t1].rearrange("p i t -> p (i t)"), b[:, 0:(t1 - t0) * SEQ], 1e-24, None, ALU.max))
                drained(dve, l, "kn1")
                v.reciprocal(big[:, 5], big[:, 5]).then_inc(s_kn, 1)
                dve.wait_ge(s_kni, l + 1)
                d(tt(big[:, 4], big[:, 4], big[:, 5], ALU.mult))
                d.sync()
                for i in range(3):
                    ins = stt(big[:, 5, i], R[:, i], vec[:, V_RK + i:V_RK + i + 1], K[:, i], ALU.mult, ALU.mult)
                ins.then_inc(s_rk, 1)
                dve.wait_ge(s_exp, l + 1)
                stt(big[:, 0].rearrange("p i t -> p (i t)"), big[:, 4].rearrange("p i t -> p (i t)"), -1.0,
                    big[:, 0].rearrange("p i t -> p (i t)"), ALU.mult, ALU.mult).then_inc(s_til, 1)
                dve.wait_ge(s_til, l * 4 + 1)
                d(tt(big[:, 4], big[:, 4], big[:, 3], ALU.mult))
                d.sync()
                tt(big[:, 4], big[:, 4], big[:, 1], ALU.mult).then_inc(s_til, 1)
                dve.wait_ge(s_til, l * 4 + 2)
                tt(big[:, 1], K, big[:, 1], ALU.mult).then_inc(s_til, 1)
                d(v.tensor_copy(pl[:], big[:, 2].rearrange("p i (n s) -> p i n s", n=NCH)[:, :, :, CH - 1]))
                d.sync()
                tt(big[:, 2], R, big[:, 2], ALU.mult).then_inc(s_til, 1)
                dve.wait_ge(s_gth, l + 1)
                d(ts(gsig[:], gsig[:], 0.5, 0.5, ALU.mult, ALU.add))

                def masked(dst, src, mask):
                    return tt(dst, src, bc(con(mask, CH), 1, 3), ALU.mult)

                def masked_products(kind, first, second):
                    for hb in range(2):
                        for t in range(TB):
                            b = take(f"{kind}{hb}{t}")[:, 0:6 * CH].rearrange("p (i w s) -> p w i s", i=3, w=2)
                            d(masked(first[:, hb, t], b[:, 0], C_STRICT))
                            free(masked(second[:, hb, t], b[:, 1], C_INCL))

                b = take("ch")
                free(v.tensor_copy(cg[:, 0], b[0:HD, 0:4 * NC]))
                drained(dve, l, "ch")
                seq(lambda: tt(cg[:, 1], cg[:, 0], cg[:, 0], ALU.mult),
                    lambda: ts(cg[:, 1], cg[:, 1], 0.044715, 1.0, ALU.mult, ALU.add))
                d.sync()
                tt(cg[:, 1], cg[:, 1], cg[:, 0], ALU.mult).then_inc(s_ct, 1)
                dve.wait_ge(s_ct2, l + 1)
                d(stt(cg[:, 3], cg[:, 2], 1.0, cg[:, 0], ALU.add, ALU.mult))
                d.sync()
                ts(cg[:, 3], cg[:, 3], 0.5, None, ALU.mult).then_inc(s_cgr, 1)
                for part, (t0, t1) in ((0, (0, 2)), (1, (2, 3))):
                    b = take(f"bo{part}")
                    free(tt(big[:, 3, t0:t1], b[:, 0:(t1 - t0) * SEQ].rearrange("p (i t) -> p i t", t=SEQ), V[:, t0:t1], ALU.mult))
                filled(dve, l, "qk4")
                d(v.memset(cPb, 0.0))
                d(v.memset(cVb, 0.0))
                d.sync()
                b = take("ckv")
                for w in range(2):
                    d(tt(ckr[:, w, :].rearrange("p (h d) -> p h d", h=2), b[0:NC, 0:P].rearrange("p (h d) -> p h d", h=2),
                         bc(cosn[0:NC, w, 2, :], 1, 2), ALU.mult))
                for h in range(NKV):
                    for i in range(3):
                        ins = v.tensor_copy(cVb[32 * i:32 * i + NC, h, i * HD:(i + 1) * HD],
                                            b[32 * i:32 * i + NC, P + h * HD:P + (h + 1) * HD])
                free(ins)
                drained(dve, l, "ckv")
                kr = [ckr[:, w, :].rearrange("p (h d) -> p h d", h=2) for w in (0, 1, 3)]
                tt(kr[2][:, :, 0:32], kr[0][:, :, 0:32], kr[1][:, :, 32:64], ALU.subtract)
                tt(kr[2][:, :, 32:64], kr[0][:, :, 32:64], kr[1][:, :, 0:32], ALU.add).then_inc(s_ckr, 1)
                b = take("ckT")
                free(v.tensor_copy(ckT[:], b[:, 0:NC]))
                cbias = con(C_CBIAS, TB * NC).rearrange("p (t n) -> p t n", t=TB)
                for h in range(NKV):
                    b = take(f"cs{h}")
                    free(tt(cSb[:, h], b[:, 0:TB * 3 * NC].rearrange("p (t i n) -> p t i n", t=TB, i=3), bc(cbias, 2, 3), ALU.add))
                drained(dve, l, "cs1")
                c12 = cSb.rearrange("p h t i n -> p (h t i) n")
                d(v.tensor_reduce(cst2[:, 0:12], c12, AX, ALU.max))
                d.sync()
                tt(c12, c12, bc(cst2[:, 0:12], 2, NC), ALU.subtract).then_inc(s_cs, 1)
                masked_products("mb", Mst, Arb)
                dve.wait_ge(s_ce, l + 1)
                c01 = con(C_C01, TB * NC).rearrange("p (t n) -> p t n", t=TB)
                for h in range(NKV):
                    d(tt(cSb[:, h], cSb[:, h], bc(c01, 2, 3), ALU.mult))
                seq(lambda: v.tensor_reduce(cst2[:, 12:24], c12, AX, ALU.add),
                    lambda: ts(cst2[:, 12:24], cst2[:, 12:24], 1e-30, None, ALU.max),
                    lambda: v.reciprocal(cst2[:, 24:36], cst2[:, 12:24]))
                d.sync()
                w12 = cst2[:, 24:36].rearrange("p (h t i) -> p h t i", h=2, t=TB)
                d(tt(w12, w12, gsig[:].rearrange("p t (h i g) -> p h t i g", h=2, i=3)[:, :, :, :, 0], ALU.mult))
                d.sync()
                for h in range(NKV):
                    ins = tt(cPb[:, :, h, :].rearrange("p t (i n) -> p t i n", i=3)[:, :, :, 0:NC], cSb[:, h],
                             bc(w12[:, h], 3, NC), ALU.mult)
                    if h == 0:
                        d(ins)
                ins.then_inc(s_cp, 1)
                b = take("cpT")
                free(v.tensor_copy(cpT[0:96], b[0:96, :].rearrange("p (t h q) -> p t h q", t=TB, h=2)))
                masked_products("mk", aak, Ark)
                for t in range(TB):
                    b = take(f"co{t}")
                    free(v.tensor_copy(onsa[:, t, :], b[:, 0:NSA_W]))

                def twelve(z):
                    return z.rearrange("p b t i s -> p (b t i) s")

                for kind, n in mixed_steps():
                    if kind == "head":
                        if n < 16:
                            b = take(f"S{n}")
                            if n >= 2:
                                filled(dve, l, f"T{n - 2}")
                            dve.sem_inc(s_vgate, 1)
                            for j, (c0, c1) in enumerate(((0, P), (P, 3 * P))):
                                ins = v.tensor_tensor_reduce(out=Ssb[:, n % 2, c0:c1], in0=b[:, c0:c1], in1=con(C_CAUSAL + c0, c1 - c0),
                                                             scale=-SCALE, scalar=3e38, op0=ALU.add, op1=ALU.min,
                                                             accum_out=amx[:, n, j:j + 1])
                            free(ins)
                        if n >= 2:
                            u = n - 2
                            branch, h = head_of(u)[4]
                            b = take(f"O{u}")
                            d(v.reciprocal(awt[:, u, :], asm[:, u, :]))
                            d.sync()
                            if branch:
                                d(tt(awt[:, u, :], awt[:, u, :], gsig[:, :, 3 * h + branch], ALU.mult))
                                d.sync()
                            o = (onsa if branch else omob)[:, :, h * HD:(h + 1) * HD]
                            for t in range(TB):
                                if branch:
                                    ins = stt(o[:, t], b[:, t * HD:(t + 1) * HD], awt[:, u, t:t + 1], o[:, t], ALU.mult, ALU.add)
                                else:
                                    ins = ts(o[:, t], b[:, t * HD:(t + 1) * HD], awt[:, u, t:t + 1], None, ALU.mult)
                                if t == 0:
                                    d(ins)
                            free(ins)
                    elif kind == "x" and n == 0:
                        drained(dve, l, "x01")
                        dve.wait_ge(s_mask, l * len(LEVELS) + 1)
                        i64 = bc(con(C_ID64, CH), 1, 12)
                        tt(twelve(Tm), twelve(Xm), i64, ALU.add).then_inc(s_mm, 1)
                        tt(twelve(TTm), twelve(mo0), i64, ALU.add).then_inc(s_mm, 1)
                    elif kind == "t":
                        for w, M_ in (("t", Tm), ("tt", TTm)):
                            if w == "t" and n == len(LEVELS) - 1:
                                continue
                            for b2 in range(2):
                                b = take(f"{w}{n}{b2}")
                                o = M_[:, b2].rearrange("p t i s -> p (t i s)")
                                free(tt(o, b[:, 0:RW], o, ALU.add))
                    elif kind == "u":
                        t, c2 = n // 2, n % 2
                        q = slice(64 * c2, 64 * c2 + 64)
                        for b2 in range(2):
                            b = take(f"u{n}{b2}")
                            free(tt(Um[q, b2, t], b[q, 0:3 * HD].rearrange("p (i s) -> p i s", i=3), Ub[q, b2, t], ALU.add))
                    elif kind == "g":
                        b = take(f"g{n}s")
                        free(tt(gtmp[:], b[:, 0:3 * HD].rearrange("p (i s) -> p i s", i=3), st[:, n], ALU.add))
                        drained(dve, l, f"g{n}s")
                        tt(st[:, n + 1], gtmp[:], bc(pl[:, :, n], 2, HD), ALU.mult).then_inc(s_st, 1)
                        dve.wait_ge(s_st, l * (NCH - 1) + n + 1)
                d.sync()
                drained(dve, l, "O15")
                dve.sem_inc(s_on, 1)
                drained(dve, l, "ys1")
                for c2 in range(2):
                    b = take(f"yu{c2}")
                    y4 = yT.rearrange("p i (t c s) -> p c t i s", t=TB, c=2)[:, c2]
                    free(tt(y4, b[:, 0:RW].rearrange("p (t i s) -> p t i s", t=TB, i=3), y4, ALU.add))
                mean_square(2, 2, [(2, 4, NSA_W), (4, 6, MOBA_W)])
                for t in range(TB):
                    d(ts(onsa[:, t], onsa[:, t], stat[:, 2 + t:3 + t], None, ALU.mult))
                for t in range(TB):
                    ins = ts(omob[:, t], omob[:, t], stat[:, 4 + t:5 + t], None, ALU.mult)
                    if t == 0:
                        d(ins)
                ins.then_inc(s_o, 1)
                drained(dve, l, "yu1")
                yf, sf, rf_ = (z.rearrange("p i t -> p (i t)") for z in (yT, ysq, big[:, 5]))
                for part, (c0, c1) in ((0, (0, 512)), (1, (512, 768))):
                    b = take(f"gm{part}")
                    free(stt(yf[:, c0:c1], b[:, 0:c1 - c0], -1.0 / HD, yf[:, c0:c1], ALU.mult, ALU.add))
                drained(dve, l, "gm1")
                tt(sf, yf, yf, ALU.mult).then_inc(s_yv, 1)
                for part, (c0, c1) in ((0, (0, 512)), (1, (512, 768))):
                    b = take(f"gv{part}")
                    free(ts(rf_[:, c0:c1], b[:, 0:c1 - c0], 1.0 / HD, GN_EPS, ALU.mult, ALU.add))
                drained(dve, l, "gv1")
                v.reciprocal(rf_, rf_).then_inc(s_yv, 1)
                dve.wait_ge(s_yr, l + 1)
                seq(lambda: tt(yf, yf, rf_, ALU.mult))
                d.sync()
                for i in range(3):
                    d(ts(yT[:, i], yT[:, i], vec[:, V_LNW + i:V_LNW + i + 1], vec[:, V_LNB + i:V_LNB + i + 1], ALU.mult, ALU.add))
                seq(lambda: tt(yf, yf, big[:, 3].rearrange("p i t -> p (i t)"), ALU.add))
                d.sync()
                tt(actT[:, 5:8, :], yT, big[:, 6], ALU.mult).then_inc(s_mixT, 1)
                def add_to_residual(b, g, t, half, signal):
                    h = slice(512 * half, 512 * half + 512)
                    tmp = junkv[:, (2 * half + t) % 2]
                    ins = tt(tmp, b[:], gate_rows[:, g, h], ALU.mult)
                    return ins, (lambda: tt(xs[:, t, h], xs[:, t, h], tmp, ALU.add))


                def low(hi_sem, lo_sem, q, j, lows, weights, highs):
                    for c, (lo, w, hi) in enumerate(zip(lows, weights, highs)):
                        dve.wait_ge(hi_sem, split_counts(l, q, j, c))
                        tt(lo, w, hi.bitcast(F32), ALU.subtract).then_inc(lo_sem, 1)

                def gate_up_low(q, j, c):
                    low(s_guhi[c], s_gulo[c], q, j, *(parts(z, 4 * c) for z in (gu_lo[j], ring[:, j], gu_hi[j])))

                def down_low(q, j):
                    low(s_dhi, s_dlo, q, j, parts(dn_lo[j]), parts(ring[:, 2], 4 * j), parts(dn_hi[j]))

                for c in range(2):
                    gate_up_low(0, 0, c)
                d(ts(before, con(C_CAUSAL, P), 0.0, None, ALU.is_lt))
                d(v.tensor_tensor_scan(iota[:, 0:P], con(C_ONES, P), con(C_ONES, P), -1.0, ALU.mult, ALU.add))
                d.sync()
                d(ts(iota[:, P:SEQ], iota[:, 0:P], float(P), None, ALU.add))
                for half in range(2):
                    for t in range(TB):
                        b = take(f"out{2 * half + t}")
                        d.sync()
                        ins, add = add_to_residual(b, 0, t, half, None)
                        free(ins)
                        drained(dve, l, f"out{2 * half + t}")
                        d(add())
                d.sync()
                dve.sem_inc(s_x, 1)
                normalised(3, 6)
                to_T("h2T", 16)

                b = take("route")
                free(v.tensor_copy(rt[:, 0:32], b[:, 0:32]))
                dve.wait_ge(s_rt, l + 1)
                aff, bia = rt[:, 32:64], rt[:, 64:96]
                d(ts(aff, aff, 0.5, 0.5, ALU.mult, ALU.add))
                d.sync()
                d(tt(bia.rearrange("p (t e) -> p t e", t=TB), aff.rearrange("p (t e) -> p t e", t=TB), bc(rbias[:], 1, TB), ALU.add))
                b8 = bia.rearrange("p (g e) -> p g e", e=4)
                d.sync()
                pair = rt[:, 96:144].rearrange("p (g n) -> p g n", n=6)
                for n, (e0, e1) in enumerate(((0, 1), (0, 2), (0, 3), (1, 2), (1, 3), (2, 3))):
                    d(tt(pair[:, :, n], b8[:, :, e0], b8[:, :, e1], ALU.add))
                d.sync()
                gs = rt[:, 144:152]
                d(v.tensor_reduce(gs, pair, AX, ALU.max))
                d.sync()

                def rank(dst, z, n, w):
                    gt, ge = (rt[:, o:o + 16 * n].rearrange("p (g a b) -> p g a b", a=4, b=4) for o in (w, w + 16 * n))
                    other, own = bc(z, 2, 4), bc(z, 3, 4)
                    d(tt(gt, other, own, ALU.is_gt))
                    d(tt(ge, other, own, ALU.is_ge))
                    d.sync()
                    m = con(C_LT, 16)
                    d(tt(rt[:, w + 16 * n:w + 32 * n].rearrange("p (g c) -> p g c", g=n),
                         rt[:, w + 16 * n:w + 32 * n].rearrange("p (g c) -> p g c", g=n), bc(m, 1, n), ALU.mult))
                    m2 = con(C_GT, 16)
                    d(tt(rt[:, w:w + 16 * n].rearrange("p (g c) -> p g c", g=n),
                         rt[:, w:w + 16 * n].rearrange("p (g c) -> p g c", g=n), bc(m2, 1, n), ALU.mult))
                    d.sync()
                    d(tt(gt, gt, ge, ALU.add))
                    d.sync()
                    d(v.tensor_reduce(dst, gt, AX, ALU.add))
                    d.sync()

                rank(rt[:, 152:160].rearrange("p (g a) -> p g a", g=TB), gs.rearrange("p (g a) -> p g a", g=TB), TB, 256)
                grp = rt[:, 152:160].rearrange("p (t g) -> p t g", t=TB)
                bel = rt[:, 576:584].rearrange("p (t g) -> p t g", t=TB)
                d(v.memset(bel[:, :, 0], 0.0))
                d(ts(grp, grp, 0.5, None, ALU.is_lt))
                d.sync()
                d(v.tensor_copy(bel[:, :, 1], grp[:, :, 0]))
                d(tt(bel[:, :, 2], grp[:, :, 0], grp[:, :, 1], ALU.add))
                d.sync()
                tt(bel[:, :, 3], bel[:, :, 2], grp[:, :, 2], ALU.add).then_inc(s_grp, 1)
                gt8 = rt[:, 160:192].rearrange("p (g a) -> p g a", g=8)
                rank(gt8, b8, 8, 320)
                b = take("rank")
                start = rt[:, 600:605]
                d(v.memset(start[:, 4:5], float(SEQ)))
                d(v.tensor_copy(start[:, 0:4], b[:, 8:12]))
                free(tt(rt[:, 592:600], b[:, 0:8], rt[:, 152:160], ALU.mult))
                drained(dve, l, "rank")
                seq(lambda: v.tensor_reduce(rt[:, 588:590], rt[:, 592:600].rearrange("p (t g) -> p t g", t=TB), AX, ALU.add))
                d.sync()
                for t in range(TB):
                    ins = ts(perm[:, t], iota, rt[:, 588 + t:589 + t], None, ALU.is_equal)
                    if t == 0:
                        d(ins)
                ins.then_inc(s_perm, 1)
                d(ts(rt[:, 160:192], rt[:, 160:192], 1.5, None, ALU.is_lt))
                sel = rt[:, 160:192]
                seq(lambda: tt(sel.rearrange("p (g e) -> p g e", e=4), sel.rearrange("p (g e) -> p g e", e=4), bc(rt[:, 152:160], 2, 4), ALU.mult),
                    lambda: tt(sel, sel, aff, ALU.mult),
                    lambda: v.tensor_reduce(rt[:, 192:194], sel.rearrange("p (t e) -> p t e", t=TB), AX, ALU.add),
                    lambda: v.reciprocal(rt[:, 194:196], rt[:, 192:194]),
                    lambda: ts(rt[:, 194:196], rt[:, 194:196], 0.5, None, ALU.mult))
                d.sync()
                tt(comb[:], sel.rearrange("p (t e) -> p t e", t=TB), bc(rt[:, 194:196], 2, E), ALU.mult).then_inc(s_comb, 1)
                cl, ov_ = rt[:, 608:613], rt[:, 640 - 6:639]
                cnt = rt[:, 614:624]
                d(v.memset(cnt[:, 0:2], 0.0))
                seq(lambda: ts(cl, start, float(P), None, ALU.min),
                    lambda: tt(ov_, start, cl, ALU.subtract))
                d.sync()
                for t, z in ((0, cl), (1, ov_)):
                    d(tt(cnt[:, 2:10].rearrange("p (g t) -> p g t", t=TB)[:, :, t], z[:, 1:5], z[:, 0:4], ALU.subtract))
                d.sync()
                v.tensor_copy(counts[:], cnt).then_inc(s_count, 1)
                for j in range(4):
                    if j % 2:
                        b = take(f"hs{j}")
                        for k in (2 * j, 2 * j + 1):
                            ins = ts(actT[:, k, :], b[:, (k % 2) * SEQ:(k % 2 + 1) * SEQ], amod[:, 8 + k:9 + k],
                                     modc[:, 16 + k:17 + k], ALU.mult, ALU.add)
                        free(ins)
                    dve.wait_ge(s_ahi, l * 4 + j + 1)
                    tt(act_lo[:, 2 * j:2 * j + 2], actT[:, 2 * j:2 * j + 2, :], act_hi[:, 2 * j:2 * j + 2].bitcast(F32), ALU.subtract).then_inc(s_alo, 1)
                b = take("combs")
                free(v.tensor_copy(combs, b[:, 0:2 * E].rearrange("p (t e) -> p t e", t=TB)))
                drained(dve, l, "combs")
                dve.wait_ge(s_count, l + 1)
                assert not expected, expected
                d.fill_up(V_STEPS)

                with dve.Fori(0, GROUPS) as g:
                    now = load_counts(dve, g + 1)
                    for r in range(PER_GROUP):
                        q, j = 2 * g + r // 2, r % 2
                        n = l * E + 4 * g + r
                        ahead = (q + j, 1 - j)
                        if r < PER_GROUP - 1:
                            gate_up_low(*ahead, 0)
                        else:
                            with dve.If(g < GROUPS - 1):
                                gate_up_low(*ahead, 0)
                        for t in range(TB):
                            with dve.If(now[t] > 0):
                                dve.wait_ge(s_th[t], n + 2)
                                b = banks[4 + t]
                                stt(t1_s[:, t], th_s[:, t], 1.0, b[:, 0:FF], ALU.add, ALU.mult).then_inc(s_t1[t], 1)
                                dve.wait_ge(s_t1[t], n + 2)
                                stt(he_s[:, t], t1_s[:, t], combs[:, t, bass.ds(2 * q + j, 1)], b[:, FF:2 * FF],
                                    ALU.mult, ALU.mult).then_inc(s_he[t], 1)
                            with dve.Else():
                                skip(dve, s_t1[t], n + 1)
                                skip(dve, s_he[t], n + 1)
                        if r < PER_GROUP - 1:
                            gate_up_low(*ahead, 1)
                        else:
                            with dve.If(g < GROUPS - 1):
                                gate_up_low(*ahead, 1)
                        for t in range(TB):
                            with dve.If(now[t] > 0):
                                dve.wait_ge(s_hTs[t], n + 2)
                                tt(heT_lo[:, t], banks[6 + t][:, 0:FF].rearrange("p (k t) -> p k t", k=2), heT_hi[:, t].bitcast(F32),
                                   ALU.subtract).then_inc(s_hTl[t], 1)
                            with dve.Else():
                                skip(dve, s_hTl[t], n + 1)
                        down_low(q, j)

                for half in range(2):
                    dve.wait_ge(s_y, l * 4 + 2 * half + 2)
                    v.tensor_copy(ysort[:, 1, 512 * half:512 * half + 512], banks[2 + half][:]).then_inc(s_ys["vector"], 1)
                for half in range(2):
                    for t in range(TB):
                        n = 2 * half + t
                        dve.wait_ge(s_unsort, l * 4 + n + 1)
                        ins, add = add_to_residual(banks[4 + n], 1, t, half, None)
                        ins.then_inc(s_yd, 1)
                        dve.wait_ge(s_yd, l * 8 + 2 * n + 1)
                        add().then_inc(s_yd, 1)
                        dve.wait_ge(s_yd, l * 8 + 2 * n + 2)
                dve.sem_inc(s_x, 1)

            fv = Chain(dve, s_vm)
            dve.wait_ge(s_ss, DEPTH * 3 + 1)
            ts(stat[:, 8:10], stat[:, 8:10], 1.0 / D, EPS, ALU.mult, ALU.add).then_inc(s_ms, 1)
            dve.wait_ge(s_rstd, DEPTH * 3 + 1)
            dve.wait_ge(s_nf, 16)
            ov = actT[:].rearrange("p (t k) c -> p t (k c)", t=TB)
            for t in range(TB):
                stt(ov[:, t], xs[:, t], stat[:, 8 + t:9 + t], final_row, ALU.mult, ALU.mult).then_inc(s_fin, 1)


_INS = ["x", "c", "positions", "w_mod", "b_mod", "norm_mix", "norm_ffn", "w_in", "nsa_phi_w1", "nsa_phi_w2",
        "nsa_phi_pos", "rwkv_mu", "rwkv_w_up", "rwkv_w0", "rwkv_a_up", "rwkv_a0", "rwkv_g_up", "rwkv_k_k",
        "rwkv_k_a", "rwkv_r_k", "rwkv_ln_w", "rwkv_ln_b", "norm_nsa_out", "norm_moba_out", "w_out",
        "w_router", "router_bias", "moe_w_gate", "moe_w_up", "moe_w_down", "norm_final"]


def shape_table():
    import numpy as np
    z = np.zeros((P, C_END), np.float32)
    p = np.arange(P)[:, None]
    z[:, C_IDENT:C_IDENT + P] = p == np.arange(P)
    tri = np.where(np.arange(P)[None, :] > p, NEG, 0.0)
    z[:, C_CAUSAL:C_CAUSAL + P] = tri
    z[:, C_CAUSAL + 2 * P:C_CAUSAL + 3 * P] = tri
    z[:, C_BLK:C_BLK + P] = p // HD == np.arange(P) // HD
    z[:, C_ONES:C_ONES + P] = 1
    s, t = p % CH, np.arange(CH)[None, :]
    z[:, C_STRICT:C_STRICT + CH] = s < t
    z[:, C_INCL:C_INCL + CH] = s <= t
    for n, w in enumerate(LEVELS):
        z[:, C_LEVEL + n * CH:C_LEVEL + (n + 1) * CH] = (s // (2 * w) == t // (2 * w)) & (t % (2 * w) >= w) & (s % (2 * w) < w)
    z[:, C_ID64:C_ID64 + CH] = s == t
    z[:, C_RESET:C_RESET + SEQ] = np.arange(SEQ) % CH != 0
    for b in range(TB):
        seen = CMP_STRIDE * np.arange(NC) + CMP_BLOCK - 1 <= b * P + p
        z[:, C_CBIAS + b * NC:C_CBIAS + (b + 1) * NC] = np.where(seen, 0.0, NEG)
        z[:, C_C01 + b * NC:C_C01 + (b + 1) * NC] = seen
    a, o = np.divmod(np.arange(16), 4)
    z[:, C_LT:C_LT + 16] = o < a
    z[:, C_GT:C_GT + 16] = o > a
    z[:, C_INV:C_INV + 32] = (10000.0 ** (-np.arange(0, HD, 2) / HD)).astype(np.float32)
    return z


def kernel(**inputs):
    import numpy as _np
    import concourse.bacc as _bacc
    from concourse import mybir as _mybir
    from concourse.bass_utils import run_bass_kernel_spmd as _run

    nc = _bacc.Bacc("TRN2", target_bir_lowering=False, num_devices=1)
    arrays, args = {}, []
    for name, a in [(n, inputs[n]) for n in _INS] + [("shape_table", shape_table())]:
        a = _np.ascontiguousarray(a)
        arrays[f"in_{name}_dram"] = a
        args.append(nc.dram_tensor(f"in_{name}_dram", a.shape, _mybir.dt.from_np(a.dtype), kind="ExternalInput").ap())
    args.append(nc.dram_tensor("out_0_dram", (1, SEQ, D), F32, kind="ExternalOutput").ap())
    trunk(nc, *args)
    r = _run(nc, [arrays], core_ids=[0])
    return r.results[0]["out_0_dram"]
```
